# Optimizing a Trainium2 kernel written in Bass

```python
import math
import jax, jax.numpy as jnp
from jax import lax
import numpy as np

D_MODEL = 1024
BATCH = 1
SEQ = 256
DEPTH = 2
DEC_BATCH = 8
DEC_SEQ = 4
PAST_LEN = 2048
PAGE_SIZE = 128

N_EVEN = (DEPTH + 1) // 2
N_ODD = DEPTH // 2
H_A = 4
DK_A = D_MODEL // 16
DV_A = D_MODEL // 8
GK_RANK = 16
GATE_NORM = 16.0
GLA_CHUNK = 16
POOL_WINDOWS = (2, 4, 8, 16)
POOL_CH = D_MODEL // 2
POOL_GROUP = POOL_CH // len(POOL_WINDOWS)
POOL_BUF = max(POOL_WINDOWS) - 1
IN_A = 2 * H_A * DK_A + 2 * H_A * DV_A + GK_RANK + POOL_CH
MIX_A = H_A * DV_A + POOL_CH
H_C = 4
DK_C = D_MODEL // H_C
DV_C = 2 * DK_C
RET_CHUNK = 64
IN_C = 2 * H_C * DK_C + 2 * H_C * DV_C
MIX_C = H_C * DV_C
N_EXPERTS = 64
N_GROUPS = 8
TOPK_GROUPS = 4
TOP_K = 8
D_EXPERT = D_MODEL // 4
D_SHARED = D_MODEL // 4
ROUTED_SCALE = 2.5
P_DIM = 256
ALPHA = (2.0 * DEPTH) ** 0.25
BETA = (8.0 * DEPTH) ** -0.25
NORM_EPS = 1e-5

kernel_name = 'gla_pool_retnet_moe_deepnorm_step'

F32 = jnp.float32

def layer_norm(x, g, b):
    xf = x.astype(F32)
    mu = jnp.mean(xf, axis=-1, keepdims=True)
    xc = xf - mu
    var = jnp.mean(xc * xc, axis=-1, keepdims=True)
    return (xc * lax.rsqrt(var + NORM_EPS) * g.astype(F32) + b.astype(F32)).astype(x.dtype)

def rms_norm(x):
    return x * lax.rsqrt(jnp.mean(x * x, axis=-1, keepdims=True) + NORM_EPS)

def chunked_linear_attention(q, k, v, log_a, s0, chunk):
    B, L, H, K = q.shape
    V = v.shape[-1]
    C = math.gcd(L, chunk)
    N = L // C

    def blocks(t):
        return jnp.moveaxis(t.reshape((B, N, C) + t.shape[2:]), 1, 0)

    causal = jnp.tril(jnp.ones((C, C), dtype=bool))

    def step(S, inp):
        qc, kc, vc, ac = inp
        b = jnp.cumsum(ac, axis=1)
        b_last = b[:, -1:]
        q_in = qc * jnp.exp(b)
        k_in = kc * jnp.exp(-b)
        o_inter = jnp.einsum('bchk,bhkv->bchv', q_in, S)
        att = jnp.einsum('bthk,bshk->bhts', q_in, k_in)
        att = jnp.where(causal, att, 0.0)
        o_intra = jnp.einsum('bhts,bshv->bthv', att, vc)
        k_dec = kc * jnp.exp(b_last - b)
        S_new = jnp.exp(b_last[:, 0])[..., None] * S + jnp.einsum('bshk,bshv->bhkv', k_dec, vc)
        return S_new, o_inter + o_intra

    S_fin, o = lax.scan(step, s0.astype(F32), (blocks(q), blocks(k), blocks(v), blocks(log_a)))
    o = jnp.moveaxis(o, 0, 1).reshape(B, L, H, V)
    return o, S_fin.astype(s0.dtype)

def rotate_every_two(x):
    x1 = x[..., 0::2]
    x2 = x[..., 1::2]
    return jnp.stack([-x2, x1], axis=-1).reshape(x.shape)

def rotate_xpos(x, pos):
    inv = 1.0 / jnp.power(10000.0, jnp.linspace(0.0, 1.0, DK_C // 2, dtype=F32))
    inv = jnp.repeat(inv, 2)
    ang = pos[:, None] * inv[None, :]
    sin = jnp.sin(ang)[None, :, None, :]
    cos = jnp.cos(ang)[None, :, None, :]
    return x * cos + rotate_every_two(x) * sin

def mix_even(x, s_gla, s_pool, start, w_in, w_gk2, b_gk, g_norm, w_pool, b_pool, pool_scale, w_out):
    B, L, _ = x.shape
    z = x @ w_in
    o1 = H_A * DK_A
    o2 = 2 * o1
    o3 = o2 + H_A * DV_A
    o4 = o3 + H_A * DV_A
    o5 = o4 + GK_RANK
    q = z[..., :o1].reshape(B, L, H_A, DK_A).astype(F32) * (DK_A ** -0.5)
    k = z[..., o1:o2].reshape(B, L, H_A, DK_A).astype(F32)
    v = z[..., o2:o3].reshape(B, L, H_A, DV_A).astype(F32)
    r = z[..., o3:o4]
    glr = z[..., o4:o5]
    u = z[..., o5:]
    log_a = jax.nn.log_sigmoid((glr @ w_gk2 + b_gk).astype(F32)).reshape(B, L, H_A, DK_A) / GATE_NORM
    o, s_gla_new = chunked_linear_attention(q, k, v, log_a, s_gla, GLA_CHUNK)
    o = rms_norm(o) * g_norm.astype(F32)
    o_a = o.reshape(B, L, H_A * DV_A) * jax.nn.silu(r.astype(F32))
    ext = jnp.concatenate([s_pool.astype(u.dtype), u], axis=1)
    cs = jnp.cumsum(ext.astype(F32), axis=1)
    cs = jnp.concatenate([jnp.zeros((B, 1, POOL_CH), F32), cs], axis=1)
    pos = start + jnp.arange(L, dtype=jnp.int32)
    uf = u.astype(F32)
    outs = []
    for gi, w in enumerate(POOL_WINDOWS):
        lo, hi = gi * POOL_GROUP, (gi + 1) * POOL_GROUP
        win = cs[:, POOL_BUF + 1:, lo:hi] - cs[:, POOL_BUF + 1 - w:POOL_BUF + 1 - w + L, lo:hi]
        cnt = jnp.minimum(pos + 1, w).astype(F32)[None, :, None]
        d = win / cnt - uf[..., lo:hi]
        outs.append(jnp.einsum('blc,cd->bld', d, w_pool[gi].astype(F32)) + b_pool[gi].astype(F32))
    pooled = jnp.concatenate(outs, axis=-1) * pool_scale.astype(F32)
    mixed = jnp.concatenate([o_a, pooled], axis=-1).astype(x.dtype)
    return mixed @ w_out, s_gla_new, ext[:, -POOL_BUF:]

def mix_odd(x, s_ret, start, w_in, w_out):
    B, L, _ = x.shape
    z = x @ w_in
    o1 = H_C * DK_C
    o2 = 2 * o1
    o3 = o2 + MIX_C
    pos = (start + jnp.arange(L, dtype=jnp.int32)).astype(F32)
    q = rotate_xpos(z[..., :o1].reshape(B, L, H_C, DK_C).astype(F32), pos)
    k = rotate_xpos(z[..., o1:o2].reshape(B, L, H_C, DK_C).astype(F32), pos) * (DK_C ** -0.5)
    v = z[..., o2:o3].reshape(B, L, H_C, DV_C).astype(F32)
    g = z[..., o3:]
    log_gamma = jnp.log1p(-jnp.exp2(-5.0 - jnp.arange(H_C, dtype=F32)))
    log_a = jnp.broadcast_to(log_gamma[None, None, :, None], (B, L, H_C, DK_C))
    o, s_new = chunked_linear_attention(q, k, v, log_a, s_ret, RET_CHUNK)
    o = rms_norm(o).reshape(B, L, MIX_C) * jax.nn.silu(g.astype(F32))
    return o.astype(x.dtype) @ w_out, s_new

def moe(x, w_router, router_bias, w_eg, w_eu, w_ed, w_sg, w_su, w_sd):
    B, L, D = x.shape
    xt = x.reshape(B * L, D)
    T = xt.shape[0]
    scores = jax.nn.sigmoid((xt @ w_router).astype(F32))
    sel = scores + router_bias.astype(F32)
    grp = sel.reshape(T, N_GROUPS, N_EXPERTS // N_GROUPS)
    gscore = jnp.sum(lax.top_k(grp, 2)[0], axis=-1)
    _, gidx = lax.top_k(gscore, TOPK_GROUPS)
    gmask = jnp.sum(jax.nn.one_hot(gidx, N_GROUPS, dtype=F32), axis=1)
    emask = jnp.repeat(gmask, N_EXPERTS // N_GROUPS, axis=1)
    masked = jnp.where(emask > 0, sel, -jnp.inf)
    _, eidx = lax.top_k(masked, TOP_K)
    wsel = jnp.take_along_axis(scores, eidx, axis=1)
    wsel = wsel / (jnp.sum(wsel, axis=-1, keepdims=True) + 1e-20) * ROUTED_SCALE
    gates = jnp.sum(jax.nn.one_hot(eidx, N_EXPERTS, dtype=F32) * wsel[..., None], axis=1)

    def expert_step(acc, ew):
        wg, wu, wd, gcol = ew
        h = jax.nn.silu(xt @ wg) * (xt @ wu)
        return acc + gcol[:, None] * (h @ wd).astype(F32), None

    acc, _ = lax.scan(expert_step, jnp.zeros((T, D), F32), (w_eg, w_eu, w_ed, gates.T))
    shared = ((jax.nn.silu(xt @ w_sg) * (xt @ w_su)) @ w_sd).astype(F32)
    return (acc + shared).astype(x.dtype).reshape(B, L, D)

def trunk(x, p, s_gla, s_pool, s_ret, start, W):
    new_gla, new_pool, new_ret = [], [], []
    for i in range(DEPTH):
        j = i // 2
        if i % 2 == 0:
            h, sg, sp = mix_even(x, s_gla[j], s_pool[j], start, W['w_in_a'][j], W['w_gk2'][j],
                                 W['b_gk'][j], W['g_norm_a'][j], W['w_pool'][j], W['b_pool'][j],
                                 W['pool_scale'][j], W['w_out_a'][j])
            new_gla.append(sg)
            new_pool.append(sp)
        else:
            h, sr = mix_odd(x, s_ret[j], start, W['w_in_c'][j], W['w_out_c'][j])
            new_ret.append(sr)
        x = layer_norm(ALPHA * x + h, W['ln1_g'][i], W['ln1_b'][i])
        f = moe(x, W['w_router'][i], W['router_bias'][i], W['w_exp_gate'][i], W['w_exp_up'][i],
                W['w_exp_down'][i], W['w_sh_gate'][i], W['w_sh_up'][i], W['w_sh_down'][i])
        x = layer_norm(ALPHA * x + f, W['ln2_g'][i], W['ln2_b'][i])
        gate = jax.nn.sigmoid((x @ W['w_ple_gate'][i]).astype(F32))
        x = (x.astype(F32) + gate * (p[i] @ W['w_ple_proj'][i]).astype(F32)).astype(x.dtype)
    return x, jnp.stack(new_gla), jnp.stack(new_pool), jnp.stack(new_ret)

def setup_inputs(seed: int = 0) -> dict:
    key = jax.random.key(seed)
    ks = jax.random.split(key, 40)

    def nrm(k, shape, scale):
        return jax.random.normal(k, shape, F32) * scale

    return {
        'x_prompt': nrm(ks[0], (BATCH, SEQ, D_MODEL), 1.0),
        'x_sample': nrm(ks[1], (DEC_BATCH, DEC_SEQ, D_MODEL), 1.0),
        'state_gla': nrm(ks[2], (N_EVEN, DEC_BATCH, H_A, DK_A, DV_A), 1.0),
        'state_pool': nrm(ks[3], (N_EVEN, DEC_BATCH, POOL_BUF, POOL_CH), 1.0),
        'state_ret': nrm(ks[4], (N_ODD, DEC_BATCH, H_C, DK_C, DV_C), 0.5),
        'p_prompt': nrm(ks[5], (DEPTH, BATCH, SEQ, P_DIM), 1.0),
        'p_sample': nrm(ks[6], (DEPTH, DEC_BATCH, DEC_SEQ, P_DIM), 1.0),
        'w_in_a': nrm(ks[7], (N_EVEN, D_MODEL, IN_A), D_MODEL ** -0.5),
        'w_gk2': nrm(ks[8], (N_EVEN, GK_RANK, H_A * DK_A), GK_RANK ** -0.5),
        'b_gk': nrm(ks[9], (N_EVEN, H_A * DK_A), 0.1),
        'g_norm_a': 1.0 + nrm(ks[10], (N_EVEN, DV_A), 0.02),
        'w_pool': nrm(ks[11], (N_EVEN, len(POOL_WINDOWS), POOL_GROUP, POOL_GROUP), POOL_GROUP ** -0.5),
        'b_pool': nrm(ks[12], (N_EVEN, len(POOL_WINDOWS), POOL_GROUP), 0.02),
        'pool_scale': 1.0 + nrm(ks[13], (N_EVEN, POOL_CH), 0.02),
        'w_out_a': nrm(ks[14], (N_EVEN, MIX_A, D_MODEL), BETA * MIX_A ** -0.5),
        'w_in_c': nrm(ks[15], (N_ODD, D_MODEL, IN_C), D_MODEL ** -0.5),
        'w_out_c': nrm(ks[16], (N_ODD, MIX_C, D_MODEL), BETA * MIX_C ** -0.5),
        'ln1_g': 1.0 + nrm(ks[17], (DEPTH, D_MODEL), 0.02),
        'ln1_b': nrm(ks[18], (DEPTH, D_MODEL), 0.02),
        'ln2_g': 1.0 + nrm(ks[19], (DEPTH, D_MODEL), 0.02),
        'ln2_b': nrm(ks[20], (DEPTH, D_MODEL), 0.02),
        'w_router': nrm(ks[21], (DEPTH, D_MODEL, N_EXPERTS), D_MODEL ** -0.5),
        'router_bias': nrm(ks[22], (DEPTH, N_EXPERTS), 0.01),
        'w_exp_gate': nrm(ks[23], (DEPTH, N_EXPERTS, D_MODEL, D_EXPERT), D_MODEL ** -0.5),
        'w_exp_up': nrm(ks[24], (DEPTH, N_EXPERTS, D_MODEL, D_EXPERT), D_MODEL ** -0.5),
        'w_exp_down': nrm(ks[25], (DEPTH, N_EXPERTS, D_EXPERT, D_MODEL), BETA * D_EXPERT ** -0.5),
        'w_sh_gate': nrm(ks[26], (DEPTH, D_MODEL, D_SHARED), D_MODEL ** -0.5),
        'w_sh_up': nrm(ks[27], (DEPTH, D_MODEL, D_SHARED), D_MODEL ** -0.5),
        'w_sh_down': nrm(ks[28], (DEPTH, D_SHARED, D_MODEL), BETA * D_SHARED ** -0.5),
        'w_ple_gate': nrm(ks[29], (DEPTH, D_MODEL, D_MODEL), D_MODEL ** -0.5),
        'w_ple_proj': nrm(ks[30], (DEPTH, P_DIM, D_MODEL), BETA * P_DIM ** -0.5),
    }

def reference(x_prompt, x_sample, state_gla, state_pool, state_ret, p_prompt, p_sample,
              w_in_a, w_gk2, b_gk, g_norm_a, w_pool, b_pool, pool_scale, w_out_a,
              w_in_c, w_out_c, ln1_g, ln1_b, ln2_g, ln2_b,
              w_router, router_bias, w_exp_gate, w_exp_up, w_exp_down,
              w_sh_gate, w_sh_up, w_sh_down, w_ple_gate, w_ple_proj):
    W = dict(w_in_a=w_in_a, w_gk2=w_gk2, b_gk=b_gk, g_norm_a=g_norm_a, w_pool=w_pool,
             b_pool=b_pool, pool_scale=pool_scale, w_out_a=w_out_a, w_in_c=w_in_c,
             w_out_c=w_out_c, ln1_g=ln1_g, ln1_b=ln1_b, ln2_g=ln2_g, ln2_b=ln2_b,
             w_router=w_router, router_bias=router_bias, w_exp_gate=w_exp_gate,
             w_exp_up=w_exp_up, w_exp_down=w_exp_down, w_sh_gate=w_sh_gate,
             w_sh_up=w_sh_up, w_sh_down=w_sh_down, w_ple_gate=w_ple_gate,
             w_ple_proj=w_ple_proj)
    B = x_prompt.shape[0]
    dt = x_prompt.dtype
    z_gla = jnp.zeros((N_EVEN, B, H_A, DK_A, DV_A), dt)
    z_pool = jnp.zeros((N_EVEN, B, POOL_BUF, POOL_CH), dt)
    z_ret = jnp.zeros((N_ODD, B, H_C, DK_C, DV_C), dt)
    y_prompt, gla_p, pool_p, ret_p = trunk(x_prompt, p_prompt, z_gla, z_pool, z_ret, 0, W)
    y_sample, gla_s, pool_s, ret_s = trunk(x_sample, p_sample, state_gla, state_pool, state_ret,
                                           PAST_LEN, W)
    return (y_prompt, y_sample, gla_p, pool_p, ret_p, gla_s, pool_s, ret_s)


_drawn_inputs = setup_inputs


def setup_inputs(seed=0):
    import zlib

    import numpy as np

    out = dict(_drawn_inputs(seed))
    spreads = {}
    factors = {}
    for name, (base, spread) in spreads.items():
        noise = np.random.default_rng([zlib.crc32(name.encode()), seed]).standard_normal(out[name].shape)
        drawn = base * np.exp(spread * noise) if base else spread * noise
        out[name] = __import__('jax').numpy.asarray(drawn.astype(out[name].dtype))
    for name, factor in factors.items():
        out[name] = (out[name] * factor).astype(out[name].dtype)
    return out
```

```python
from contextlib import ExitStack

import numpy as np

import concourse.bass as bass
from concourse import mybir

F32 = mybir.dt.float32
U32 = mybir.dt.uint32
I32 = mybir.dt.int32
ALU = mybir.AluOpType
ACT = mybir.ActivationFunctionType
AX = mybir.AxisListType

P = 128
D = 1024
SEQ = 256
NSEQ = 8
DSEQ = 4
PAST = 2048
TS = NSEQ * DSEQ
T = SEQ + TS
CH = [(0, 128), (128, 128), (256, TS)]
KC = D // P
DEPTH = 2
H = 4
DKA = 64
DVA = 128
RANK = 16
CA = 16
NCA = SEQ // CA
WINDOWS = (2, 4, 8, 16)
PBUF = 15
DKC = 256
DVC = 512
E = 64
EG = 8
TOPG = 4
TOPK = 8
DE = 256
ROUTED = 2.5
PD = 256
ALPHA = (2.0 * DEPTH) ** 0.25
EPS = 1e-5
BLK = 64
PAIRS = E // 2
SLOTS = 6
PW = 4096
FAR = 4096.0
BIG = 1e30
EP = E + 4
QCOL, KCOL, VCOL, RCOL, GCOL, UCOL = 0, 256, 512, 1024, 1536, 1552


class Cut:

    def __init__(self, ap, size):
        self.ap, self.size, self.at = ap, size, 0

    def take(self, n):
        a = self.ap[:, self.at:self.at + n]
        self.at += n
        assert self.at <= self.size, (self.at, self.size)
        return a


def constants():
    p = np.arange(P)
    common = [np.eye(P), (p[:, None] < p[None, :]) * 1.0,
              np.tile(np.arange(BLK * 5), (P, 1)),
              np.stack([p + o - FAR for o, _ in CH], 1),
              np.stack([p + o - FAR - T for o, _ in CH], 1),
              np.tile((np.arange(8)[None, :] < np.arange(8)[:, None]).reshape(-1), (P, 1)),
              np.tile(np.eye(TS), (4, 1))]
    t = np.arange(T)
    first = np.where(t < SEQ, t % CA == 0, t % DSEQ == 0)
    causal = (p[:, None] // CA == p[None, :] // CA) & (p[:, None] <= p[None, :])
    s = np.arange(TS)
    causal_s = np.zeros((P, TS), bool)
    causal_s[:TS] = (s[:, None] // DSEQ == s[None, :] // DSEQ) & (s[:, None] <= s[None, :])
    inv = np.stack([1.0 / np.minimum(np.arange(16) + 1, w) for w in WINDOWS])
    even = [np.tile(1.0 - first, (P, 1)), causal * 1.0, causal_s * 1.0,
            (p[:, None] // CA == np.arange(8)[None, :]) * 1.0,
            ((p[:, None] // DSEQ) == np.arange(8)[None, :]) * 1.0,
            np.tile(inv.reshape(-1), (P, 1))]
    f = np.float32
    freq = (f(1.0) / np.power(f(10000.0), np.linspace(0.0, 1.0, DKC // 2, dtype=f), dtype=f)).astype(f)
    pos = np.concatenate([np.arange(SEQ), np.tile(PAST + np.arange(DSEQ), NSEQ)]).astype(f)
    ang = (freq[:, None] * pos[None, :]).astype(f).astype(np.float64)
    gam = 1.0 - 2.0 ** (-5.0 - np.arange(H))
    kscale = DKC ** -0.5
    dm = np.zeros((P, H, SEQ))
    tt = np.arange(SEQ)[None, :] - p[:, None]
    for h in range(H):
        dm[:, h] = np.where(tt >= 0, gam[h] ** np.maximum(tt, 0), 0) * kscale
    ds = np.zeros((P, H, TS))
    for h in range(H):
        ds[:TS, h] = causal_s[:TS] * gam[h] ** np.maximum(s[None, :] - s[:, None], 0) * kscale
    qm = np.zeros((P, H, NSEQ, TS))
    for h in range(H):
        for b in range(NSEQ):
            qm[:, h, b] = (s // DSEQ == b) * gam[h] ** (s % DSEQ + 1)
    kd = np.zeros((P, 2, H))
    for j in range(2):
        kd[:, j] = gam[None, :] ** (SEQ - 1 - 128 * j - p)[:, None] * kscale
    kds = np.zeros((P, 2, H))
    for a in range(2):
        kds[:, a] = (((p % TS) // DSEQ == p // TS + 4 * a)[:, None]
                     * gam[None, :] ** (DSEQ - 1 - p % DSEQ)[:, None] * kscale)
    odd = [np.cos(ang), np.sin(ang), dm.reshape(P, -1), ds.reshape(P, -1), qm.reshape(P, -1),
           kd.reshape(P, -1), kds.reshape(P, -1)]
    return [np.ascontiguousarray(np.concatenate([np.asarray(a, f) for a in x], 1), dtype=f)
            for x in (common, even, odd)]


def group_order():
    g = []

    def xt(tag):
        g.extend((tag, j, q) for j in range(3) for q in range(2))

    def out(tag):
        g.extend((tag, j, n) for n in range(2) for j in range(3))

    for l in range(DEPTH):
        xt(f"xTa{l}")
        if l % 2 == 0:
            g.append(("glr",))
            g.extend(("gk", f) for f in range(2))
            g.extend(("qk", f) for f in range(4))
            g.extend(("v", j) for j in range(3))
            g.extend(("r", f) for f in range(4))
            g.extend(("u", f) for f in range(4))
            g.append(("spT",))
            g.extend(("att", h) for h in range(H))
            for j in range(3):
                g.append(("kdT", j))
                g.extend(("dS", j, f, i) for f in range(2) for i in range(2))
            g.append(("puT",))
            g.append(("usT",))
            g.extend(("pool", f) for f in range(4))
            g.extend(("oT", h) for h in range(H))
            g.extend(("ms", h) for h in range(H))
        else:
            for h in range(H):
                g.extend(("qkh", h, f) for f in range(4))
                g.extend(("vv", h, j) for j in range(3))
                g.extend(("gg", h, f) for f in range(4))
                g.append(("ratt", h))
                g.append(("kT", h))
                g.append(("kTs", h))
                g.append(("o4", h))
                g.extend(("sn", h, b, e) for b in range(NSEQ) for e in range(2))
                g.extend(("sp", h, e) for e in range(2))
                g.extend(("roT", h, f) for f in range(4))
                g.append(("rms", h))
        out(f"out{l}")
        xt(f"xTb{l}")
        g.append((f"router{l}",))
        g.extend((f"sh{l}", f) for f in range(4))
        g.append((f"pT{l}",))
        g.append((f"cum{l}",))
        g.append((f"flag{l}",))
        out(f"shd{l}")
        out(f"pw{l}")
        g.append((f"moe{l}",))
        xt(f"xTc{l}")
        out(f"pg{l}")
    return g


ODD_GROUPS = ("qkh", "vv", "gg", "ratt", "kT", "kTs", "roT", "sn", "sp", "rms")


def plan_groups():
    at, used, nxt, banks = {}, [0] * 8, 0, 8
    for name in group_order():
        if name[0].startswith("moe"):
            at[name] = list(used)
            for b, n in ((0, 33), (1, 33), (2, 32), (3, 32), (4, 32), (5, 32), (6, 33)):
                used[b] += n
            continue
        if name[0] == "o4":
            b = 7
        else:
            banks = 7 if name[0] in ODD_GROUPS else 8
            b = nxt % banks
            nxt += 1
        at[name] = (b, used[b])
        used[b] += 1
    return at


def plan_panels():
    p = []
    for l in range(DEPTH):
        if l % 2 == 0:
            p += [(("qk",), ("qk", 3)), (("v",), ("v", 2)), (("r",), ("r", 3)), (("u",), ("u", 3))]
            p += [((f"out{l}", n), (f"out{l}", 2, n)) for n in range(2)]
        else:
            for h in range(H):
                p += [(("qk", h), ("qkh", h, 3)), (("v", h), ("vv", h, 2)), (("g", h), ("gg", h, 3))]
            p += [((f"out{l}", n, k), (f"out{l}", 2, n)) for n in range(2) for k in range(2)]
        p += [((f"shgu{l}",), (f"sh{l}", 3)), ((f"dp{l}",), (f"pw{l}", 2, 1))]
        p += [((f"moe{l}",), None)]
        p += [((f"pg{l}", n), (f"pg{l}", 2, n)) for n in range(2)]
    return p


def trunk(nc, A, O, C):
    GRP = plan_groups()
    PANELS = plan_panels()
    NUM, n = {}, 0
    for name, _ in PANELS:
        NUM[name] = n
        n += 3 * PAIRS if name[0].startswith("moe") else 1
    LAST = {}
    for name, g in PANELS:
        if name[0].startswith("moe"):
            l = int(name[0][3:])
            for k in range(3 * PAIRS):
                LAST[NUM[name] + k] = (f"moe{l}", k // 3, 5 if k % 3 == 2 else 2)
        else:
            LAST[NUM[name]] = g

    with ExitStack() as ctx:
        def sb(name, cols, dt=F32):
            return ctx.enter_context(nc.sbuf_tensor(name, [P, cols], dt))

        names = {}

        def sem(*name):
            key = "_".join(map(str, name))
            if key not in names:
                names[key] = ctx.enter_context(nc.semaphore(key))
            return names[key]

        W = sb("weights", SLOTS * PW)
        Xb = sb("x_tok", 3 * D)
        XTb = sb("x_feat", KC * T)
        LNb = sb("ln_rows", 2 * D)
        CC = sb("const", C[0].shape[1])
        SIDE = sb("side", 2048)
        SMb = sb("small", 600)
        ASZ = 17600
        AR = sb("arena", ASZ)
        PS = ctx.enter_context(nc.psum_tensor("ps", [P, 8, 512], F32))
        xd = nc.dram_tensor("x_rows", (T, D), F32, kind="Internal").ap()
        yd = nc.dram_tensor("y_slots", (TOPK * T, D), F32, kind="Internal").ap()

        X = Xb[:, :].rearrange("p (j n) -> p j n", j=3)
        XT = XTb[:, :].rearrange("p (c t) -> p c t", c=KC)
        LN = LNb[:, :].rearrange("p (k n) -> p k n", k=2)
        cc = Cut(CC[:, :], C[0].shape[1])
        ident, tri = cc.take(P), cc.take(P)
        iota = cc.take(BLK * 5)
        tokc, slotc = cc.take(3), cc.take(3)
        tri8 = cc.take(64)
        fold4 = cc.take(TS)

        sm = Cut(SMb[:, :], 600)
        ones = sm.take(P)
        onesA = sm.take(P)
        onesC = sm.take(P)
        eps, zero1 = sm.take(1), sm.take(1)
        rbias = sm.take(E)
        bnst = sm.take(12)
        bnag = sm.take(6)
        rstd = sm.take(3)
        colmax, flagf = sm.take(1), sm.take(1)
        flagi = sm.take(1).bitcast(I32)

        a = Cut(AR[:, :], ASZ)
        MTE = a.take(8 * T).rearrange("p (f t) -> p f t", f=8)
        CE = a.take(C[1].shape[1])
        ce = Cut(CE, C[1].shape[1])
        keep, mcau, mcau_s = ce.take(T), ce.take(P).bitcast(U32), ce.take(TS).bitcast(U32)
        mch, mch_s = ce.take(8), ce.take(8)
        invc = ce.take(64)
        wglr = a.take(8 * RANK).rearrange("p (c n) -> p c n", c=8)
        wgk2 = a.take(256)
        bgk, gnorm, bpool, pscale = a.take(2), a.take(1), a.take(4), a.take(4)
        wpool = a.take(512)
        glrT = a.take(T)
        LXB = a.take(4 * T)
        LX, LB = (LXB[:, 2 * T * i:2 * T * i + 2 * T].rearrange("p (f t) -> p f t", f=2) for i in range(2))
        KDF, QI, KI, EB = (a.take(2 * T).rearrange("p (f t) -> p f t", f=2) for _ in range(4))
        EN = LX
        SQE = LXB.rearrange("p (h t) -> p h t", h=4)
        V = a.take(3 * 512).rearrange("p (j n) -> p j n", j=3)
        UE = a.take(4 * (PBUF + SEQ)).rearrange("p (g t) -> p g t", g=4)
        US = a.take(4 * NSEQ * 19).rearrange("p (g b t) -> p g b t", g=4, b=NSEQ)
        PWK = [a.take(272) for _ in range(2)]
        USC = a.take(4 * TS).rearrange("p (g t) -> p g t", g=4)
        PUO = a.take(512)
        spl = a.take(512)
        SS = a.take(2 * 17 * 128).rearrange("p (f i v) -> p f i v", f=2, i=17)
        gs0 = LNb[:, :].rearrange("p (f b v) -> p f b v", f=2, b=8)
        KDM = SIDE[:, :].rearrange("p (i n) -> p i n", i=8)
        gsn = SIDE[:, :].rearrange("p (f b v) -> p f b v", f=2, b=8)
        DD = XTb[:, 0:4 * T].rearrange("p (g t) -> p g t", g=4)
        AT = XTb[:, 4 * T:8 * T].rearrange("p (h t) -> p h t", h=4)
        RSE = KDF
        a = Cut(AR[:, :], ASZ)
        MT = a.take(16 * T).rearrange("p (f t) -> p f t", f=16)
        CO = a.take(C[2].shape[1])
        co = Cut(CO, C[2].shape[1])
        cos, sin = co.take(T), co.take(T)
        dmask = co.take(4 * SEQ).rearrange("p (h t) -> p h t", h=4)
        dmask_s = co.take(4 * TS).rearrange("p (h t) -> p h t", h=4)
        qmask = co.take(4 * NSEQ * TS).rearrange("p (h b t) -> p h b t", h=4, b=NSEQ)
        kdec = co.take(8).rearrange("p (j h) -> p j h", j=2)
        kdec_s = co.take(8).rearrange("p (a h) -> p a h", a=2)
        RQ = a.take(4 * T).rearrange("p (f t) -> p f t", f=4)
        RT = a.take(2 * T).rearrange("p (f t) -> p f t", f=2)
        RV = a.take(3 * 512).rearrange("p (j n) -> p j n", j=3)
        KD = a.take(2 * 256).rearrange("p (j n) -> p j n", j=2)
        KDS = a.take(2 * 256).rearrange("p (a n) -> p a n", a=2)
        O4 = a.take(512)
        RSQ = a.take(4 * T).rearrange("p (f t) -> p f t", f=4)
        SPo = a.take(1024).rearrange("p (e n) -> p e n", e=2)
        NS0 = 3
        S0 = [a.take(1024).rearrange("p (e n) -> p e n", e=2) for _ in range(NS0)]
        XS4 = SIDE[:, 0:1024].rearrange("p (c a t) -> p c a t", c=8, a=4)
        QM = SIDE[:, 1024:1536].rearrange("p (e b t) -> p e b t", e=2, b=8)
        KS4 = SIDE[:, 1536:1792].rearrange("p (e a t) -> p e a t", e=2, a=4)
        ROT = LNb[:, 0:4 * T].rearrange("p (f t) -> p f t", f=4)
        RAT = LNb[:, 4 * T:4 * T + 384 + TS]
        a = Cut(AR[:, :], ASZ)
        F = a.take(3 * D).rearrange("p (j n) -> p j n", j=3)
        PP = a.take(3 * D).rearrange("p (j n) -> p j n", j=3)
        mark = a.at
        SC, SEL, MK, MR, MSK, CUM = (a.take(3 * E).rearrange("p (j e) -> p j e", j=3) for _ in range(6))
        G8 = a.take(24 * 8).rearrange("p (g k) -> p g k", g=24)
        GS, RK = a.take(24), a.take(24)
        GT8, GE8 = (a.take(192) for _ in range(2))
        T8 = a.take(24).rearrange("p (j k) -> p j k", j=3)
        DEN = a.take(3)
        POS = a.take(3 * EP).rearrange("p (j e) -> p j e", j=3)
        TAB = a.take(3 * EP * 4).rearrange("p (j e k) -> p j e k", j=3, e=EP)
        OH = [a.take(3 * P).rearrange("p (j a k) -> p j a k", j=3, a=2) for _ in range(2)]
        META = [a.take(8) for _ in range(2)]
        GATE = [a.take(1) for _ in range(2)]
        GI = [a.take(1).bitcast(U32) for _ in range(2)]
        SI = [a.take(1).bitcast(U32) for _ in range(2)]
        HSf = a.take(2 * T).rearrange("p (f t) -> p f t", f=2)
        PT = a.take(2 * T).rearrange("p (f t) -> p f t", f=2)
        PIN = a.take(3 * PD).rearrange("p (j n) -> p j n", j=3)
        WR = a.take(KC * E)
        XG = [a.take(D) for _ in range(2)]
        HS = [a.take(DE) for _ in range(2)]
        HH = [a.take(DE) for _ in range(2)]
        HT = [a.take(2 * P).rearrange("p (c t) -> p c t", c=2) for _ in range(2)]
        YS = [SIDE[:, D * i:D * i + D] for i in range(2)]
        XGT = [XTb[:, D * i:D * i + D].rearrange("p (c t) -> p c t", c=KC) for i in range(2)]
        YK = AR[:, mark:mark + TOPK * D].rearrange("p (k n) -> p k n", k=TOPK)
        SG = [AR[:, mark + 512 * i:mark + 512 * i + 512] for i in range(2)]

        def wp(num):
            s = num % SLOTS
            return W[:, s * PW:(s + 1) * PW]

        bank_full = [sem("bank_full", b) for b in range(8)]
        bank_free = [sem("bank_emptied", b) for b in range(8)]
        slot_full = [sem("panel_landed", s) for s in range(SLOTS)]
        phase_end = sem("phase_end")

        def bank(name):
            return PS[:, GRP[name][0], :]

        def full(eng, name):
            b, u = GRP[name]
            eng.wait_ge(bank_full[b], u + 1)

        def emptied(eng, name):
            b, u = GRP[name]
            eng.wait_ge(bank_free[b], u + 1)

        def landed(eng, name):
            n = NUM[name]
            eng.wait_ge(slot_full[n % SLOTS], 32 * (n // SLOTS + 1))

        class Steps:

            def __init__(self, eng, s):
                self.eng, self.sem, self.n, self.last, self.counts, self.phases = eng, s, 0, None, {}, 0

            @property
            def after(self):
                if self.last is not None:
                    self.eng.wait_ge(*self.last)
                return self.eng

            def run(self, ins):
                ins.then_inc(self.sem, 1)
                self.n += 1
                self.last = (self.sem, self.n)

            def free(self, ins, name):
                b, u = GRP[name]
                ins.then_inc(bank_free[b], 1)
                self.last = (bank_free[b], u + 1)

            def tell(self, ins, s):
                k = self.counts.get(id(s), 0) + 1
                self.counts[id(s)] = k
                ins.then_inc(s, 1)
                self.last = (s, k)

            def phase(self):
                self.phases += 1
                self.after.nop().then_inc(phase_end, 1)
                self.eng.wait_ge(phase_end, 4 * self.phases)
                self.last = None

        block = ctx.enter_context(nc.Block())

        def tokens(eng, dst, src, s):
            pr, sa = src
            eng.dma_start(dst[:, 0:2, :], pr.rearrange("(j p) n -> p j n", p=P)).then_inc(s, 16)
            eng.dma_start(dst[0:TS, 2, :], sa).then_inc(s, 16)

        def norm_rows(eng, l, k):
            for i, nm in enumerate((f"ln{k}_g", f"ln{k}_b")):
                eng.dma_start(LN[:, i, :], A[nm][l:l + 1, :].broadcast_to([P, D])).then_inc(sem("ln_in", l, k), 16)

        @block.sync
        def _(sp):
            def wait_slot(num):
                if num >= SLOTS:
                    g = LAST[num - SLOTS]
                    if g[0].startswith("moe"):
                        sp.wait_ge(bank_full[g[2]], GRP[(g[0],)][g[2]] + g[1] + 1)
                    else:
                        full(sp, g)

            def panel(name, parts):
                num = NUM[name]
                wait_slot(num)
                for dst, src in parts(wp(num)):
                    sp.dma_start(dst, src).then_inc(slot_full[num % SLOTS], 16)

            def split_cols(w, lo):
                s = w.rearrange("(p c) n -> p c n", c=KC)
                return lambda dst: [
                    (dst.rearrange("p (c n) -> p c n", c=KC)[:, 4 * k:4 * k + 4, :],
                     s[:, 4 * k:4 * k + 4, lo:lo + 512]) for k in range(2)]

            def out_rows(w, k0, lo):
                s = w.rearrange("(t p) n -> p t n", p=P)
                return lambda dst: [
                    (dst.rearrange("p (t n) -> p t n", t=8)[:, 4 * k:4 * k + 4, :],
                     s[:, k0 + 4 * k:k0 + 4 * k + 4, lo:lo + 512]) for k in range(2)]

            def two(a0, a1, how):
                return lambda dst: [(how(dst[:, 0:2048]), a0), (how(dst[:, 2048:4096]), a1)]

            def flat(x):
                return x

            sp.dma_start(CC[:, :], C[0]).then_inc(sem("const_in"), 16)
            tokens(sp, X, (A["x_prompt"][0], A["x_sample"].rearrange("b s d -> (b s) d")), sem("x_in"))

            for l in range(DEPTH):
                if l % 2 == 0:
                    wi = A["w_in_a"][0]
                    s = sem("even_in")
                    sp.dma_start(wglr, wi.rearrange("(p c) n -> p c n", c=KC)[:, :, GCOL:GCOL + RANK]).then_inc(s, 16)
                    sp.dma_start(wgk2[0:RANK, :], A["w_gk2"][0]).then_inc(s, 16)
                    sp.dma_start(bgk, A["b_gk"][0].rearrange("(f p) -> p f", p=P), allow_slow_non_contiguous=True).then_inc(s, 16)
                    sp.dma_start(CE, C[1]).then_inc(s, 16)
                    sp.dma_start(gnorm, A["g_norm_a"][0].rearrange("(p o) -> p o", o=1), allow_slow_non_contiguous=True).then_inc(s, 16)
                    sp.dma_start(bpool, A["b_pool"][0].rearrange("g p -> p g"), allow_slow_non_contiguous=True).then_inc(s, 16)
                    sp.dma_start(pscale, A["pool_scale"][0].rearrange("(g p) -> p g", p=P), allow_slow_non_contiguous=True).then_inc(s, 16)
                    sp.dma_start(wpool.rearrange("p (g n) -> p g n", g=4), A["w_pool"][0].rearrange("g c d -> c g d")).then_inc(s, 16)
                    sp.dma_start(spl[0:NSEQ * PBUF, :], A["state_pool"][0].rearrange("b t c -> (b t) c")).then_inc(s, 16)
                    for f in range(2):
                        for r in range(2):
                            sp.dma_start(gs0[64 * r:64 * r + 64, f, :, :],
                                         A["state_gla"][0][:, 2 * f + r].rearrange("b k v -> k b v")).then_inc(s, 16)
                    panel(("qk",), split_cols(wi, 0))
                    panel(("v",), split_cols(wi, VCOL))
                    panel(("r",), split_cols(wi, RCOL))
                    panel(("u",), split_cols(wi, UCOL))
                    for n in range(2):
                        panel((f"out{l}", n), out_rows(A["w_out_a"][0], 0, 512 * n))
                else:
                    wi = A["w_in_c"][0].rearrange("(p c) n -> p c n", c=KC)
                    for h in range(H):
                        panel(("qk", h), two(wi[:, :, 256 * h:256 * h + 256], wi[:, :, 1024 + 256 * h:1280 + 256 * h],
                                             lambda x: x.rearrange("p (c n) -> p c n", c=KC)))
                        panel(("v", h), split_cols(A["w_in_c"][0], 2048 + 512 * h))
                        panel(("g", h), split_cols(A["w_in_c"][0], 4096 + 512 * h))
                    for n in range(2):
                        for k in range(2):
                            panel((f"out{l}", n, k), out_rows(A["w_out_c"][0], 8 * k, 512 * n))
                rp = lambda w: w.rearrange("(p c) n -> p (c n)", c=KC)
                panel((f"shgu{l}",), two(rp(A["w_sh_gate"][l]), rp(A["w_sh_up"][l]), flat))
                tp = lambda w: w.rearrange("(f p) n -> p f n", p=P)
                panel((f"dp{l}",), two(tp(A["w_sh_down"][l]), tp(A["w_ple_proj"][l]),
                                       lambda x: x.rearrange("p (f n) -> p f n", f=2)))
                n0 = NUM[(f"moe{l}",)]
                base = GRP[(f"moe{l}",)]

                def expert_panel(num, e0, k):
                    s, dst = num % SLOTS, wp(num)
                    if k < 2:
                        halves = [(A["w_exp_gate"], e0 + k), (A["w_exp_up"], e0 + k)]
                    else:
                        halves = [(A["w_exp_down"], e0), (A["w_exp_down"], e0 + 1)]
                    for q, (w, e) in enumerate(halves):
                        if isinstance(e, int):
                            src = w[l, e:e + 1]
                        else:
                            src = w[l, bass.ds(e, 1)]
                        c = KC if k < 2 else 2
                        sp.dma_start(dst[:, 2048 * q:2048 * q + 2048],
                                     src.rearrange("o (p c) n -> (o p) (c n)", c=c)).then_inc(slot_full[s], 16)

                for pr in range(2):
                    for k in range(3):
                        wait_slot(n0 + 3 * pr + k)
                        expert_panel(n0 + 3 * pr + k, 2 * pr, k)
                with sp.Fori(1, PAIRS // 2) as it:
                    for u in range(2):
                        for k in range(3):
                            b = 5 if k == 2 else 2
                            sp.wait_ge(bank_full[b], base[b] + u - 1 + 2 * it)
                            expert_panel(n0 + 3 * u + k, 4 * it + 2 * u, k)
                for b in (2, 5):
                    sp.wait_ge(bank_full[b], base[b] + PAIRS)
                sp.wait_ge(sem("flag_ready", l), 1)
                go = sp.value_load(flagi[0:1, 0:1], min_val=0, max_val=1)
                with sp.If(go > 0):
                    sp.sem_inc(sem("ov_y", l), 1)
                    with sp.Fori(0, 4) as m:
                        with sp.Fori(0, PAIRS) as pr:
                            sp.wait_ge(sem("ov_y", l), m * PAIRS + pr + 1)
                            for k in range(3):
                                dst = W[:, k * PW:(k + 1) * PW]
                                for q in range(2):
                                    w = (A["w_exp_gate"], A["w_exp_up"])[q] if k < 2 else A["w_exp_down"]
                                    e = 2 * pr + (k if k < 2 else q)
                                    sp.dma_start(dst[:, 2048 * q:2048 * q + 2048],
                                                 w[l, bass.ds(e, 1)].rearrange("o (p c) n -> (o p) (c n)", c=KC if k < 2 else 2)
                                                 ).then_inc(sem("ov_w", l), 16)
                    sp.wait_ge(sem("ov_y", l), 4 * PAIRS + 1)
                sp.nop()
                for n in range(2):
                    panel((f"pg{l}", n), split_cols(A["w_ple_gate"][l], 512 * n))
                sp.wait_ge(sem("all_scattered", l), 1)
                ys = yd.rearrange("(k t) n -> t k n", k=TOPK)
                for j, (o, r) in enumerate(CH):
                    if j:
                        sp.wait_ge(sem("y_summed", l), j)
                    sp.dma_start(YK[0:r, :, :], ys[o:o + r]).then_inc(sem("y_in", l), 16)

        def even_pe(pe, st, begin, end, feat, tok):
            pe.wait_ge(sem("even_in"), 16 * 13)
            ps = begin(("glr",))
            for c in range(KC):
                last = pe.matmul(ps[0:RANK, 0:T], wglr[:, c, :], XT[:, c, :], start=(c == 0), stop=(c == KC - 1))
            end(last, ("glr",))
            emptied(pe, ("glr",))
            for f in range(2):
                ps = begin(("gk", f))
                end(pe.matmul(ps[:, 0:T], wgk2[0:RANK, P * f:P * f + P], glrT[0:RANK, :], start=True, stop=True), ("gk", f))
            landed(pe, ("qk",))
            w = wp(NUM[("qk",)]).rearrange("p (c n) -> p c n", c=KC)
            for f in range(4):
                feat(("qk", f), lambda c: w[:, c, P * f:P * f + P])
            landed(pe, ("v",))
            w1 = wp(NUM[("v",)]).rearrange("p (c n) -> p c n", c=KC)
            for j, (o, r) in enumerate(CH):
                tok(("v", j), lambda c: XT[:, c, o:o + r], lambda c: w1[:, c, :], r, KC)
            for nm in ("r", "u"):
                landed(pe, (nm,))
                w2 = wp(NUM[(nm,)]).rearrange("p (c n) -> p c n", c=KC)
                for f in range(4):
                    feat((nm, f), lambda c: w2[:, c, P * f:P * f + P])
            ps = begin(("spT",))
            nb = NSEQ * PBUF
            for g in range(4):
                last = pe.transpose(ps[:, nb * g:nb * g + nb], spl[0:nb, P * g:P * g + P], ident[0:nb, 0:nb])
            end(last, ("spT",))
            for f in range(4):
                emptied(pe, ("qk", f))
            for h in range(H):
                f, b = h // 2, 64 * (h % 2)
                ps = begin(("att", h))
                for j, (o, r) in enumerate(CH):
                    last = pe.matmul(ps[0:r, o:o + r], KI[b:b + 64, f, o:o + r], QI[b:b + 64, f, o:o + r],
                                     start=True, stop=True)
                end(last, ("att", h))
            for j, (o, r) in enumerate(CH):
                ps = begin(("kdT", j))
                for f in range(2):
                    last = pe.transpose(ps[0:r, P * f:P * f + P], KDF[:, f, o:o + r], ident)
                end(last, ("kdT", j))
                emptied(pe, ("kdT", j))
                emptied(pe, ("v", j))
                for f in range(2):
                    for i2 in range(2):
                        ps = begin(("dS", j, f, i2))
                        for i in range(4):
                            for k in range(2):
                                h = 2 * f + k
                                last = pe.matmul(ps[64 * k:64 * k + 64, P * i:P * i + P],
                                                 KDM[0:r, 4 * i2 + i, 64 * h:64 * h + 64],
                                                 V[0:r, j, P * h:P * h + P], start=True, stop=True)
                        end(last, ("dS", j, f, i2))
            for nm, n in (("puT", PBUF), ("usT", TS)):
                for f in range(4):
                    emptied(pe, ("u", f))
                ps = begin((nm,))
                for g in range(4):
                    src = UE[:, g, SEQ:SEQ + PBUF] if nm == "puT" else USC[:, g, :]
                    last = pe.transpose(ps[0:n, P * g:P * g + P], src, ident)
                end(last, (nm,))
            for g in range(4):
                pe.wait_ge(sem("pool_d"), g + 1)
                ps = begin(("pool", g))
                end(pe.matmul(ps[:, 0:T], wpool[:, P * g:P * g + P], DD[:, g, :], start=True, stop=True), ("pool", g))
            pe.wait_ge(sem("states"), 1)
            for h in range(H):
                f, b = h // 2, 64 * (h % 2)
                emptied(pe, ("att", h))
                ps = begin(("oT", h))
                for j, (o, r) in enumerate(CH):
                    pe.matmul(ps[:, o:o + r], V[0:r, j, P * h:P * h + P], AT[0:r, h, o:o + r],
                              start=(j == 0), stop=False, skip_group_check=True)
                for i in range(1, NCA):
                    pe.matmul(ps[:, CA * i:CA * i + CA], SS[b:b + 64, f, i, :], QI[b:b + 64, f, CA * i:CA * i + CA],
                              start=False, stop=False, skip_group_check=True)
                for i in range(NSEQ):
                    c = SEQ + DSEQ * i
                    last = pe.matmul(ps[:, c:c + DSEQ], gs0[b:b + 64, f, i, :], QI[b:b + 64, f, c:c + DSEQ],
                                     start=False, stop=(i == NSEQ - 1), skip_group_check=True)
                end(last, ("oT", h))
            for h in range(H):
                pe.wait_ge(sem("sq"), h + 1)
                ps = begin(("ms", h))
                end(pe.matmul(ps[:, 0:T], onesA, SQE[:, h, :], start=True, stop=True), ("ms", h))

        def odd_pe(pe, st, begin, end, feat, tok):
            pe.wait_ge(sem("xs4"), 1)
            for h in range(H):
                landed(pe, ("qk", h))
                w = wp(NUM[("qk", h)]).rearrange("p (m c n e) -> p m c n e", m=2, c=KC, e=2)
                for f in range(4):
                    feat(("qkh", h, f), lambda c: w[:, f // 2, c, :, f % 2])
                landed(pe, ("v", h))
                w1 = wp(NUM[("v", h)]).rearrange("p (c n) -> p c n", c=KC)
                for j, (o, r) in enumerate(CH):
                    if j < 2:
                        tok(("vv", h, j), lambda c: XT[:, c, o:o + r], lambda c: w1[:, c, :], r, KC)
                    else:
                        tok(("vv", h, j), lambda c: XS4[:, c].rearrange("p a t -> p (a t)"), lambda c: w1[:, c, :], P, KC)
                landed(pe, ("g", h))
                w2 = wp(NUM[("g", h)]).rearrange("p (c n) -> p c n", c=KC)
                for f in range(4):
                    feat(("gg", h, f), lambda c: w2[:, c, P * f:P * f + P])
                pe.wait_ge(sem("roped"), 2 * h + 2)
                pe.wait_ge(sem("odd_in"), 16)
                ps = begin(("ratt", h))
                for (s0, t0, n, r, c0) in ((0, 0, SEQ, P, 0), (P, P, P, P, SEQ), (SEQ, SEQ, TS, TS, SEQ + P)):
                    for e in range(2):
                        last = pe.matmul(ps[0:r, c0:c0 + n], RQ[:, 2 + e, s0:s0 + r], RQ[:, e, t0:t0 + n],
                                         start=(e == 0), stop=(e == 1))
                end(last, ("ratt", h))
                ps = begin(("kT", h))
                for j in range(2):
                    for e in range(2):
                        last = pe.transpose(ps[:, 256 * j + P * e:256 * j + P * e + P], RQ[:, 2 + e, P * j:P * j + P], ident)
                end(last, ("kT", h))
                pe.wait_ge(sem("sample_qk"), h + 1)
                ps = begin(("kTs", h))
                for e in range(2):
                    last = pe.transpose(ps[:, P * e:P * e + P], KS4[:, e].rearrange("p a t -> p (a t)"), ident)
                end(last, ("kTs", h))
                pso = begin(("o4", h))
                emptied(pe, ("kTs", h))
                emptied(pe, ("vv", h, 2))
                for b in range(NSEQ):
                    k = NSEQ * h + b
                    q = 32 * (b % 4)
                    pe.wait_ge(sem("s0_in", k % NS0), 16 * (k // NS0 + 1))
                    for e in range(2):
                        last = pe.matmul(pso[q:q + 32, :], QM[:, e, b, :], S0[k % NS0][:, e, :],
                                         start=(b < 4 and e == 0), stop=(b >= 4 and e == 1), skip_group_check=True)
                    if b == NSEQ - 1:
                        end(last, ("o4", h))
                    for e in range(2):
                        ps = begin(("sn", h, b, e))
                        end(pe.matmul(ps, KDS[q:q + 32, b // 4, P * e:P * e + P], RV[q:q + 32, 2, :],
                                      start=True, stop=True), ("sn", h, b, e))
                emptied(pe, ("kT", h))
                for e in range(2):
                    ps = begin(("sp", h, e))
                    for j in range(2):
                        emptied(pe, ("vv", h, j))
                        last = pe.matmul(ps, KD[:, j, P * e:P * e + P], RV[:, j, :], start=(j == 0), stop=(j == 1))
                    end(last, ("sp", h, e))
                emptied(pe, ("ratt", h))
                emptied(pe, ("o4", h))
                for f in range(4):
                    ps = begin(("roT", h, f))
                    vf = slice(P * f, P * f + P)
                    pe.matmul(ps[:, 0:SEQ], RV[:, 0, vf], RAT[:, 0:SEQ], start=True, stop=False, skip_group_check=True)
                    pe.matmul(ps[:, P:SEQ], RV[:, 1, vf], RAT[:, SEQ:SEQ + P], start=False, stop=False, skip_group_check=True)
                    pe.matmul(ps[:, SEQ:T], RV[0:TS, 2, vf], RAT[0:TS, SEQ + P:SEQ + P + TS], start=False, stop=False,
                              skip_group_check=True)
                    end(pe.matmul(ps[:, SEQ:T], O4[:, vf], fold4, start=False, stop=True, skip_group_check=True),
                        ("roT", h, f))
                pe.wait_ge(sem("osq"), 4 * h + 4)
                ps = begin(("rms", h))
                for f in range(4):
                    last = pe.matmul(ps[:, 0:T], onesC, RSQ[:, f, :], start=(f == 0), stop=(f == 3))
                end(last, ("rms", h))

        @block.tensor
        def _(pe):
            st = Steps(pe, sem("pe_steps"))
            order = iter(group_order())

            def begin(name):
                assert next(order) == name, name
                b, u = GRP[name]
                if u:
                    pe.wait_ge(bank_free[b], u)
                return PS[:, b, :]

            def end(ins, name):
                b, u = GRP[name]
                ins.then_inc(bank_full[b], 1)
                st.last = (bank_full[b], u + 1)

            def transpose_x(tag):
                for j, (o, r) in enumerate(CH):
                    xc = X[0:r, j, :].rearrange("p (m c) -> p c m", c=KC)
                    for q in range(2):
                        ps = begin((tag, j, q))
                        for c in range(4):
                            last = pe.transpose(ps[:, c * P:c * P + r], xc[:, 4 * q + c, :], ident[0:r, 0:r])
                        end(last, (tag, j, q))

            def have_xt(tag):
                for j in range(3):
                    for q in range(2):
                        emptied(pe, (tag, j, q))

            def feat(name, lhs, n=KC):
                ps = begin(name)
                for c in range(n):
                    last = pe.matmul(ps[:, 0:T], lhs(c), XT[:, c, :], start=(c == 0), stop=(c == n - 1))
                end(last, name)

            def tok(name, lhs, rhs, r, n, w=512):
                ps = begin(name)
                for c in range(n):
                    last = pe.matmul(ps[0:r, 0:w], lhs(c), rhs(c), start=(c == 0), stop=(c == n - 1))
                end(last, name)

            pe.wait_ge(sem("const_in"), 16)
            pe.wait_ge(sem("x_in"), 32)
            pe.wait_ge(sem("ones_set"), 1)
            for l in range(DEPTH):
                if l:
                    pe.wait_ge(sem("x_out", l - 1), 1)
                transpose_x(f"xTa{l}")
                have_xt(f"xTa{l}")
                if l % 2 == 0:
                    even_pe(pe, st, begin, end, feat, tok)
                else:
                    odd_pe(pe, st, begin, end, feat, tok)
                nk = 8 if l % 2 == 0 else 16
                pe.wait_ge(sem("mixed", l), 1)
                MX = MTE if l % 2 == 0 else MT
                for n in range(2):
                    for j, (o, r) in enumerate(CH):
                        name = (f"out{l}", j, n)
                        if l % 2 == 0:
                            landed(pe, (f"out{l}", n))
                            w = [wp(NUM[(f"out{l}", n)]).rearrange("p (t n) -> p t n", t=8)]
                        else:
                            landed(pe, (f"out{l}", n, 0))
                            landed(pe, (f"out{l}", n, 1))
                            w = [wp(NUM[(f"out{l}", n, k)]).rearrange("p (t n) -> p t n", t=8) for k in range(2)]
                        tok(name, lambda c: MX[:, c, o:o + r], lambda c: w[c // 8][:, c % 8, :], r, nk)
                st.phase()

                pe.wait_ge(sem("x_mid", l), 3)
                transpose_x(f"xTb{l}")
                have_xt(f"xTb{l}")
                pe.wait_ge(sem("router_in", l), 16)
                ps = begin((f"router{l}",))
                wr = WR.rearrange("p (c n) -> p c n", c=KC)
                for j, (o, r) in enumerate(CH):
                    for c in range(KC):
                        last = pe.matmul(ps[0:r, E * j:E * j + E], XT[:, c, o:o + r], wr[:, c, :],
                                         start=(c == 0), stop=(c == KC - 1))
                end(last, (f"router{l}",))
                landed(pe, (f"shgu{l}",))
                sg = wp(NUM[(f"shgu{l}",)]).rearrange("p (m c n) -> p m c n", m=2, c=KC)
                for f in range(4):
                    feat((f"sh{l}", f), lambda c: sg[:, f // 2, c, P * (f % 2):P * (f % 2) + P])
                pe.wait_ge(sem("p_in", l), 32)
                ps = begin((f"pT{l}",))
                for f in range(2):
                    for j in range(2):
                        last = pe.transpose(ps[:, P * (2 * f + j):P * (2 * f + j) + P], PIN[:, j, P * f:P * f + P], ident)
                end(last, (f"pT{l}",))
                pe.wait_ge(sem("chosen", l), 1)
                ps = begin((f"cum{l}",))
                for j, (o, r) in enumerate(CH):
                    for jj in range(j):
                        pe.matmul(ps[0:r, E * j:E * j + E], ones[:, 0:r], MSK[:, jj, :], start=(jj == 0), stop=False)
                    last = pe.matmul(ps[0:r, E * j:E * j + E], tri[0:r, 0:r], MSK[0:r, j, :], start=(j == 0), stop=True)
                for f in range(2):
                    last = pe.transpose(ps[:, 256 + TS * f:256 + TS * f + TS], PIN[0:TS, 2, P * f:P * f + P], ident[0:TS, 0:TS])
                end(last, (f"cum{l}",))
                pe.wait_ge(sem("colmax", l), 1)
                ps = begin((f"flag{l}",))
                end(pe.transpose(ps[0:1, 0:P], colmax, ident), (f"flag{l}",))
                landed(pe, (f"dp{l}",))
                dp = wp(NUM[(f"dp{l}",)]).rearrange("p (m f n) -> p m f n", m=2, f=2)
                for f in range(2):
                    emptied(pe, (f"sh{l}", 2 + f))
                for n in range(2):
                    for j, (o, r) in enumerate(CH):
                        tok((f"shd{l}", j, n), lambda c: HSf[:, c, o:o + r],
                            lambda c: dp[:, 0, c, 512 * n:512 * n + 512], r, 2)

                emptied(pe, (f"pT{l}",))
                emptied(pe, (f"cum{l}",))
                for n in range(2):
                    for j, (o, r) in enumerate(CH):
                        tok((f"pw{l}", j, n), lambda c: PT[:, c, o:o + r],
                            lambda c: dp[:, 1, c, 512 * n:512 * n + 512], r, 2)

                assert next(order) == (f"moe{l}",)
                base = GRP[(f"moe{l}",)]
                n0 = NUM[(f"moe{l}",)]

                def meta(u, pr, ps):
                    for j, (o, r) in enumerate(CH):
                        tb = TAB[0:r, j].rearrange("p e k -> p (e k)")
                        rhs = tb[:, 8 * pr:8 * pr + 8] if isinstance(pr, int) else tb[:, bass.ds(8 * pr, 8)]
                        last = pe.matmul(ps[:, 0:8], OH[u][0:r, j].rearrange("p a k -> p (a k)"), rhs,
                                         start=(j == 0), stop=(j == 2))
                    return last

                def turn_rows(u, q, ps):
                    xc = XG[u].rearrange("p (m c) -> p c m", c=KC)
                    for c in range(4):
                        last = pe.transpose(ps[:, c * P:c * P + P], xc[:, 4 * q + c, :], ident)
                    return last

                def gate_up(u, w, ps):
                    for c in range(KC):
                        for s in range(2):
                            rhs = w[s].rearrange("p (m c n) -> p m c n", m=2, c=KC)[:, :, c, :]
                            last = pe.matmul(ps[64 * s:64 * s + 64, :], XGT[u][:, c, 64 * s:64 * s + 64], rhs,
                                             start=(c == 0), stop=(c == KC - 1))
                    return last

                def turn_hidden(u, ps):
                    hc = HH[u].rearrange("p (m c) -> p c m", c=2)
                    for c in range(2):
                        last = pe.transpose(ps[:, c * P:c * P + P], hc[:, c, :], ident)
                    return last

                def down(u, n, w, ps):
                    wd = w.rearrange("p (s c n) -> p s c n", s=2, c=2)
                    for c in range(2):
                        for s in range(2):
                            last = pe.matmul(ps[64 * s:64 * s + 64, :], HT[u][:, c, 64 * s:64 * s + 64],
                                             wd[:, s, c, 512 * n:512 * n + 512], start=(c == 0), stop=(c == 1))
                    return last

                pe.wait_ge(sem("onehot", l), 1)
                if base[6]:
                    pe.wait_ge(bank_free[6], base[6])
                meta(0, 0, PS[:, 6, :]).then_inc(bank_full[6], 1)
                pe.wait_ge(sem("gathered", l, 0), 16)
                for q in range(2):
                    pe.wait_ge(bank_free[q], base[q])
                    turn_rows(0, q, PS[:, q, :]).then_inc(bank_full[q], 1)
                for b in range(2, 6):
                    pe.wait_ge(bank_free[b], base[b])
                with pe.Fori(0, PAIRS // 2) as it:
                    for u in range(2):
                        v = 1 - u
                        pr = 2 * it + u
                        pe.wait_ge(sem("onehot", l), pr + 2)
                        pe.wait_ge(bank_free[6], base[6] + 1 + pr)
                        meta(v, pr + 1, PS[:, 6, :]).then_inc(bank_full[6], 1)
                        for q in range(2):
                            pe.wait_ge(bank_free[q], base[q] + 1 + pr)
                        for k in range(2):
                            n = n0 + 3 * u + k
                            pe.wait_ge(slot_full[n % SLOTS], 32 * (n // SLOTS + 1) + 32 * it)
                        pe.wait_ge(bank_free[2], base[2] + pr)
                        gate_up(u, [wp(n0 + 3 * u), wp(n0 + 3 * u + 1)], PS[:, 2, :]).then_inc(bank_full[2], 1)
                        if u == 0:
                            pe.wait_ge(sem("gathered", l, 1), 16 + 16 * it)
                        else:
                            pe.wait_ge(sem("gathered", l, 0), 32 + 16 * it)
                        for q in range(2):
                            turn_rows(v, q, PS[:, q, :]).then_inc(bank_full[q], 1)
                        pe.wait_ge(bank_free[2], base[2] + pr + 1)
                        pe.wait_ge(bank_free[3], base[3] + pr)
                        turn_hidden(u, PS[:, 3, :]).then_inc(bank_full[3], 1)
                        pe.wait_ge(bank_free[3], base[3] + pr + 1)
                        n = n0 + 3 * u + 2
                        pe.wait_ge(slot_full[n % SLOTS], 32 * (n // SLOTS + 1) + 32 * it)
                        for h in range(2):
                            pe.wait_ge(bank_free[4 + h], base[4 + h] + pr)
                            down(u, h, wp(n0 + 3 * u + 2), PS[:, 4 + h, :]).then_inc(bank_full[4 + h], 1)
                pe.wait_ge(sem("flag_ready", l), 1)
                go = pe.value_load(flagi[0:1, 0:1], min_val=0, max_val=1)
                with pe.If(go > 0):
                    for b, k in ((0, 33), (1, 33), (2, 32), (3, 32), (4, 32), (5, 32), (6, 33)):
                        pe.wait_ge(bank_free[b], base[b] + k)
                    with pe.Fori(0, 4) as m:
                        with pe.Fori(0, PAIRS) as pr:
                            s = m * PAIRS + pr
                            pe.wait_ge(sem("ov_onehot", l), s + 1)
                            meta(0, pr, PS[:, 6, :]).then_inc(sem("ov_meta", l), 1)
                            pe.wait_ge(sem("ov_gathered", l), 16 * s + 16)
                            turn_rows(0, 0, PS[:, 0, :])
                            turn_rows(0, 1, PS[:, 1, :]).then_inc(sem("ov_rows", l), 1)
                            pe.wait_ge(sem("ov_xgt", l), s + 1)
                            pe.wait_ge(sem("ov_w", l), 96 * s + 96)
                            gate_up(0, [W[:, k * PW:(k + 1) * PW] for k in range(2)], PS[:, 2, :]).then_inc(sem("ov_gu", l), 1)
                            pe.wait_ge(sem("ov_hidden", l), s + 1)
                            turn_hidden(0, PS[:, 3, :]).then_inc(sem("ov_hT", l), 1)
                            pe.wait_ge(sem("ov_hTc", l), s + 1)
                            down(0, 0, W[:, 2 * PW:3 * PW], PS[:, 4, :])
                            down(0, 1, W[:, 2 * PW:3 * PW], PS[:, 5, :]).then_inc(sem("ov_y", l), 1)
                pe.nop()
                st.last = None

                pe.wait_ge(sem("x_ln2", l), 3)
                transpose_x(f"xTc{l}")
                have_xt(f"xTc{l}")
                for n in range(2):
                    landed(pe, (f"pg{l}", n))
                    w = wp(NUM[(f"pg{l}", n)]).rearrange("p (c n) -> p c n", c=KC)
                    for j, (o, r) in enumerate(CH):
                        tok((f"pg{l}", j, n), lambda c: XT[:, c, o:o + r], lambda c: w[:, c, :], r, KC)
                st.phase()

        @block.scalar
        def _(act):
            st = Steps(act, sem("act_steps"))

            def copy(dst, src, **k):
                return act.activation(dst, src, ACT.Copy, **k)

            def x_half(tag):
                for j, (o, r) in enumerate(CH):
                    full(act, (tag, j, 0))
                    st.free(copy(XT[:, 0:4, o:o + r],
                                 bank((tag, j, 0)).rearrange("p (c t) -> p c t", c=4)[:, :, 0:r]), (tag, j, 0))

            def norm_root(l, k):
                act.wait_ge(sem("variance", l, k), 3)
                st.tell(act.activation(rstd, bnag.rearrange("p (j k) -> p j k", j=3)[:, :, 1], ACT.Sqrt, bias=eps),
                        sem("std", l, k))

            act.wait_ge(sem("ones_set"), 1)
            for l in range(DEPTH):
                if l % 2:
                    act.dma_start(CO, C[2]).then_inc(sem("odd_in"), 16)
                x_half(f"xTa{l}")
                if l % 2 == 0:
                    full(act, ("glr",))
                    st.free(copy(glrT[0:RANK, :], bank(("glr",))[0:RANK, 0:T]), ("glr",))
                    act.wait_ge(sem("gate_logits"), 1)
                    st.run(act.activation(LB, LB, ACT.Exp, scale=-1.0))
                    st.tell(st.after.activation(LB, LB, ACT.Ln, bias=ones[:, 0:1]), sem("log_term"))
                    act.wait_ge(sem("summed"), 1)
                    st.tell(act.activation(EB, LB, ACT.Exp, scale=1.0 / 16), sem("decays"))
                    st.tell(act.activation(EN, LB, ACT.Exp, scale=-1.0 / 16), sem("decays"))
                    act.wait_ge(sem("to_end"), 1)
                    st.tell(act.activation(KDF, KDF, ACT.Exp, scale=1.0 / 16), sem("decays"))
                    for j, (o, r) in enumerate(CH):
                        full(act, ("v", j))
                        st.free(copy(V[0:r, j, :], bank(("v", j))[0:r, :]), ("v", j))
                    for f in range(4):
                        full(act, ("r", f))
                        st.free(act.activation(MTE[:, f, :], bank(("r", f))[:, 0:T], ACT.Silu), ("r", f))
                    for f in range(4):
                        full(act, ("u", f))
                        ps = bank(("u", f))
                        st.run(copy(UE[:, f, PBUF:], ps[:, 0:SEQ]))
                        st.run(copy(USC[:, f, :], ps[:, SEQ:T]))
                        st.free(copy(US[:, f, :, PBUF:19], ps[:, SEQ:T].rearrange("p (b t) -> p b t", b=NSEQ)), ("u", f))
                    full(act, ("spT",))
                    for g in range(4):
                        n = NSEQ * PBUF
                        ins = copy(US[:, g, :, 0:PBUF], bank(("spT",))[:, n * g:n * g + n].rearrange("p (b t) -> p b t", b=NSEQ))
                        if g < 3:
                            st.run(ins)
                        else:
                            st.free(ins, ("spT",))
                    full(act, ("puT",))
                    st.free(copy(PUO[0:PBUF, :], bank(("puT",))[0:PBUF, :]), ("puT",))
                    full(act, ("usT",))
                    st.free(copy(spl[0:TS, :], bank(("usT",))[0:TS, :]), ("usT",))
                    for h in range(H):
                        full(act, ("oT", h))
                        ps = bank(("oT", h))[:, 0:T]
                        st.tell(act.activation(SQE[:, h, :], ps, ACT.Square), sem("sq"))
                        st.free(copy(AT[:, h, :], ps), ("oT", h))
                    norm_rows(act, l, 1)
                    for h in range(H):
                        full(act, ("ms", h))
                        if h > 1:
                            act.wait_ge(sem("headnorm"), h - 1)
                        st.free(act.activation(RSE[:, h % 2, :], bank(("ms", h))[:, 0:T], ACT.Sqrt, bias=eps), ("ms", h))
                else:
                    for h in range(H):
                        for j in range(3):
                            full(act, ("vv", h, j))
                            st.free(copy(RV[:, j, :], bank(("vv", h, j))), ("vv", h, j))
                        for f in range(4):
                            full(act, ("gg", h, f))
                            st.free(act.activation(MT[:, 4 * h + f, :], bank(("gg", h, f))[:, 0:T], ACT.Silu), ("gg", h, f))
                        if h == 0:
                            act.wait_ge(sem("odd_in"), 16)
                        full(act, ("kT", h))
                        st.run(copy(KD[:, 0, :], bank(("kT", h))[:, 0:256], scale=kdec[:, 0, h:h + 1]))
                        st.free(copy(KD[:, 1, :], bank(("kT", h))[:, 256:512], scale=kdec[:, 1, h:h + 1]), ("kT", h))
                        full(act, ("kTs", h))
                        st.run(copy(KDS[:, 0, :], bank(("kTs", h))[:, 0:256], scale=kdec_s[:, 0, h:h + 1]))
                        st.free(copy(KDS[:, 1, :], bank(("kTs", h))[:, 0:256], scale=kdec_s[:, 1, h:h + 1]), ("kTs", h))
                        full(act, ("o4", h))
                        st.free(copy(O4, bank(("o4", h))), ("o4", h))
                        for e in range(2):
                            full(act, ("sp", h, e))
                            if h and e == 0:
                                act.wait_ge(sem("sp_out"), 16 * h)
                            st.free(copy(SPo[:, e, :], bank(("sp", h, e))), ("sp", h, e))
                        for f in range(4):
                            full(act, ("roT", h, f))
                            if h and f == 0:
                                act.wait_ge(sem("headmix"), h)
                            ps = bank(("roT", h, f))[:, 0:T]
                            st.tell(act.activation(RSQ[:, f, :], ps, ACT.Square), sem("osq"))
                            st.free(copy(ROT[:, f, :], ps), ("roT", h, f))
                        full(act, ("rms", h))
                        st.free(act.activation(RSQ[:, 0, :], bank(("rms", h))[:, 0:T], ACT.Sqrt, bias=eps), ("rms", h))
                    act.wait_ge(sem("mixed", l), 1)
                    norm_rows(act, l, 1)
                norm_root(l, 1)
                st.phase()

                act.dma_start(WR, A["w_router"][l].rearrange("(p c) n -> p (c n)", c=KC)).then_inc(sem("router_in", l), 16)
                act.dma_start(rbias, A["router_bias"][l:l + 1, :].broadcast_to([P, E])).then_inc(sem("rbias_in", l), 16)
                tokens(act, PIN, (A["p_prompt"][l, 0], A["p_sample"][l].rearrange("b s d -> (b s) d")), sem("p_in", l))
                act.wait_ge(sem("x_mid", l), 3)
                norm_rows(act, l, 2)
                x_half(f"xTb{l}")
                full(act, (f"router{l}",))
                act.wait_ge(sem("scores_cleared", l), 1)
                ps = bank((f"router{l}",))
                st.run(act.activation(SC[:, 0:2, :], ps[:, 0:2 * E].rearrange("p (j e) -> p j e", j=2), ACT.Sigmoid))
                st.free(act.activation(SC[0:TS, 2, :], ps[0:TS, 2 * E:3 * E], ACT.Sigmoid), (f"router{l}",))
                for f in range(2):
                    full(act, (f"sh{l}", f))
                    st.free(act.activation(HSf[:, f, :], bank((f"sh{l}", f))[:, 0:T], ACT.Silu), (f"sh{l}", f))
                full(act, (f"pT{l}",))
                for f in range(2):
                    ins = copy(PT[:, f, 0:SEQ], bank((f"pT{l}",))[:, 256 * f:256 * f + 256])
                    if f:
                        st.free(ins, (f"pT{l}",))
                    else:
                        st.run(ins)
                for n in range(2):
                    for j, (o, r) in enumerate(CH):
                        full(act, (f"shd{l}", j, n))
                        st.free(copy(F[0:r, j, 512 * n:512 * n + 512], bank((f"shd{l}", j, n))[0:r, :]), (f"shd{l}", j, n))
                for n in range(2):
                    for j, (o, r) in enumerate(CH):
                        full(act, (f"pw{l}", j, n))
                        st.free(copy(PP[0:r, j, 512 * n:512 * n + 512], bank((f"pw{l}", j, n))[0:r, :]), (f"pw{l}", j, n))
                base = GRP[(f"moe{l}",)]

                def rows(u, q):
                    return copy(XGT[u][:, 4 * q:4 * q + 4, :], PS[:, q, :].rearrange("p (c t) -> p c t", c=4))

                for q in range(2):
                    act.wait_ge(bank_full[q], base[q] + 1)
                    rows(0, q).then_inc(bank_free[q], 1)

                def two_pairs(it):
                    for u in range(2):
                        pr = 2 * it + u
                        act.wait_ge(bank_full[2], base[2] + pr + 1)
                        act.activation(HS[u], PS[:, 2, 0:DE], ACT.Silu).then_inc(sem("silu", l), 1)
                        for q in range(2):
                            act.wait_ge(bank_full[q], base[q] + pr + 2)
                            rows(1 - u, q).then_inc(bank_free[q], 1)
                        act.wait_ge(bank_full[3], base[3] + pr + 1)
                        copy(HT[u], PS[:, 3, 0:256].rearrange("p (c t) -> p c t", c=2)).then_inc(bank_free[3], 1)
                        act.wait_ge(bank_full[5], base[5] + pr + 1)
                        if not isinstance(it, int):
                            act.wait_ge(sem("scattered", l, u), 16 * it)
                        copy(YS[u][:, 512:1024], PS[:, 5, :]).then_inc(bank_free[5], 1)

                two_pairs(0)
                with act.Fori(1, PAIRS // 2) as it:
                    two_pairs(it)
                act.wait_ge(sem("flag_ready", l), 1)
                go = act.value_load(flagi[0:1, 0:1], min_val=0, max_val=1)
                with act.If(go > 0):
                    with act.Fori(0, 4) as m:
                        with act.Fori(0, PAIRS) as pr:
                            s = m * PAIRS + pr
                            act.wait_ge(sem("ov_rows", l), s + 1)
                            rows(0, 0)
                            rows(0, 1).then_inc(sem("ov_xgt", l), 1)
                            act.wait_ge(sem("ov_gu", l), s + 1)
                            act.activation(HS[0], PS[:, 2, 0:DE], ACT.Silu).then_inc(sem("ov_silu", l), 1)
                            act.wait_ge(sem("ov_hT", l), s + 1)
                            copy(HT[0], PS[:, 3, 0:256].rearrange("p (c t) -> p c t", c=2)).then_inc(sem("ov_hTc", l), 1)
                act.nop()
                st.last = None
                norm_root(l, 2)
                x_half(f"xTc{l}")
                k = 0
                for n in range(2):
                    for j, (o, r) in enumerate(CH):
                        full(act, (f"pg{l}", j, n))
                        if k > 1:
                            act.wait_ge(sem("gated", l), k - 1)
                        st.free(act.activation(SG[k % 2][0:r, :], bank((f"pg{l}", j, n))[0:r, :], ACT.Sigmoid), (f"pg{l}", j, n))
                        k += 1
                st.phase()

        def even_dve(dve, st, TT, TSc, STT):
            dve.wait_ge(sem("even_in"), 16 * 13)
            for f in range(2):
                full(dve, ("gk", f))
                st.free(TSc(LX[:, f, :], bank(("gk", f))[:, 0:T], bgk[:, f:f + 1], None, ALU.add), ("gk", f))
            st.after
            st.tell(STT(LB, LX, -1.0, LX, ALU.mult, ALU.max), sem("gate_logits"))
            st.after
            st.run(TSc(LX, LX, 0.0, None, ALU.min))
            dve.wait_ge(sem("log_term"), 1)
            st.after
            st.run(TT(LX, LX, LB, ALU.subtract))
            for f in range(2):
                st.after
                ins = dve.tensor_tensor_scan(LB[:, f, :], keep, LX[:, f, :], 0.0, ALU.mult, ALU.add)
                if f:
                    st.tell(ins, sem("summed"))
                else:
                    st.run(ins)
            st.after
            for f in range(2):
                for k, (o, n, c) in enumerate(((0, SEQ, CA), (SEQ, TS, DSEQ))):
                    b = LB[:, f, o:o + n].rearrange("p (i c) -> p i c", c=c)
                    ins = TT(KDF[:, f, o:o + n].rearrange("p (i c) -> p i c", c=c),
                             b[:, :, c - 1:c].broadcast_to([P, n // c, c]), b, ALU.subtract)
                    if f and k:
                        st.tell(ins, sem("to_end"))
                    else:
                        st.run(ins)
            dve.wait_ge(sem("decays"), 3)
            for f in range(4):
                full(dve, ("qk", f))
                ps = bank(("qk", f))[:, 0:T]
                if f < 2:
                    st.free(STT(QI[:, f, :], ps, DKA ** -0.5, EB[:, f, :], ALU.mult, ALU.mult), ("qk", f))
                else:
                    st.run(TT(KI[:, f - 2, :], ps, EN[:, f - 2, :], ALU.mult))
                    st.free(TT(KDF[:, f - 2, :], ps, KDF[:, f - 2, :], ALU.mult), ("qk", f))

            def mask_keys(j):
                r = CH[j][1]
                if j:
                    full(dve, ("dS", j - 1, 1, 1))
                full(dve, ("kdT", j))
                m = mch if j < 2 else mch_s
                st.free(TT(KDM[0:r], bank(("kdT", j))[0:r, 0:256].unsqueeze(1).broadcast_to([r, 8, 256]),
                           m[0:r, :].unsqueeze(2).broadcast_to([r, 8, 256]), ALU.mult), ("kdT", j))

            dve.wait_ge(sem("scores_zeroed"), 1)
            for h in range(H):
                full(dve, ("att", h))
                ps = bank(("att", h))
                for o in (0, P):
                    st.run(dve.copy_predicated(AT[:, h, o:o + P], mcau, ps[:, o:o + P]))
                st.free(dve.copy_predicated(AT[0:TS, h, SEQ:T], mcau_s[0:TS, :], ps[0:TS, SEQ:T]), ("att", h))
            mask_keys(0)
            for j in range(2):
                for f in range(2):
                    for i2 in range(2):
                        name = ("dS", j, f, i2)
                        full(dve, name)
                        ps = bank(name)
                        for i in range(4):
                            n = 8 * j + 4 * i2 + i
                            ds_ = ps[:, P * i:P * i + P]
                            st.after
                            if n == 0:
                                st.run(dve.tensor_copy(SS[:, f, 1, :], ds_))
                                continue
                            t = CA * n + CA - 1
                            ins = STT(SS[:, f, n + 1, :], SS[:, f, n, :], EB[:, f, t:t + 1], ds_, ALU.mult, ALU.add)
                            if i == 3:
                                st.free(ins, name)
                            else:
                                st.run(ins)
                mask_keys(j + 1)
            st.after.nop().then_inc(sem("states"), 1)
            for f in range(2):
                for i2 in range(2):
                    full(dve, ("dS", 2, f, i2))
            for f in range(2):
                for i2 in range(2):
                    name = ("dS", 2, f, i2)
                    for i in range(4):
                        b = 4 * i2 + i
                        t = SEQ + DSEQ * b + DSEQ - 1
                        ins = STT(gsn[:, f, b, :], gs0[:, f, b, :], EB[:, f, t:t + 1], bank(name)[:, P * i:P * i + P],
                                  ALU.mult, ALU.add)
                        if i == 3:
                            st.free(ins, name)
                        else:
                            st.run(ins)
            for g in range(4):
                full(dve, ("pool", g))
                st.free(TSc(MTE[:, 4 + g, :], bank(("pool", g))[:, 0:T], bpool[:, g:g + 1], pscale[:, g:g + 1],
                            ALU.add, ALU.mult), ("pool", g))
            for h in range(H):
                emptied(dve, ("ms", h))
                rs = RSE[:, h % 2, :]
                st.run(dve.reciprocal(rs, rs))
                st.after
                st.tell(STT(AT[:, h, :], AT[:, h, :], gnorm, rs, ALU.mult, ALU.mult), sem("headnorm"))
                st.after
                ins = TT(MTE[:, h, :], MTE[:, h, :], AT[:, h, :], ALU.mult)
                if h == H - 1:
                    st.tell(ins, sem("mixed", 0))
                else:
                    st.run(ins)

        def odd_dve(dve, st, TT, TSc, STT):
            gam = [1.0 - 2.0 ** (-5.0 - h) for h in range(H)]
            emptied(dve, ("xTa1", 2, 0))
            st.after
            st.tell(dve.tensor_copy(XS4, XT[:, :, SEQ:T].unsqueeze(2).broadcast_to([P, KC, 4, TS])), sem("xs4"))
            dve.wait_ge(sem("odd_in"), 16)
            for h in range(H):
                for m in range(2):
                    ne, no = ("qkh", h, 2 * m), ("qkh", h, 2 * m + 1)
                    full(dve, ne)
                    full(dve, no)
                    pe_, po = bank(ne)[:, 0:T], bank(no)[:, 0:T]
                    st.after
                    st.run(TT(RT[:, 0, :], pe_, cos, ALU.mult))
                    st.run(TT(RT[:, 1, :], po, sin, ALU.mult))
                    st.after
                    st.run(TT(RQ[:, 2 * m, :], RT[:, 0, :], RT[:, 1, :], ALU.subtract))
                    st.after
                    st.free(TT(RT[:, 0, :], pe_, sin, ALU.mult), ne)
                    st.free(TT(RT[:, 1, :], po, cos, ALU.mult), no)
                    st.after
                    dve.wait_ge(*(bank_free[GRP[ne][0]], GRP[ne][1] + 1))
                    st.tell(TT(RQ[:, 2 * m + 1, :], RT[:, 0, :], RT[:, 1, :], ALU.add), sem("roped"))
                st.after
                for e in range(2):
                    st.run(TT(QM[:, e], RQ[:, e, SEQ:T].unsqueeze(1).broadcast_to([P, NSEQ, TS]), qmask[:, h], ALU.mult))
                for e in range(2):
                    ins = dve.tensor_copy(KS4[:, e], RQ[:, 2 + e, SEQ:T].unsqueeze(1).broadcast_to([P, 4, TS]))
                    if e:
                        st.tell(ins, sem("sample_qk"))
                    else:
                        st.run(ins)
                full(dve, ("ratt", h))
                ps = bank(("ratt", h))
                st.run(TT(RAT[:, 0:SEQ], ps[:, 0:SEQ], dmask[:, h, :], ALU.mult))
                st.run(TT(RAT[:, SEQ:SEQ + P], ps[:, SEQ:SEQ + P], dmask[:, h, 0:P], ALU.mult))
                st.free(TT(RAT[0:TS, SEQ + P:SEQ + P + TS], ps[0:TS, SEQ + P:SEQ + P + TS], dmask_s[0:TS, h, :], ALU.mult),
                        ("ratt", h))
                for b in range(NSEQ):
                    k = NSEQ * h + b
                    for e in range(2):
                        full(dve, ("sn", h, b, e))
                        s = S0[k % NS0][:, e, :]
                        st.free(STT(s, s, gam[h] ** DSEQ, bank(("sn", h, b, e)), ALU.mult, ALU.add), ("sn", h, b, e))
                emptied(dve, ("rms", h))
                st.run(dve.reciprocal(RSQ[:, 0, :], RSQ[:, 0, :]))
                st.after
                for f in range(4):
                    st.run(TT(ROT[:, f, :], ROT[:, f, :], RSQ[:, 0, :], ALU.mult))
                st.after
                for f in range(4):
                    ins = TT(MT[:, 4 * h + f, :], MT[:, 4 * h + f, :], ROT[:, f, :], ALU.mult)
                    if f < 3:
                        st.run(ins)
                    else:
                        st.tell(ins, sem("headmix"))
            st.after.nop().then_inc(sem("mixed", 1), 1)
            st.last = None

        def experts_dve(dve, st, TT, TSc, STT, l, x_half):
            R3 = [P, 3, E]
            x_half(f"xTb{l}")
            st.run(dve.memset(MSK, 0.0))
            st.run(dve.memset(POS, -1.0))
            st.run(dve.memset(TAB, 0.0))
            st.after
            for j in range(3):
                st.run(TSc(TAB[:, j, 0:E, 0], MSK[:, j, :], tokc[:, j:j + 1], None, ALU.add))
            emptied(dve, (f"router{l}",))
            dve.wait_ge(sem("rbias_in", l), 16)
            dve.wait_ge(sem("scores_cleared", l), 1)
            st.run(TT(SEL, SC, rbias.unsqueeze(1).broadcast_to(R3), ALU.add))
            sel8 = SEL.rearrange("p j (g k) -> p (j g) k", g=EG)
            st.after
            for g in range(24):
                st.run(dve.max(G8[:, g, :], sel8[:, g, :]))
            st.after
            st.run(TT(GS, G8[:, :, 0], G8[:, :, 1], ALU.add))
            st.after
            for j in range(3):
                g = GS[:, EG * j:EG * j + EG]
                other = g.unsqueeze(1).broadcast_to([P, EG, EG])
                own = g.unsqueeze(2).broadcast_to([P, EG, EG])
                a = GT8[:, 64 * j:64 * j + 64].rearrange("p (g k) -> p g k", g=EG)
                b = GE8[:, 64 * j:64 * j + 64].rearrange("p (g k) -> p g k", g=EG)
                st.run(TT(a, other, own, ALU.is_gt))
                st.run(TT(b, other, own, ALU.is_equal))
                st.after
                st.run(TT(b, b, tri8.rearrange("p (g k) -> p g k", g=EG), ALU.mult))
                st.after
                st.run(TT(a, a, b, ALU.add))
            st.after
            st.run(dve.tensor_reduce(RK, GT8.rearrange("p (g k) -> p g k", k=EG), AX.X, ALU.add))
            st.after
            st.run(TSc(RK, RK, TOPG - 0.5, None, ALU.is_lt))
            st.after
            mk8 = MK.rearrange("p j (g k) -> p (j g) k", g=EG)
            st.run(TT(mk8, sel8, RK.unsqueeze(2).broadcast_to([P, 24, EG]), ALU.mult))
            st.run(TSc(GS, RK, BIG, -BIG, ALU.mult, ALU.add))
            st.after
            st.run(TT(mk8, mk8, GS.unsqueeze(2).broadcast_to([P, 24, EG]), ALU.add))
            st.after
            for j in range(3):
                st.run(dve.max(T8[:, j, :], MK[:, j, :]))
            st.after
            for j in range(3):
                st.run(dve.match_replace(MR[:, j, :], T8[:, j, :], MK[:, j, :], -2 * BIG))
            st.after
            st.run(TSc(MSK[:, 0:2, :], MR[:, 0:2, :], -1.5 * BIG, None, ALU.is_lt))
            st.run(TSc(MSK[0:TS, 2, :], MR[0:TS, 2, :], -1.5 * BIG, None, ALU.is_lt))
            st.after.nop().then_inc(sem("chosen", l), 1)
            st.run(TT(MR, SC, MSK, ALU.mult))
            st.after
            st.run(dve.tensor_reduce(DEN, MR, AX.X, ALU.add))
            st.after
            st.run(TSc(DEN, DEN, 1e-20, None, ALU.add))
            st.after
            st.run(dve.reciprocal(DEN, DEN))
            st.after
            for j in range(3):
                st.run(TSc(TAB[:, j, 0:E, 2], MR[:, j, :], DEN[:, j:j + 1], ROUTED, ALU.mult, ALU.mult))
            for j in range(3):
                st.run(dve.tensor_tensor_scan(SEL[:, j, :], ones[:, 0:E], MSK[:, j, :], 0.0, ALU.mult, ALU.add))
            st.after
            for j in range(3):
                st.run(TSc(TAB[:, j, 0:E, 1], SEL[:, j, :], float(T), slotc[:, j:j + 1], ALU.mult, ALU.add))
            for f in range(2):
                full(dve, (f"sh{l}", 2 + f))
                emptied(dve, (f"sh{l}", f))
                st.free(TT(HSf[:, f, :], HSf[:, f, :], bank((f"sh{l}", 2 + f))[:, 0:T], ALU.mult), (f"sh{l}", 2 + f))
            full(dve, (f"cum{l}",))
            ps = bank((f"cum{l}",))
            st.run(STT(CUM[:, 0:2, :], ps[:, 0:2 * E].rearrange("p (j e) -> p j e", j=2), 1.0, MSK[:, 0:2, :], ALU.add, ALU.mult))
            st.run(STT(CUM[0:TS, 2, :], ps[0:TS, 2 * E:3 * E], 1.0, MSK[0:TS, 2, :], ALU.add, ALU.mult))
            st.free(dve.tensor_copy(PT[:, :, SEQ:T], ps[:, 256:256 + 2 * TS].rearrange("p (f t) -> p f t", f=2)), (f"cum{l}",))
            st.after
            st.run(TSc(POS[:, 0:2, 0:E], CUM[:, 0:2, :], -1.0, None, ALU.add))
            st.run(TSc(POS[0:TS, 2, 0:E], CUM[0:TS, 2, :], -1.0, None, ALU.add))
            st.after
            st.tell(dve.tensor_reduce(colmax, POS, AX.XY, ALU.max), sem("colmax", l))

            def onehot(u, pr, off):
                pos = POS[:, :, 2 * pr:2 * pr + 2] if isinstance(pr, int) else POS[:, :, bass.ds(2 * pr, 2)]
                it_ = iota[:, 0:BLK] if isinstance(off, int) else iota[:, bass.ds(off, BLK)]
                for j in range(3):
                    last = TT(OH[u][:, j], it_.unsqueeze(1).broadcast_to([P, 2, BLK]),
                              pos[:, j].unsqueeze(2).broadcast_to([P, 2, BLK]), ALU.is_equal)
                return last

            def meta(u, ps):
                return dve.tensor_copy(META[u], ps[:, 0:8])

            def gather_rows(u):
                TSc(GI[u][0:64, :], META[u][0:64, 0:1], FAR, None, ALU.add)
                dve.tensor_copy(GATE[u][0:64, :], META[u][0:64, 2:3])
                dve.tensor_copy(GATE[u][64:128, :], META[u][64:128, 6:7])
                return TSc(GI[u][64:128, :], META[u][64:128, 4:5], FAR, None, ALU.add)

            def slot_rows(u):
                TSc(SI[u][0:64, :], META[u][0:64, 1:2], FAR, None, ALU.add)
                return TSc(SI[u][64:128, :], META[u][64:128, 5:6], FAR, None, ALU.add)

            def hidden(u):
                return STT(HH[u], HS[u], GATE[u], PS[:, 2, DE:2 * DE], ALU.mult, ALU.mult)

            base = GRP[(f"moe{l}",)]
            st.after
            onehot(0, 0, 0).then_inc(sem("onehot", l), 1)
            full(dve, (f"flag{l}",))
            st.free(dve.tensor_reduce(flagf[0:1, :], bank((f"flag{l}",))[0:1, 0:P], AX.X, ALU.max), (f"flag{l}",))
            st.after
            st.tell(TSc(flagi[0:1, :], flagf[0:1, :], BLK - 0.5, None, ALU.is_gt), sem("flag_ready", l))
            dve.wait_ge(bank_full[6], base[6] + 1)
            meta(0, PS[:, 6, :]).then_inc(bank_free[6], 1)
            dve.wait_ge(bank_free[6], base[6] + 1)
            gather_rows(0).then_inc(sem("gather_rows", l), 1)
            onehot(1, 1, 0).then_inc(sem("onehot", l), 1)

            def two_pairs(it):
                for u in range(2):
                    v = 1 - u
                    pr = 2 * it + u
                    dve.wait_ge(bank_full[6], base[6] + pr + 2)
                    dve.wait_ge(bank_free[4], base[4] + pr)
                    meta(v, PS[:, 6, :]).then_inc(bank_free[6], 1)
                    dve.wait_ge(bank_free[6], base[6] + pr + 2)
                    dve.wait_ge(bank_full[1], base[1] + pr)
                    gather_rows(v).then_inc(sem("gather_rows", l), 1)
                    onehot(u, pr + 2, 0).then_inc(sem("onehot", l), 1)
                    dve.wait_ge(bank_full[2], base[2] + pr + 1)
                    dve.wait_ge(sem("silu", l), pr + 1)
                    hidden(u).then_inc(bank_free[2], 1)
                    if not isinstance(it, int):
                        dve.wait_ge(sem("scattered", l, u), 16 * it)
                    slot_rows(u).then_inc(sem("slot_rows", l), 1)
                    dve.wait_ge(bank_full[4], base[4] + pr + 1)
                    dve.tensor_copy(YS[u][:, 0:512], PS[:, 4, :]).then_inc(bank_free[4], 1)

            two_pairs(0)
            with dve.Fori(1, PAIRS // 2) as it:
                two_pairs(it)
            dve.wait_ge(sem("flag_ready", l), 1)
            go = dve.value_load(flagi[0:1, 0:1], min_val=0, max_val=1)
            with dve.If(go > 0):
                dve.wait_ge(sem("scattered", l, 0), 16 * (PAIRS // 2))
                dve.wait_ge(sem("scattered", l, 1), 16 * (PAIRS // 2))
                with dve.Fori(0, 4) as m:
                    with dve.Fori(0, PAIRS) as pr:
                        s = m * PAIRS + pr
                        onehot(0, pr, m * BLK + BLK).then_inc(sem("ov_onehot", l), 1)
                        dve.wait_ge(sem("ov_meta", l), s + 1)
                        meta(0, PS[:, 6, :]).then_inc(sem("ov_metac", l), 1)
                        dve.wait_ge(sem("ov_metac", l), s + 1)
                        dve.wait_ge(sem("ov_rows_left", l), s + 1)
                        slot_rows(0)
                        gather_rows(0).then_inc(sem("ov_lists", l), 1)
                        dve.wait_ge(sem("ov_silu", l), s + 1)
                        hidden(0).then_inc(sem("ov_hidden", l), 1)
                        dve.wait_ge(sem("ov_y", l), s + 2)
                        dve.tensor_copy(YS[0][:, 0:512], PS[:, 4, :])
                        dve.tensor_copy(YS[0][:, 512:1024], PS[:, 5, :]).then_inc(sem("ov_yc", l), 1)
            dve.nop()
            st.last = None
            for j, (o, r) in enumerate(CH):
                for n in range(2):
                    emptied(dve, (f"shd{l}", j, n))
                dve.wait_ge(sem("y_in", l), 16 * (j + 1))
                f = F[0:r, j, :]
                for k in range(TOPK):
                    st.after
                    ins = TT(f, f, YK[0:r, k, :], ALU.add)
                    if k == TOPK - 1:
                        st.tell(ins, sem("y_summed", l))
                    else:
                        st.run(ins)
                st.after
                st.run(STT(X[0:r, j, :], X[0:r, j, :], ALPHA, f, ALU.mult, ALU.add))

        @block.vector
        def _(dve):
            st = Steps(dve, sem("dve_steps"))
            TT, TSc, STT = dve.tensor_tensor, dve.tensor_scalar, dve.scalar_tensor_tensor

            def x_half(tag):
                for j, (o, r) in enumerate(CH):
                    full(dve, (tag, j, 1))
                    st.free(dve.tensor_copy(XT[:, 4:8, o:o + r],
                                            bank((tag, j, 1)).rearrange("p (c t) -> p c t", c=4)[:, :, 0:r]), (tag, j, 1))

            def norm(l, k, done):
                for j, (o, r) in enumerate(CH):
                    for n in range(2):
                        st.after
                        st.run(dve.bn_stats(bnst[0:r, 6 * n:6 * n + 6], X[0:r, j, 512 * n:512 * n + 512]))
                    st.after
                    st.tell(dve.bn_aggr(bnag[0:r, 2 * j:2 * j + 2], bnst[0:r, :]), sem("variance", l, k))
                dve.wait_ge(sem("std", l, k), 1)
                st.run(dve.reciprocal(rstd, rstd))
                dve.wait_ge(sem("ln_in", l, k), 32)
                for j, (o, r) in enumerate(CH):
                    x = X[0:r, j, :]
                    st.after
                    st.run(TSc(x, x, bnag[0:r, 2 * j:2 * j + 1], rstd[0:r, j:j + 1], ALU.subtract, ALU.mult))
                    st.after
                    st.run(TT(x, x, LN[0:r, 0, :], ALU.mult))
                    st.after
                    st.tell(TT(x, x, LN[0:r, 1, :], ALU.add), done)

            dve.wait_ge(sem("ones_set"), 1)
            dve.wait_ge(sem("const_in"), 16)
            for l in range(DEPTH):
                x_half(f"xTa{l}")
                if l % 2 == 0:
                    even_dve(dve, st, TT, TSc, STT)
                else:
                    odd_dve(dve, st, TT, TSc, STT)
                for n in range(2):
                    for j, (o, r) in enumerate(CH):
                        name = (f"out{l}", j, n)
                        full(dve, name)
                        x = X[0:r, j, 512 * n:512 * n + 512]
                        st.free(STT(x, x, ALPHA, bank(name)[0:r, :], ALU.mult, ALU.add), name)
                norm(l, 1, sem("x_mid", l))
                st.phase()
                experts_dve(dve, st, TT, TSc, STT, l, x_half)
                norm(l, 2, sem("x_ln2", l))
                x_half(f"xTc{l}")
                k = 0
                for n in range(2):
                    for j, (o, r) in enumerate(CH):
                        emptied(dve, (f"pg{l}", j, n))
                        st.run(TT(SG[k % 2][0:r, :], SG[k % 2][0:r, :], PP[0:r, j, 512 * n:512 * n + 512], ALU.mult))
                        k += 1
                        x = X[0:r, j, 512 * n:512 * n + 512]
                        if n == 0 and j == 0:
                            full(dve, (f"xTc{l}", 2, 1))
                        st.after
                        st.tell(TT(x, x, SG[(k - 1) % 2][0:r, :], ALU.add), sem("gated", l))
                st.after.nop().then_inc(sem("x_out", l), 1)
                st.last = None
                st.phase()

        def even_pool(pool, st, store):
            s = sem("even_out")
            n_out = 0
            store(O["pool_sample"][0, :, 0:PBUF - DSEQ, :], A["state_pool"][0, :, DSEQ:PBUF, :], s)
            st.run(pool.memset(UE[:, :, 0:PBUF], 0.0))
            for f in range(4):
                emptied(pool, ("u", f))
            emptied(pool, ("spT",))
            st.tell(pool.memset(AT, 0.0), sem("scores_zeroed"))
            for g, w in enumerate(WINDOWS):
                for kind in range(2):
                    if kind == 0:
                        n, new = SEQ, SEQ
                        ext = UE[:, g, :].unsqueeze(1)
                        buf = [b[:, 0:PBUF + SEQ].unsqueeze(1) for b in PWK]
                        dst = DD[:, g, 0:SEQ].unsqueeze(1)
                    else:
                        n, new = 1, DSEQ
                        ext = US[:, g]
                        buf = [b[:, 0:NSEQ * 19].rearrange("p (b t) -> p b t", b=NSEQ) for b in PWK]
                        dst = DD[:, g, SEQ:T].rearrange("p (b t) -> p b t", b=NSEQ)
                    cur, step, k, ln = ext, 1, 0, PBUF + new
                    while step < w:
                        nxt = buf[k % 2]
                        st.after
                        st.run(pool.tensor_tensor(nxt[:, :, 2 * step - 1:ln], cur[:, :, 2 * step - 1:ln],
                                                  cur[:, :, step - 1:ln - step], ALU.add))
                        cur, step, k = nxt, 2 * step, k + 1
                    win = cur[:, :, PBUF:ln]
                    st.after
                    if kind == 0:
                        st.run(pool.tensor_tensor(win[:, :, 0:16], win[:, :, 0:16],
                                                  invc[:, 16 * g:16 * g + 16].unsqueeze(1), ALU.mult))
                        st.run(pool.tensor_scalar(win[:, :, 16:SEQ], win[:, :, 16:SEQ], 1.0 / w, None, ALU.mult))
                    else:
                        st.run(pool.tensor_scalar(win, win, 1.0 / w, None, ALU.mult))
                    st.after
                    ins = pool.tensor_tensor(dst, win, ext[:, :, PBUF:ln], ALU.subtract)
                    if kind:
                        st.tell(ins, sem("pool_d"))
                    else:
                        st.run(ins)
            emptied(pool, ("puT",))
            store(O["pool_prompt"][0, 0], PUO[0:PBUF, :], s)
            emptied(pool, ("usT",))
            for b in range(NSEQ):
                store(O["pool_sample"][0, b, PBUF - DSEQ:PBUF, :], spl[DSEQ * b:DSEQ * b + DSEQ, :], s)
            pool.wait_ge(sem("states"), 1)
            for f in range(2):
                for i2 in range(2):
                    emptied(pool, ("dS", 2, f, i2))
            for h in range(H):
                f, r = h // 2, 64 * (h % 2)
                store(O["gla_prompt"][0, 0, h], SS[r:r + 64, f, 16, :], s)
                store(O["gla_sample"][0, :, h].rearrange("b k v -> k b v"), gsn[r:r + 64, f, :, :], s)
            pool.wait_ge(s, 16 * (1 + 1 + NSEQ + 2 * H))

        def odd_pool(pool, st, store):
            def rows(x):
                return x.rearrange("(p e) v -> p e v", e=2)

            def load(k):
                pool.dma_start(S0[k % NS0], rows(A["state_ret"][0, k % NSEQ, k // NSEQ])).then_inc(sem("s0_in", k % NS0), 16)

            for k in range(NS0):
                load(k)
            for k in range(NSEQ * H):
                h, b = k // NSEQ, k % NSEQ
                for e in range(2):
                    emptied(pool, ("sn", h, b, e))
                store(rows(O["ret_sample"][0, b, h]), S0[k % NS0], sem("s0_out", k % NS0))
                if k + NS0 < NSEQ * H:
                    pool.wait_ge(sem("s0_out", k % NS0), 16 * (k // NS0 + 1))
                    load(k + NS0)
                if b == NSEQ - 1:
                    for e in range(2):
                        emptied(pool, ("sp", h, e))
                    store(rows(O["ret_prompt"][0, 0, h]), SPo, sem("sp_out"))
            pool.wait_ge(sem("sp_out"), 16 * H)
            for i in range(NS0):
                pool.wait_ge(sem("s0_out", i), 16 * ((NSEQ * H - i + NS0 - 1) // NS0))

        def experts_pool(pool, st, store, l):
            st.run(pool.memset(SC[:, 2, :], 0.0))
            for i in range(2):
                st.run(pool.memset(XG[i], 0.0))
            st.after.nop().then_inc(sem("scores_cleared", l), 1)
            st.last = None
            pool.wait_ge(sem("x_mid", l), 3)
            store(xd[0:SEQ, :].rearrange("(j p) n -> p j n", p=P), X[:, 0:2, :], sem("x_rows", l))
            store(xd[SEQ:T, :], X[0:TS, 2, :], sem("x_rows", l))
            pool.wait_ge(sem("x_rows", l), 32)
            base = GRP[(f"moe{l}",)]

            last_token, last_slot = pool.to_reg(T - 1), pool.to_reg(TOPK * T - 1)

            def gather(u, s):
                pool.sem_inc(sem("gathers_begun", l))
                pool.indirect_dma_start(XG[u], None, xd, bass.IndirectOffsetOnAxis(ap=GI[u], axis=0),
                                        bounds_check=last_token, oob_is_err=False).then_inc(s, 16)

            def scatter(u, s):
                pool.sem_inc(sem("scatters_begun", l))
                pool.indirect_dma_start(yd, bass.IndirectOffsetOnAxis(ap=SI[u], axis=0), YS[u], None,
                                        bounds_check=last_slot, oob_is_err=False).then_inc(s, 16)

            pool.wait_ge(sem("gather_rows", l), 1)
            gather(0, sem("gathered", l, 0))
            with pool.Fori(0, PAIRS // 2) as it:
                for u in range(2):
                    pr = 2 * it + u
                    pool.wait_ge(sem("gather_rows", l), pr + 2)
                    pool.wait_ge(bank_full[1], base[1] + pr)
                    gather(1 - u, sem("gathered", l, 1 - u))
                    pool.wait_ge(sem("slot_rows", l), pr + 1)
                    for b in (4, 5):
                        pool.wait_ge(bank_free[b], base[b] + pr + 1)
                    scatter(u, sem("scattered", l, u))
            for u in range(2):
                pool.wait_ge(sem("scattered", l, u), 16 * (PAIRS // 2))
            pool.wait_ge(sem("gathered", l, 0), 16 * (PAIRS // 2 + 1))
            pool.wait_ge(sem("gathered", l, 1), 16 * (PAIRS // 2))
            pool.wait_ge(bank_full[1], base[1] + PAIRS + 1)
            pool.wait_ge(sem("flag_ready", l), 1)
            go = pool.value_load(flagi[0:1, 0:1], min_val=0, max_val=1)
            with pool.If(go > 0):
                pool.sem_inc(sem("ov_rows_left", l), 1)
                with pool.Fori(0, 4) as m:
                    with pool.Fori(0, PAIRS) as pr:
                        s = m * PAIRS + pr
                        pool.wait_ge(sem("ov_lists", l), s + 1)
                        gather(0, sem("ov_gathered", l))
                        pool.wait_ge(sem("ov_yc", l), s + 1)
                        scatter(0, sem("ov_scattered", l))
                        pool.wait_ge(sem("ov_scattered", l), 16 * s + 16)
                        pool.sem_inc(sem("ov_rows_left", l), 1)
            pool.nop().then_inc(sem("all_scattered", l), 1)


        @block.gpsimd
        def _(pool):
            st = Steps(pool, sem("pool_steps"))
            st.run(pool.memset(ones, 1.0))
            st.run(pool.memset(onesA, 1.0 / DVA))
            st.run(pool.memset(onesC, 1.0 / DVC))
            st.run(pool.memset(eps, EPS))
            st.run(pool.memset(bnag, 1.0))
            st.after.nop().then_inc(sem("ones_set"), 1)
            st.last = None

            def store(dst, src, s):
                pool.dma_start(dst, src).then_inc(s, 16)

            for l in range(DEPTH):
                if l % 2 == 0:
                    even_pool(pool, st, store)
                else:
                    odd_pool(pool, st, store)
                st.phase()
                experts_pool(pool, st, store, l)
                if l == DEPTH - 1:
                    n = 0
                    pool.wait_ge(sem("x_out", l), 1)
                    store(O["y_prompt"][0].rearrange("(j p) n -> p j n", p=P), X[:, 0:2, :], sem("stored"))
                    store(O["y_sample"].rearrange("b s d -> (b s) d"), X[0:TS, 2, :], sem("stored"))
                    pool.wait_ge(sem("stored"), 32)
                st.phase()

_INS = ['x_prompt', 'x_sample', 'state_gla', 'state_pool', 'state_ret', 'p_prompt', 'p_sample',
        'w_in_a', 'w_gk2', 'b_gk', 'g_norm_a', 'w_pool', 'b_pool', 'pool_scale', 'w_out_a',
        'w_in_c', 'w_out_c', 'ln1_g', 'ln1_b', 'ln2_g', 'ln2_b',
        'w_router', 'router_bias', 'w_exp_gate', 'w_exp_up', 'w_exp_down',
        'w_sh_gate', 'w_sh_up', 'w_sh_down', 'w_ple_gate', 'w_ple_proj']
_OUTS = [("y_prompt", (1, SEQ, D)), ("y_sample", (NSEQ, DSEQ, D)), ("gla_prompt", (1, 1, H, DKA, DVA)),
         ("pool_prompt", (1, 1, PBUF, 512)), ("ret_prompt", (1, 1, H, DKC, DVC)),
         ("gla_sample", (1, NSEQ, H, DKA, DVA)), ("pool_sample", (1, NSEQ, PBUF, 512)),
         ("ret_sample", (1, NSEQ, H, DKC, DVC))]


def kernel(**inputs):
    import numpy as _np
    import concourse.bacc as _bacc
    from concourse import mybir as _mybir
    from concourse.bass_utils import run_bass_kernel_spmd as _run

    nc = _bacc.Bacc("TRN2", target_bir_lowering=False, num_devices=1)
    arrays, args = {}, {}
    for name in _INS:
        a = _np.ascontiguousarray(inputs[name])
        arrays[f"in_{name}"] = a
        args[name] = nc.dram_tensor(f"in_{name}", a.shape, _mybir.dt.from_np(a.dtype), kind="ExternalInput").ap()
    tables = []
    for i, a in enumerate(constants()):
        arrays[f"table_{i}"] = a
        tables.append(nc.dram_tensor(f"table_{i}", a.shape, F32, kind="ExternalInput").ap())
    outs = {n: nc.dram_tensor(f"out_{n}", s, F32, kind="ExternalOutput").ap() for n, s in _OUTS}
    trunk(nc, args, outs, tables)
    r = _run(nc, [arrays], core_ids=[0])
    return tuple(r.results[0][f"out_{n}"] for n, _ in _OUTS)
```

```python
from contextlib import ExitStack

import numpy as np

import concourse.bass as bass
from concourse import mybir

F32 = mybir.dt.float32
U32 = mybir.dt.uint32
I32 = mybir.dt.int32
ALU = mybir.AluOpType
ACT = mybir.ActivationFunctionType
AX = mybir.AxisListType

P = 128
D = 1024
SEQ = 256
NSEQ = 8
DSEQ = 4
PAST = 2048
TS = NSEQ * DSEQ
T = SEQ + TS
CH = [(0, 128), (128, 128), (256, TS)]
ORD = (2, 0, 1)
KC = D // P
DEPTH = 2
H = 4
DKA = 64
DVA = 128
RANK = 16
CA = 16
NCA = SEQ // CA
WINDOWS = (2, 4, 8, 16)
PBUF = 15
DKC = 256
DVC = 512
E = 64
EG = 8
TOPG = 4
TOPK = 8
DE = 256
ROUTED = 2.5
PD = 256
ALPHA = (2.0 * DEPTH) ** 0.25
EPS = 1e-5
BLK = 64
PAIRS = E // 2
SLOTS = 6
PW = 4096
FAR = 4096.0
BIG = 1e30
EP = E + 4
QCOL, KCOL, VCOL, RCOL, GCOL, UCOL = 0, 256, 512, 1024, 1536, 1552


class Cut:

    def __init__(self, ap, size):
        self.ap, self.size, self.at = ap, size, 0

    def take(self, n):
        a = self.ap[:, self.at:self.at + n]
        self.at += n
        assert self.at <= self.size, (self.at, self.size)
        return a


def constants():
    p = np.arange(P)
    common = [np.eye(P), (p[:, None] < p[None, :]) * 1.0,
              np.tile(np.arange(BLK * 5), (P, 1)),
              np.stack([p + o - FAR - T for o, _ in CH], 1),
              np.tile((np.arange(8)[None, :] < np.arange(8)[:, None]).reshape(-1), (P, 1)),
              np.tile(np.eye(TS), (4, 1))]
    t = np.arange(T)
    first = np.where(t < SEQ, t % CA == 0, t % DSEQ == 0)
    causal = (p[:, None] // CA == p[None, :] // CA) & (p[:, None] <= p[None, :])
    s = np.arange(TS)
    causal_s = np.zeros((P, TS), bool)
    causal_s[:TS] = (s[:, None] // DSEQ == s[None, :] // DSEQ) & (s[:, None] <= s[None, :])
    inv = np.stack([1.0 / np.minimum(np.arange(16) + 1, w) for w in WINDOWS])
    even = [np.tile(1.0 - first, (P, 1)), causal * 1.0, causal_s * 1.0,
            (p[:, None] // CA == np.arange(8)[None, :]) * 1.0,
            ((p[:, None] // DSEQ) == np.arange(8)[None, :]) * 1.0,
            np.tile(inv.reshape(-1), (P, 1))]
    f = np.float32
    freq = (f(1.0) / np.power(f(10000.0), np.linspace(0.0, 1.0, DKC // 2, dtype=f), dtype=f)).astype(f)
    pos = np.concatenate([np.arange(SEQ), np.tile(PAST + np.arange(DSEQ), NSEQ)]).astype(f)
    ang = (freq[:, None] * pos[None, :]).astype(f).astype(np.float64)
    gam = 1.0 - 2.0 ** (-5.0 - np.arange(H))
    kscale = DKC ** -0.5
    dm = np.zeros((P, H, SEQ))
    tt = np.arange(SEQ)[None, :] - p[:, None]
    for h in range(H):
        dm[:, h] = np.where(tt >= 0, gam[h] ** np.maximum(tt, 0), 0) * kscale
    ds = np.zeros((P, H, TS))
    for h in range(H):
        ds[:TS, h] = causal_s[:TS] * gam[h] ** np.maximum(s[None, :] - s[:, None], 0) * kscale
    qm = np.zeros((P, H, NSEQ, TS))
    for h in range(H):
        for b in range(NSEQ):
            qm[:, h, b] = (s // DSEQ == b) * gam[h] ** (s % DSEQ + 1)
    kd = np.zeros((P, 2, H))
    for j in range(2):
        kd[:, j] = gam[None, :] ** (SEQ - 1 - 128 * j - p)[:, None] * kscale
    kds = np.zeros((P, 2, H))
    for a in range(2):
        kds[:, a] = (((p % TS) // DSEQ == p // TS + 4 * a)[:, None]
                     * gam[None, :] ** (DSEQ - 1 - p % DSEQ)[:, None] * kscale)
    odd = [np.cos(ang), np.sin(ang), dm.reshape(P, -1), ds.reshape(P, -1), qm.reshape(P, -1),
           kd.reshape(P, -1), kds.reshape(P, -1)]
    return [np.ascontiguousarray(np.concatenate([np.asarray(a, f) for a in x], 1), dtype=f)
            for x in (common, even, odd)]


def group_order():
    g = []

    def xt(tag, chunks):
        g.extend((tag, j, q) for j in chunks for q in range(2))

    def out(tag, chunks=range(3)):
        g.extend((tag, j, n) for j in chunks for n in range(2))

    for l in range(DEPTH):
        xt(f"xTa{l}", ORD)
        if l % 2 == 0:
            g.append(("glr",))
            g.extend(("gk", f) for f in range(2))
            g.extend(("qk", f) for f in range(4))
            g.extend(("v", j) for j in range(3))
            g.append(("spT",))
            g.extend(("u", f) for f in range(4))
            g.extend((("kdT", 0), ("puT",), ("usT",)))
            for j in range(2):
                g.extend(("r", 2 * j + f) for f in range(2))
                g.extend(("dS", j, f, i) for f in range(2) for i in range(2))
                g.append(("kdT", j + 1))
            g.extend(("att", h) for h in range(H))
            g.extend(("dS", 2, f, i) for f in range(2) for i in range(2))
            g.extend((("oT", 0), ("oT", 1), ("oTs",)))
            g.extend(("pool", f) for f in range(4))
            g.extend(("ms", h) for h in range(H))
        else:
            for h in range(H):
                g.extend(("qkh", h, f) for f in range(4))
                g.extend(("vv", h, j) for j in range(3))
                g.extend(("gg", h, f) for f in range(4))
                g.append(("ratt", h))
                g.append(("kT", h))
                g.append(("kTs", h))
                g.append(("o4", h))
                g.extend(("sn", h, b, e) for b in range(NSEQ) for e in range(2))
                g.extend(("sp", h, e) for e in range(2))
                g.extend(("roT", h, f) for f in range(4))
                g.append(("rms", h))
        out(f"out{l}")
        xt(f"xTb{l}", range(3))
        g.append((f"router{l}",))
        g.extend((f"sh{l}", f) for f in range(4))
        g.append((f"pT{l}",))
        g.append((f"cum{l}",))
        g.append((f"flag{l}",))
        g.append((f"lists{l}",))
        out(f"shd{l}")
        g.extend((f"rows{l}", q) for q in range(2))
        g.append((f"moe{l}",))
        out(f"pw{l}", ORD)
        for j in ORD:
            xt(f"xTc{l}", (j,))
            out(f"pg{l}", (j,))
    return g


ODD_GROUPS = ("qkh", "vv", "gg", "ratt", "kT", "kTs", "roT", "sn", "sp", "rms")


def plan_groups():
    at, used, nxt, banks = {}, [0] * 8, 0, 8
    for name in group_order():
        if name[0].startswith("moe"):
            at[name] = list(used)
            for b in range(7):
                used[b] += PAIRS
            continue
        if name[0] == "o4":
            b = 7
        else:
            banks = 7 if name[0] in ODD_GROUPS else 8
            b = nxt % banks
            nxt += 1
        at[name] = (b, used[b])
        used[b] += 1
    return at


def plan_panels():
    p = []
    for l in range(DEPTH):
        if l % 2 == 0:
            p += [(("qk",), ("qk", 3)), (("v",), ("v", 2)), (("u",), ("u", 3)), (("r",), ("r", 3))]
            p += [((f"out{l}", n), (f"out{l}", 2, 1)) for n in range(2)]
        else:
            for h in range(H):
                p += [(("qk", h), ("qkh", h, 3)), (("v", h), ("vv", h, 2)), (("g", h), ("gg", h, 3))]
            p += [((f"out{l}", n, k), (f"out{l}", 2, 1)) for n in range(2) for k in range(2)]
        p += [((f"shgu{l}",), (f"sh{l}", 3)), ((f"shd{l}",), (f"shd{l}", 2, 1))]
        p += [((f"moe{l}",), None)]
        p += [((f"pw{l}",), (f"pw{l}", ORD[-1], 1))]
        p += [((f"pg{l}", n), (f"pg{l}", ORD[-1], 1)) for n in range(2)]
    return p


def trunk(nc, A, O, C):
    GRP = plan_groups()
    PANELS = plan_panels()
    NUM, n = {}, 0
    for name, _ in PANELS:
        NUM[name] = n
        n += 3 * PAIRS if name[0].startswith("moe") else 1
    LAST = {}
    for name, g in PANELS:
        if name[0].startswith("moe"):
            l = int(name[0][3:])
            for k in range(3 * PAIRS):
                LAST[NUM[name] + k] = (f"moe{l}", k // 3, 5 if k % 3 == 2 else 2)
        else:
            LAST[NUM[name]] = g

    with ExitStack() as ctx:
        def sb(name, cols, dt=F32):
            return ctx.enter_context(nc.sbuf_tensor(name, [P, cols], dt))

        names = {}

        def sem(*name):
            key = "_".join(map(str, name))
            if key not in names:
                names[key] = ctx.enter_context(nc.semaphore(key))
            return names[key]

        W = sb("weights", SLOTS * PW)
        Xb = sb("x_tok", 3 * D)
        XTb = sb("x_feat", KC * T)
        LNb = sb("ln_rows", 2 * D)
        CC = sb("const", C[0].shape[1])
        SIDE = sb("side", 2048)
        SMb = sb("small", 600)
        ASZ = 17600
        AR = sb("arena", ASZ)
        PS = ctx.enter_context(nc.psum_tensor("ps", [P, 8, 512], F32))
        yd = nc.dram_tensor("y_slots", (TOPK * T, D), F32, kind="Internal").ap()

        X = Xb[:, :].rearrange("p (j n) -> p j n", j=3)
        XT = XTb[:, :].rearrange("p (c t) -> p c t", c=KC)
        LN = LNb[:, :].rearrange("p (k n) -> p k n", k=2)
        cc = Cut(CC[:, :], C[0].shape[1])
        ident, tri = cc.take(P), cc.take(P)
        iota = cc.take(BLK * 5)
        slotc = cc.take(3)
        tri8 = cc.take(64)
        fold4 = cc.take(TS)

        sm = Cut(SMb[:, :], 600)
        ones = sm.take(P)
        onesA = sm.take(P)
        onesC = sm.take(P)
        eps, zero1 = sm.take(1), sm.take(1)
        rbias = sm.take(E)
        bnst = sm.take(12)
        bnag = sm.take(6)
        rstd = sm.take(3)
        colmax, flagf = sm.take(1), sm.take(1)
        flagi = sm.take(1).bitcast(I32)

        a = Cut(AR[:, :], ASZ)
        MTE = a.take(8 * T).rearrange("p (f t) -> p f t", f=8)
        CE = a.take(C[1].shape[1])
        ce = Cut(CE, C[1].shape[1])
        keep, mcau, mcau_s = ce.take(T), ce.take(P).bitcast(U32), ce.take(TS).bitcast(U32)
        mch, mch_s = ce.take(8), ce.take(8)
        invc = ce.take(64)
        wglr = a.take(8 * RANK).rearrange("p (c n) -> p c n", c=8)
        wgk2 = a.take(256)
        bgk, gnorm, bpool, pscale = a.take(2), a.take(1), a.take(4), a.take(4)
        wpool = a.take(512)
        glrT = a.take(T)
        LXB = a.take(4 * T)
        LX, LB = (LXB[:, 2 * T * i:2 * T * i + 2 * T].rearrange("p (f t) -> p f t", f=2) for i in range(2))
        KDF, KI, EB = (a.take(2 * T).rearrange("p (f t) -> p f t", f=2) for _ in range(3))
        QI = a.take(4 * T).rearrange("p (f k t) -> p f k t", f=2, k=2)
        EN = LX
        DD = LXB.rearrange("p (g t) -> p g t", g=4)
        V = a.take(3 * 512).rearrange("p (j n) -> p j n", j=3)
        UE = a.take(4 * (PBUF + SEQ)).rearrange("p (g t) -> p g t", g=4)
        US = a.take(4 * NSEQ * 19).rearrange("p (g b t) -> p g b t", g=4, b=NSEQ)
        PWK = [a.take(272) for _ in range(2)]
        USC = a.take(4 * TS).rearrange("p (g t) -> p g t", g=4)
        PUO = a.take(512)
        spl = a.take(512)
        SS = a.take(2 * 17 * 128).rearrange("p (f i v) -> p f i v", f=2, i=17)
        gs0 = LNb[:, :].rearrange("p (f b v) -> p f b v", f=2, b=8)
        KDM = SIDE[:, :].rearrange("p (i n) -> p i n", i=8)
        gsn = SIDE[:, :].rearrange("p (f b v) -> p f b v", f=2, b=8)
        SQE = XTb[:, 0:4 * T].rearrange("p (h t) -> p h t", h=4)
        AT = XTb[:, 4 * T:8 * T].rearrange("p (h t) -> p h t", h=4)
        RSE = KDF
        a = Cut(AR[:, :], ASZ)
        MT = a.take(16 * T).rearrange("p (f t) -> p f t", f=16)
        CO = a.take(C[2].shape[1])
        co = Cut(CO, C[2].shape[1])
        cos, sin = co.take(T), co.take(T)
        dmask = co.take(4 * SEQ).rearrange("p (h t) -> p h t", h=4)
        dmask_s = co.take(4 * TS).rearrange("p (h t) -> p h t", h=4)
        qmask = co.take(4 * NSEQ * TS).rearrange("p (h b t) -> p h b t", h=4, b=NSEQ)
        kdec = co.take(8).rearrange("p (j h) -> p j h", j=2)
        kdec_s = co.take(8).rearrange("p (a h) -> p a h", a=2)
        RQ = a.take(4 * T).rearrange("p (f t) -> p f t", f=4)
        RT = a.take(2 * T).rearrange("p (f t) -> p f t", f=2)
        RV = a.take(3 * 512).rearrange("p (j n) -> p j n", j=3)
        KD = a.take(2 * 256).rearrange("p (j n) -> p j n", j=2)
        KDS = a.take(2 * 256).rearrange("p (a n) -> p a n", a=2)
        O4 = a.take(512)
        RSQ = a.take(4 * T).rearrange("p (f t) -> p f t", f=4)
        SPo = a.take(1024).rearrange("p (e n) -> p e n", e=2)
        NS0 = 3
        S0 = [a.take(1024).rearrange("p (e n) -> p e n", e=2) for _ in range(NS0)]
        XS4 = SIDE[:, 0:1024].rearrange("p (c a t) -> p c a t", c=8, a=4)
        QM = SIDE[:, 1024:1536].rearrange("p (e b t) -> p e b t", e=2, b=8)
        KS4 = SIDE[:, 1536:1792].rearrange("p (e a t) -> p e a t", e=2, a=4)
        ROT = LNb[:, 0:4 * T].rearrange("p (f t) -> p f t", f=4)
        RAT = LNb[:, 4 * T:4 * T + 384 + TS]
        a = Cut(AR[:, :], ASZ)
        F, PP = (a.take(3 * D).rearrange("p (j n) -> p j n", j=3) for _ in range(2))
        YR = a.take(512)
        PT = a.take(2 * T).rearrange("p (f t) -> p f t", f=2)
        mark = a.at
        SC, SEL, MK, MR, MSK, CUM = (a.take(3 * E).rearrange("p (j e) -> p j e", j=3) for _ in range(6))
        G8 = a.take(24 * 8).rearrange("p (g k) -> p g k", g=24)
        GS, RK = a.take(24), a.take(24)
        GT8, GE8 = (a.take(192) for _ in range(2))
        T8 = a.take(24).rearrange("p (j k) -> p j k", j=3)
        DEN = a.take(3)
        POS = a.take(3 * EP).rearrange("p (j e) -> p j e", j=3)
        TAB = a.take(3 * EP * 2).rearrange("p (j e k) -> p j e k", j=3, e=EP)
        OH = [a.take(3 * P).rearrange("p (j a k) -> p j a k", j=3, a=2) for _ in range(2)]
        META = [a.take(4) for _ in range(2)]
        GATE = [a.take(1) for _ in range(2)]
        SI = [a.take(1).bitcast(U32) for _ in range(2)]
        HSf = a.take(2 * T).rearrange("p (f t) -> p f t", f=2)
        PIN = a.take(3 * PD).rearrange("p (j n) -> p j n", j=3)
        WR = a.take(KC * E)
        HS = [a.take(DE) for _ in range(2)]
        HH = [a.take(DE) for _ in range(2)]
        HT = [a.take(2 * P).rearrange("p (c t) -> p c t", c=2) for _ in range(2)]
        YS = [SIDE[:, D * i:D * i + D] for i in range(2)]
        XGT = [XTb[:, D * i:D * i + D].rearrange("p (c t) -> p c t", c=KC) for i in range(2)]
        a = Cut(AR[:, mark:], ASZ - mark)
        YK = [a.take(TOPK * 512).rearrange("p (k n) -> p k n", k=TOPK) for _ in range(2)]
        SG = [a.take(512) for _ in range(2)]

        def wp(num):
            s = num % SLOTS
            return W[:, s * PW:(s + 1) * PW]

        bank_full = [sem("bank_full", b) for b in range(8)]
        bank_free = [sem("bank_emptied", b) for b in range(8)]
        slot_full = [sem("panel_landed", s) for s in range(SLOTS)]
        phase_end = sem("phase_end")

        def bank(name):
            return PS[:, GRP[name][0], :]

        def full(eng, name):
            b, u = GRP[name]
            eng.wait_ge(bank_full[b], u + 1)

        def emptied(eng, name):
            b, u = GRP[name]
            eng.wait_ge(bank_free[b], u + 1)

        def landed(eng, name):
            n = NUM[name]
            eng.wait_ge(slot_full[n % SLOTS], 32 * (n // SLOTS + 1))

        class Steps:

            def __init__(self, eng, s):
                self.eng, self.sem, self.n, self.last, self.counts, self.phases = eng, s, 0, None, {}, 0

            @property
            def after(self):
                if self.last is not None:
                    self.eng.wait_ge(*self.last)
                return self.eng

            def run(self, ins):
                ins.then_inc(self.sem, 1)
                self.n += 1
                self.last = (self.sem, self.n)

            def free(self, ins, name):
                b, u = GRP[name]
                ins.then_inc(bank_free[b], 1)
                self.last = (bank_free[b], u + 1)

            def tell(self, ins, s):
                k = self.counts.get(id(s), 0) + 1
                self.counts[id(s)] = k
                ins.then_inc(s, 1)
                self.last = (s, k)

            def phase(self):
                self.phases += 1
                self.after.nop().then_inc(phase_end, 1)
                self.eng.wait_ge(phase_end, 4 * self.phases)
                self.last = None

        block = ctx.enter_context(nc.Block())

        def tokens(eng, dst, src, s):
            pr, sa = src
            eng.dma_start(dst[:, 0:2, :], pr.rearrange("(j p) n -> p j n", p=P)).then_inc(s, 16)
            eng.dma_start(dst[0:TS, 2, :], sa).then_inc(s, 16)

        def norm_rows(eng, l, k):
            for i, nm in enumerate((f"ln{k}_g", f"ln{k}_b")):
                eng.dma_start(LN[:, i, :], A[nm][l:l + 1, :].broadcast_to([P, D])).then_inc(sem("ln_in", l, k), 16)

        @block.sync
        def _(sp):
            def wait_slot(num):
                if num >= SLOTS:
                    g = LAST[num - SLOTS]
                    if g[0].startswith("moe"):
                        sp.wait_ge(bank_full[g[2]], GRP[(g[0],)][g[2]] + g[1] + 1)
                    else:
                        full(sp, g)

            def panel(name, parts):
                num = NUM[name]
                wait_slot(num)
                for dst, src in parts(wp(num)):
                    sp.dma_start(dst, src).then_inc(slot_full[num % SLOTS], 16)

            def split_cols(w, lo):
                s = w.rearrange("(p c) n -> p c n", c=KC)
                return lambda dst: [
                    (dst.rearrange("p (c n) -> p c n", c=KC)[:, 4 * k:4 * k + 4, :],
                     s[:, 4 * k:4 * k + 4, lo:lo + 512]) for k in range(2)]

            def out_rows(w, k0, lo):
                s = w.rearrange("(t p) n -> p t n", p=P)
                return lambda dst: [
                    (dst.rearrange("p (t n) -> p t n", t=8)[:, 4 * k:4 * k + 4, :],
                     s[:, k0 + 4 * k:k0 + 4 * k + 4, lo:lo + 512]) for k in range(2)]

            def two(a0, a1, how):
                return lambda dst: [(how(dst[:, 0:2048]), a0), (how(dst[:, 2048:4096]), a1)]

            def flat(x):
                return x

            sp.dma_start(CC[:, :], C[0]).then_inc(sem("const_in"), 16)
            tokens(sp, X, (A["x_prompt"][0], A["x_sample"].rearrange("b s d -> (b s) d")), sem("x_in"))

            for l in range(DEPTH):
                if l % 2 == 0:
                    wi = A["w_in_a"][0]
                    s = sem("even_in")
                    sp.dma_start(wglr, wi.rearrange("(p c) n -> p c n", c=KC)[:, :, GCOL:GCOL + RANK]).then_inc(s, 16)
                    sp.dma_start(wgk2[0:RANK, :], A["w_gk2"][0]).then_inc(s, 16)
                    sp.dma_start(bgk, A["b_gk"][0].rearrange("(f p) -> p f", p=P), allow_slow_non_contiguous=True).then_inc(s, 16)
                    sp.dma_start(CE, C[1]).then_inc(s, 16)
                    sp.dma_start(gnorm, A["g_norm_a"][0].rearrange("(p o) -> p o", o=1), allow_slow_non_contiguous=True).then_inc(s, 16)
                    sp.dma_start(bpool, A["b_pool"][0].rearrange("g p -> p g"), allow_slow_non_contiguous=True).then_inc(s, 16)
                    sp.dma_start(pscale, A["pool_scale"][0].rearrange("(g p) -> p g", p=P), allow_slow_non_contiguous=True).then_inc(s, 16)
                    sp.dma_start(wpool.rearrange("p (g n) -> p g n", g=4), A["w_pool"][0].rearrange("g c d -> c g d")).then_inc(s, 16)
                    sp.dma_start(spl[0:NSEQ * PBUF, :], A["state_pool"][0].rearrange("b t c -> (b t) c")).then_inc(s, 16)
                    for f in range(2):
                        for r in range(2):
                            sp.dma_start(gs0[64 * r:64 * r + 64, f, :, :],
                                         A["state_gla"][0][:, 2 * f + r].rearrange("b k v -> k b v")).then_inc(s, 16)
                    panel(("qk",), split_cols(wi, 0))
                    panel(("v",), split_cols(wi, VCOL))
                    panel(("u",), split_cols(wi, UCOL))
                    panel(("r",), split_cols(wi, RCOL))
                    for n in range(2):
                        panel((f"out{l}", n), out_rows(A["w_out_a"][0], 0, 512 * n))
                else:
                    wi = A["w_in_c"][0].rearrange("(p c) n -> p c n", c=KC)
                    for h in range(H):
                        panel(("qk", h), two(wi[:, :, 256 * h:256 * h + 256], wi[:, :, 1024 + 256 * h:1280 + 256 * h],
                                             lambda x: x.rearrange("p (c n) -> p c n", c=KC)))
                        panel(("v", h), split_cols(A["w_in_c"][0], 2048 + 512 * h))
                        panel(("g", h), split_cols(A["w_in_c"][0], 4096 + 512 * h))
                    for n in range(2):
                        for k in range(2):
                            panel((f"out{l}", n, k), out_rows(A["w_out_c"][0], 8 * k, 512 * n))
                rp = lambda w: w.rearrange("(p c) n -> p (c n)", c=KC)
                panel((f"shgu{l}",), two(rp(A["w_sh_gate"][l]), rp(A["w_sh_up"][l]), flat))
                by_rows = lambda w: lambda dst: [
                    (dst[:, 0:2048].rearrange("p (f n) -> p f n", f=2)[:, k:k + 1, :],
                     w.rearrange("(f p) n -> p f n", p=P)[:, k:k + 1, :]) for k in range(2)]
                panel((f"shd{l}",), by_rows(A["w_sh_down"][l]))
                n0 = NUM[(f"moe{l}",)]
                base = GRP[(f"moe{l}",)]

                def expert_panel(num, e0, k):
                    s, dst = num % SLOTS, wp(num)
                    if k < 2:
                        halves = [(A["w_exp_gate"], e0 + k), (A["w_exp_up"], e0 + k)]
                    else:
                        halves = [(A["w_exp_down"], e0), (A["w_exp_down"], e0 + 1)]
                    for q, (w, e) in enumerate(halves):
                        if isinstance(e, int):
                            src = w[l, e:e + 1]
                        else:
                            src = w[l, bass.ds(e, 1)]
                        c = KC if k < 2 else 2
                        sp.dma_start(dst[:, 2048 * q:2048 * q + 2048],
                                     src.rearrange("o (p c) n -> (o p) (c n)", c=c)).then_inc(slot_full[s], 16)

                for pr in range(2):
                    for k in range(3):
                        wait_slot(n0 + 3 * pr + k)
                        expert_panel(n0 + 3 * pr + k, 2 * pr, k)
                with sp.Fori(1, PAIRS // 2) as it:
                    for u in range(2):
                        for k in range(3):
                            b = 5 if k == 2 else 2
                            sp.wait_ge(bank_full[b], base[b] + u - 1 + 2 * it)
                            expert_panel(n0 + 3 * u + k, 4 * it + 2 * u, k)
                for b in (2, 5):
                    sp.wait_ge(bank_full[b], base[b] + PAIRS)
                sp.wait_ge(sem("flag_ready", l), 1)
                go = sp.value_load(flagi[0:1, 0:1], min_val=0, max_val=1)
                with sp.If(go > 0):
                    sp.sem_inc(sem("ov_y", l), 1)
                    with sp.Fori(0, 4) as m:
                        with sp.Fori(0, PAIRS) as pr:
                            sp.wait_ge(sem("ov_y", l), m * PAIRS + pr + 1)
                            for k in range(3):
                                dst = W[:, k * PW:(k + 1) * PW]
                                for q in range(2):
                                    w = (A["w_exp_gate"], A["w_exp_up"])[q] if k < 2 else A["w_exp_down"]
                                    e = 2 * pr + (k if k < 2 else q)
                                    sp.dma_start(dst[:, 2048 * q:2048 * q + 2048],
                                                 w[l, bass.ds(e, 1)].rearrange("o (p c) n -> (o p) (c n)", c=KC if k < 2 else 2)
                                                 ).then_inc(sem("ov_w", l), 16)
                    sp.wait_ge(sem("ov_y", l), 4 * PAIRS + 1)
                sp.nop()
                panel((f"pw{l}",), by_rows(A["w_ple_proj"][l]))
                for n in range(2):
                    panel((f"pg{l}", n), split_cols(A["w_ple_gate"][l], 512 * n))
                sp.wait_ge(sem("all_scattered", l), 1)
                ys = yd.rearrange("(k t) n -> t k n", k=TOPK)
                for i in range(6):
                    o, r = CH[ORD[i // 2]]
                    if i > 1:
                        sp.wait_ge(sem("y_summed", l), i - 1)
                    sp.dma_start(YK[i % 2][0:r, :, :], ys[o:o + r, :, 512 * (i % 2):512 * (i % 2) + 512]
                                 ).then_inc(sem("y_in", l, i % 2), 16)

        def even_pe(pe, st, begin, end, feat, tok):
            pe.wait_ge(sem("even_in"), 16 * 13)
            ps = begin(("glr",))
            for c in range(KC):
                last = pe.matmul(ps[0:RANK, 0:T], wglr[:, c, :], XT[:, c, :], start=(c == 0), stop=(c == KC - 1))
            end(last, ("glr",))
            emptied(pe, ("glr",))
            for f in range(2):
                ps = begin(("gk", f))
                end(pe.matmul(ps[:, 0:T], wgk2[0:RANK, P * f:P * f + P], glrT[0:RANK, :], start=True, stop=True), ("gk", f))
            landed(pe, ("qk",))
            w = wp(NUM[("qk",)]).rearrange("p (c n) -> p c n", c=KC)
            for f in range(4):
                feat(("qk", f), lambda c: w[:, c, P * f:P * f + P])
            landed(pe, ("v",))
            w1 = wp(NUM[("v",)]).rearrange("p (c n) -> p c n", c=KC)
            for j, (o, r) in enumerate(CH):
                tok(("v", j), lambda c: XT[:, c, o:o + r], lambda c: w1[:, c, :], r, KC)
            nb = NSEQ * PBUF
            ps = begin(("spT",))
            for g in range(4):
                last = pe.transpose(ps[:, nb * g:nb * g + nb], spl[0:nb, P * g:P * g + P], ident[0:nb, 0:nb])
            end(last, ("spT",))

            def turn_keys(j):
                o, r = CH[j]
                ps = begin(("kdT", j))
                for f in range(2):
                    last = pe.transpose(ps[0:r, P * f:P * f + P], KDF[:, f, o:o + r], ident)
                end(last, ("kdT", j))

            def state_parts(j):
                r = CH[j][1]
                emptied(pe, ("kdT", j))
                emptied(pe, ("v", j))
                for f in range(2):
                    for i2 in range(2):
                        ps = begin(("dS", j, f, i2))
                        for i in range(4):
                            for k in range(2):
                                h = 2 * f + k
                                last = pe.matmul(ps[64 * k:64 * k + 64, P * i:P * i + P],
                                                 KDM[0:r, 4 * i2 + i, 64 * h:64 * h + 64],
                                                 V[0:r, j, P * h:P * h + P], start=True, stop=True)
                        end(last, ("dS", j, f, i2))

            landed(pe, ("u",))
            w2 = wp(NUM[("u",)]).rearrange("p (c n) -> p c n", c=KC)
            for f in range(4):
                feat(("u", f), lambda c: w2[:, c, P * f:P * f + P])
            for f in (2, 3):
                emptied(pe, ("qk", f))
            turn_keys(0)
            for f in range(4):
                emptied(pe, ("u", f))
            for nm, n in (("puT", PBUF), ("usT", TS)):
                ps = begin((nm,))
                for g in range(4):
                    src = UE[:, g, SEQ:SEQ + PBUF] if nm == "puT" else USC[:, g, :]
                    last = pe.transpose(ps[0:n, P * g:P * g + P], src, ident)
                end(last, (nm,))
            landed(pe, ("r",))
            w3 = wp(NUM[("r",)]).rearrange("p (c n) -> p c n", c=KC)
            for j in range(2):
                for f in range(2 * j, 2 * j + 2):
                    feat(("r", f), lambda c: w3[:, c, P * f:P * f + P])
                state_parts(j)
                turn_keys(j + 1)
            for f in range(4):
                emptied(pe, ("qk", f))
            for h in range(H):
                ps = begin(("att", h))
                for j, (o, r) in enumerate(CH):
                    last = pe.matmul(ps[0:r, o:o + r], KI[:, h // 2, o:o + r], QI[:, h // 2, h % 2, o:o + r],
                                     start=True, stop=True)
                end(last, ("att", h))
            state_parts(2)
            pe.wait_ge(sem("states"), 1)
            outs = []
            for f in range(2):
                out2 = begin(("oT", f)).rearrange("p (k t) -> p k t", k=2)
                outs.append(out2)
                for i in range(1, NCA):
                    pe.matmul(out2[:, :, CA * i:CA * i + CA], SS[:, f, i, :], QI[:, f, :, CA * i:CA * i + CA],
                              start=(i == 1), stop=False, skip_group_check=True)
            out4 = begin(("oTs",))[:, 0:H * TS].rearrange("p (h t) -> p h t", h=H)
            for f in range(2):
                for i in range(NSEQ):
                    c = DSEQ * i
                    pe.matmul(out4[:, 2 * f:2 * f + 2, c:c + DSEQ], gs0[:, f, i, :], QI[:, f, :, SEQ + c:SEQ + c + DSEQ],
                              start=(f == 0 and i == 0), stop=False, skip_group_check=True)
            for g in range(4):
                pe.wait_ge(sem("pool_d"), g + 1)
                ps = begin(("pool", g))
                end(pe.matmul(ps[:, 0:T], wpool[:, P * g:P * g + P], DD[:, g, :], start=True, stop=True), ("pool", g))
            for h in range(H):
                emptied(pe, ("att", h))
            for f in range(2):
                for k in range(2):
                    h = 2 * f + k
                    for j in range(2):
                        last = pe.matmul(outs[f][:, k, P * j:P * j + P], V[:, j, P * h:P * h + P],
                                         AT[:, h, P * j:P * j + P], start=False, stop=(k == 1 and j == 1),
                                         skip_group_check=True)
                end(last, ("oT", f))
            for h in range(H):
                last = pe.matmul(out4[:, h, :], V[0:TS, 2, P * h:P * h + P], AT[0:TS, h, SEQ:T],
                                 start=False, stop=(h == H - 1), skip_group_check=True)
            end(last, ("oTs",))
            pe.wait_ge(sem("sq"), 3)
            for h in range(H):
                ps = begin(("ms", h))
                end(pe.matmul(ps[:, 0:T], onesA, SQE[:, h, :], start=True, stop=True), ("ms", h))

        def odd_pe(pe, st, begin, end, feat, tok):
            pe.wait_ge(sem("xs4"), 1)
            for h in range(H):
                landed(pe, ("qk", h))
                w = wp(NUM[("qk", h)]).rearrange("p (m c n e) -> p m c n e", m=2, c=KC, e=2)
                for f in range(4):
                    feat(("qkh", h, f), lambda c: w[:, f // 2, c, :, f % 2])
                landed(pe, ("v", h))
                w1 = wp(NUM[("v", h)]).rearrange("p (c n) -> p c n", c=KC)
                for j, (o, r) in enumerate(CH):
                    if j < 2:
                        tok(("vv", h, j), lambda c: XT[:, c, o:o + r], lambda c: w1[:, c, :], r, KC)
                    else:
                        tok(("vv", h, j), lambda c: XS4[:, c].rearrange("p a t -> p (a t)"), lambda c: w1[:, c, :], P, KC)
                landed(pe, ("g", h))
                w2 = wp(NUM[("g", h)]).rearrange("p (c n) -> p c n", c=KC)
                for f in range(4):
                    feat(("gg", h, f), lambda c: w2[:, c, P * f:P * f + P])
                pe.wait_ge(sem("roped"), 2 * h + 2)
                pe.wait_ge(sem("odd_in"), 16)
                ps = begin(("ratt", h))
                for (s0, t0, n, r, c0) in ((0, 0, SEQ, P, 0), (P, P, P, P, SEQ), (SEQ, SEQ, TS, TS, SEQ + P)):
                    for e in range(2):
                        last = pe.matmul(ps[0:r, c0:c0 + n], RQ[:, 2 + e, s0:s0 + r], RQ[:, e, t0:t0 + n],
                                         start=(e == 0), stop=(e == 1))
                end(last, ("ratt", h))
                ps = begin(("kT", h))
                for j in range(2):
                    for e in range(2):
                        last = pe.transpose(ps[:, 256 * j + P * e:256 * j + P * e + P], RQ[:, 2 + e, P * j:P * j + P], ident)
                end(last, ("kT", h))
                pe.wait_ge(sem("sample_qk"), h + 1)
                ps = begin(("kTs", h))
                for e in range(2):
                    last = pe.transpose(ps[:, P * e:P * e + P], KS4[:, e].rearrange("p a t -> p (a t)"), ident)
                end(last, ("kTs", h))
                pso = begin(("o4", h))
                emptied(pe, ("kTs", h))
                emptied(pe, ("vv", h, 2))
                for b in range(NSEQ):
                    k = NSEQ * h + b
                    q = 32 * (b % 4)
                    pe.wait_ge(sem("s0_in", k % NS0), 16 * (k // NS0 + 1))
                    for e in range(2):
                        last = pe.matmul(pso[q:q + 32, :], QM[:, e, b, :], S0[k % NS0][:, e, :],
                                         start=(b < 4 and e == 0), stop=(b >= 4 and e == 1), skip_group_check=True)
                    if b == NSEQ - 1:
                        end(last, ("o4", h))
                    for e in range(2):
                        ps = begin(("sn", h, b, e))
                        end(pe.matmul(ps, KDS[q:q + 32, b // 4, P * e:P * e + P], RV[q:q + 32, 2, :],
                                      start=True, stop=True), ("sn", h, b, e))
                emptied(pe, ("kT", h))
                for e in range(2):
                    ps = begin(("sp", h, e))
                    for j in range(2):
                        emptied(pe, ("vv", h, j))
                        last = pe.matmul(ps, KD[:, j, P * e:P * e + P], RV[:, j, :], start=(j == 0), stop=(j == 1))
                    end(last, ("sp", h, e))
                emptied(pe, ("ratt", h))
                emptied(pe, ("o4", h))
                for f in range(4):
                    ps = begin(("roT", h, f))
                    vf = slice(P * f, P * f + P)
                    pe.matmul(ps[:, 0:SEQ], RV[:, 0, vf], RAT[:, 0:SEQ], start=True, stop=False, skip_group_check=True)
                    pe.matmul(ps[:, P:SEQ], RV[:, 1, vf], RAT[:, SEQ:SEQ + P], start=False, stop=False, skip_group_check=True)
                    pe.matmul(ps[:, SEQ:T], RV[0:TS, 2, vf], RAT[0:TS, SEQ + P:SEQ + P + TS], start=False, stop=False,
                              skip_group_check=True)
                    end(pe.matmul(ps[:, SEQ:T], O4[:, vf], fold4, start=False, stop=True, skip_group_check=True),
                        ("roT", h, f))
                pe.wait_ge(sem("osq"), 4 * h + 4)
                ps = begin(("rms", h))
                for f in range(4):
                    last = pe.matmul(ps[:, 0:T], onesC, RSQ[:, f, :], start=(f == 0), stop=(f == 3))
                end(last, ("rms", h))

        @block.tensor
        def _(pe):
            st = Steps(pe, sem("pe_steps"))
            order = iter(group_order())

            def begin(name):
                assert next(order) == name, name
                b, u = GRP[name]
                if u:
                    pe.wait_ge(bank_free[b], u)
                return PS[:, b, :]

            def end(ins, name):
                b, u = GRP[name]
                ins.then_inc(bank_full[b], 1)
                st.last = (bank_full[b], u + 1)

            def transpose_x(tag, j, ready=None):
                if ready:
                    pe.wait_ge(*ready)
                r = CH[j][1]
                xc = X[0:r, j, :].rearrange("p (m c) -> p c m", c=KC)
                for q in range(2):
                    ps = begin((tag, j, q))
                    for c in range(4):
                        last = pe.transpose(ps[:, c * P:c * P + r], xc[:, 4 * q + c, :], ident[0:r, 0:r])
                    end(last, (tag, j, q))

            def have_xt(tag, chunks=range(3)):
                for j in chunks:
                    for q in range(2):
                        emptied(pe, (tag, j, q))

            def feat(name, lhs, n=KC):
                ps = begin(name)
                for c in range(n):
                    last = pe.matmul(ps[:, 0:T], lhs(c), XT[:, c, :], start=(c == 0), stop=(c == n - 1))
                end(last, name)

            def tok(name, lhs, rhs, r, n, w=512):
                ps = begin(name)
                for c in range(n):
                    last = pe.matmul(ps[0:r, 0:w], lhs(c), rhs(c), start=(c == 0), stop=(c == n - 1))
                end(last, name)

            pe.wait_ge(sem("const_in"), 16)
            pe.wait_ge(sem("x_in"), 32)
            pe.wait_ge(sem("ones_set"), 1)
            for l in range(DEPTH):
                for i, j in enumerate(ORD):
                    transpose_x(f"xTa{l}", j, (sem("x_out", l - 1), i + 1) if l else None)
                have_xt(f"xTa{l}")
                if l % 2 == 0:
                    even_pe(pe, st, begin, end, feat, tok)
                else:
                    odd_pe(pe, st, begin, end, feat, tok)
                nk = 8 if l % 2 == 0 else 16
                pe.wait_ge(sem("mixed", l), 1)
                MX = MTE if l % 2 == 0 else MT
                for j, (o, r) in enumerate(CH):
                    for n in range(2):
                        name = (f"out{l}", j, n)
                        if l % 2 == 0:
                            landed(pe, (f"out{l}", n))
                            w = [wp(NUM[(f"out{l}", n)]).rearrange("p (t n) -> p t n", t=8)]
                        else:
                            landed(pe, (f"out{l}", n, 0))
                            landed(pe, (f"out{l}", n, 1))
                            w = [wp(NUM[(f"out{l}", n, k)]).rearrange("p (t n) -> p t n", t=8) for k in range(2)]
                        tok(name, lambda c: MX[:, c, o:o + r], lambda c: w[c // 8][:, c % 8, :], r, nk)
                st.phase()

                for j in range(3):
                    transpose_x(f"xTb{l}", j, (sem("x_mid", l), j + 1))
                have_xt(f"xTb{l}")
                pe.wait_ge(sem("router_in", l), 16)
                ps = begin((f"router{l}",))
                wr = WR.rearrange("p (c n) -> p c n", c=KC)
                for j, (o, r) in enumerate(CH):
                    for c in range(KC):
                        last = pe.matmul(ps[0:r, E * j:E * j + E], XT[:, c, o:o + r], wr[:, c, :],
                                         start=(c == 0), stop=(c == KC - 1))
                end(last, (f"router{l}",))
                landed(pe, (f"shgu{l}",))
                sg = wp(NUM[(f"shgu{l}",)]).rearrange("p (m c n) -> p m c n", m=2, c=KC)
                for f in range(4):
                    feat((f"sh{l}", f), lambda c: sg[:, f // 2, c, P * (f % 2):P * (f % 2) + P])
                pe.wait_ge(sem("p_in", l), 32)
                ps = begin((f"pT{l}",))
                for f in range(2):
                    for j in range(2):
                        last = pe.transpose(ps[:, P * (2 * f + j):P * (2 * f + j) + P], PIN[:, j, P * f:P * f + P], ident)
                end(last, (f"pT{l}",))
                pe.wait_ge(sem("chosen", l), 1)
                ps = begin((f"cum{l}",))
                for j, (o, r) in enumerate(CH):
                    for jj in range(j):
                        pe.matmul(ps[0:r, E * j:E * j + E], ones[:, 0:r], MSK[:, jj, :], start=(jj == 0), stop=False)
                    last = pe.matmul(ps[0:r, E * j:E * j + E], tri[0:r, 0:r], MSK[0:r, j, :], start=(j == 0), stop=True)
                for f in range(2):
                    last = pe.transpose(ps[:, 256 + TS * f:256 + TS * f + TS], PIN[0:TS, 2, P * f:P * f + P], ident[0:TS, 0:TS])
                end(last, (f"cum{l}",))
                pe.wait_ge(sem("colmax", l), 1)
                ps = begin((f"flag{l}",))
                end(pe.transpose(ps[0:1, 0:P], colmax, ident), (f"flag{l}",))
                base = GRP[(f"moe{l}",)]
                n0 = NUM[(f"moe{l}",)]

                def meta(u, pr, ps):
                    for j, (o, r) in enumerate(CH):
                        tb = TAB[0:r, j].rearrange("p e k -> p (e k)")
                        rhs = tb[:, 4 * pr:4 * pr + 4] if isinstance(pr, int) else tb[:, bass.ds(4 * pr, 4)]
                        last = pe.matmul(ps[:, 0:4], OH[u][0:r, j].rearrange("p a k -> p (a k)"), rhs,
                                         start=(j == 0), stop=(j == 2))
                    return last

                def rows(u, q, ps):
                    for c in range(4):
                        for j, (o, r) in enumerate(CH):
                            xc = X[0:r, j, :].rearrange("p (m c) -> p c m", c=KC)
                            last = pe.matmul(ps[:, c * P:c * P + P], xc[:, 4 * q + c, :],
                                             OH[u][0:r, j].rearrange("p a k -> p (a k)"), start=(j == 0), stop=(j == 2))
                    return last

                def gate_up(u, w, ps):
                    for c in range(KC):
                        for s in range(2):
                            rhs = w[s].rearrange("p (m c n) -> p m c n", m=2, c=KC)[:, :, c, :]
                            last = pe.matmul(ps[64 * s:64 * s + 64, :], XGT[u][:, c, 64 * s:64 * s + 64], rhs,
                                             start=(c == 0), stop=(c == KC - 1))
                    return last

                def turn_hidden(u, ps):
                    hc = HH[u].rearrange("p (m c) -> p c m", c=2)
                    for c in range(2):
                        last = pe.transpose(ps[:, c * P:c * P + P], hc[:, c, :], ident)
                    return last

                def down(u, n, w, ps):
                    wd = w.rearrange("p (s c n) -> p s c n", s=2, c=2)
                    for c in range(2):
                        for s in range(2):
                            last = pe.matmul(ps[64 * s:64 * s + 64, :], HT[u][:, c, 64 * s:64 * s + 64],
                                             wd[:, s, c, 512 * n:512 * n + 512], start=(c == 0), stop=(c == 1))
                    return last

                pe.wait_ge(sem("onehot", l), 1)
                end(meta(0, 0, begin((f"lists{l}",))), (f"lists{l}",))
                landed(pe, (f"shd{l}",))
                wd = wp(NUM[(f"shd{l}",)])[:, 0:2048].rearrange("p (f n) -> p f n", f=2)
                for f in range(2):
                    emptied(pe, (f"sh{l}", 2 + f))
                for j, (o, r) in enumerate(CH):
                    for n in range(2):
                        tok((f"shd{l}", j, n), lambda c: HSf[:, c, o:o + r], lambda c: wd[:, c, 512 * n:512 * n + 512], r, 2)
                for q in range(2):
                    end(rows(0, q, begin((f"rows{l}", q))), (f"rows{l}", q))
                assert next(order) == (f"moe{l}",)
                for q in range(2):
                    emptied(pe, (f"rows{l}", q))
                for b in range(7):
                    pe.wait_ge(bank_free[b], base[b])
                with pe.Fori(0, PAIRS // 2) as it:
                    for u in range(2):
                        v = 1 - u
                        pr = 2 * it + u
                        pe.wait_ge(sem("onehot", l), pr + 2)
                        pe.wait_ge(bank_free[6], base[6] + pr)
                        meta(v, pr + 1, PS[:, 6, :]).then_inc(bank_full[6], 1)
                        for q in range(2):
                            pe.wait_ge(bank_free[q], base[q] + pr)
                        for k in range(2):
                            n = n0 + 3 * u + k
                            pe.wait_ge(slot_full[n % SLOTS], 32 * (n // SLOTS + 1) + 32 * it)
                        pe.wait_ge(bank_free[2], base[2] + pr)
                        gate_up(u, [wp(n0 + 3 * u), wp(n0 + 3 * u + 1)], PS[:, 2, :]).then_inc(bank_full[2], 1)
                        for q in range(2):
                            rows(v, q, PS[:, q, :]).then_inc(bank_full[q], 1)
                        pe.wait_ge(bank_free[2], base[2] + pr + 1)
                        pe.wait_ge(bank_free[3], base[3] + pr)
                        turn_hidden(u, PS[:, 3, :]).then_inc(bank_full[3], 1)
                        pe.wait_ge(bank_free[3], base[3] + pr + 1)
                        n = n0 + 3 * u + 2
                        pe.wait_ge(slot_full[n % SLOTS], 32 * (n // SLOTS + 1) + 32 * it)
                        for h in range(2):
                            pe.wait_ge(bank_free[4 + h], base[4 + h] + pr)
                            down(u, h, wp(n0 + 3 * u + 2), PS[:, 4 + h, :]).then_inc(bank_full[4 + h], 1)
                pe.wait_ge(sem("flag_ready", l), 1)
                go = pe.value_load(flagi[0:1, 0:1], min_val=0, max_val=1)
                with pe.If(go > 0):
                    for b in range(7):
                        pe.wait_ge(bank_free[b], base[b] + PAIRS)
                    with pe.Fori(0, 4) as m:
                        with pe.Fori(0, PAIRS) as pr:
                            s = m * PAIRS + pr
                            pe.wait_ge(sem("ov_onehot", l), s + 1)
                            meta(0, pr, PS[:, 6, :]).then_inc(sem("ov_meta", l), 1)
                            rows(0, 0, PS[:, 0, :])
                            rows(0, 1, PS[:, 1, :]).then_inc(sem("ov_rows", l), 1)
                            pe.wait_ge(sem("ov_xgt", l), s + 1)
                            pe.wait_ge(sem("ov_w", l), 96 * s + 96)
                            gate_up(0, [W[:, k * PW:(k + 1) * PW] for k in range(2)], PS[:, 2, :]).then_inc(sem("ov_gu", l), 1)
                            pe.wait_ge(sem("ov_hidden", l), s + 1)
                            turn_hidden(0, PS[:, 3, :]).then_inc(sem("ov_hT", l), 1)
                            pe.wait_ge(sem("ov_hTc", l), s + 1)
                            down(0, 0, W[:, 2 * PW:3 * PW], PS[:, 4, :])
                            down(0, 1, W[:, 2 * PW:3 * PW], PS[:, 5, :]).then_inc(sem("ov_y", l), 1)
                pe.nop()
                st.last = None

                emptied(pe, (f"pT{l}",))
                emptied(pe, (f"cum{l}",))
                landed(pe, (f"pw{l}",))
                wpw = wp(NUM[(f"pw{l}",)])[:, 0:2048].rearrange("p (f n) -> p f n", f=2)
                for j in ORD:
                    o, r = CH[j]
                    for n in range(2):
                        tok((f"pw{l}", j, n), lambda c: PT[:, c, o:o + r], lambda c: wpw[:, c, 512 * n:512 * n + 512], r, 2)
                for i, j in enumerate(ORD):
                    o, r = CH[j]
                    transpose_x(f"xTc{l}", j, (sem("x_ln2", l), i + 1))
                    have_xt(f"xTc{l}", (j,))
                    for n in range(2):
                        landed(pe, (f"pg{l}", n))
                        w = wp(NUM[(f"pg{l}", n)]).rearrange("p (c n) -> p c n", c=KC)
                        tok((f"pg{l}", j, n), lambda c: XT[:, c, o:o + r], lambda c: w[:, c, :], r, KC)
                st.phase()

        @block.scalar
        def _(act):
            st = Steps(act, sem("act_steps"))

            def copy(dst, src, **k):
                return act.activation(dst, src, ACT.Copy, **k)

            def x_half(tag, chunks):
                for j in chunks:
                    o, r = CH[j]
                    full(act, (tag, j, 0))
                    st.free(copy(XT[:, 0:4, o:o + r],
                                 bank((tag, j, 0)).rearrange("p (c t) -> p c t", c=4)[:, :, 0:r]), (tag, j, 0))

            def norm_root(l, k, i, j):
                act.wait_ge(sem("variance", l, k), i + 1)
                st.tell(act.activation(rstd[:, j:j + 1], bnag[:, 2 * j + 1:2 * j + 2], ACT.Sqrt, bias=eps), sem("std", l, k))

            act.wait_ge(sem("ones_set"), 1)
            for l in range(DEPTH):
                if l % 2:
                    act.dma_start(CO, C[2]).then_inc(sem("odd_in"), 16)
                x_half(f"xTa{l}", ORD)
                if l % 2 == 0:
                    full(act, ("glr",))
                    st.free(copy(glrT[0:RANK, :], bank(("glr",))[0:RANK, 0:T]), ("glr",))
                    act.wait_ge(sem("gate_logits"), 1)
                    st.run(act.activation(LB, LB, ACT.Exp, scale=-1.0))
                    st.tell(st.after.activation(LB, LB, ACT.Ln, bias=ones[:, 0:1]), sem("log_term"))
                    act.wait_ge(sem("summed"), 1)
                    st.tell(act.activation(EB, LB, ACT.Exp, scale=1.0 / 16), sem("decays"))
                    st.tell(act.activation(EN, LB, ACT.Exp, scale=-1.0 / 16), sem("decays"))
                    act.wait_ge(sem("to_end"), 1)
                    st.tell(act.activation(KDF, KDF, ACT.Exp, scale=1.0 / 16), sem("decays"))
                    for j, (o, r) in enumerate(CH):
                        full(act, ("v", j))
                        st.free(copy(V[0:r, j, :], bank(("v", j))[0:r, :]), ("v", j))
                    full(act, ("spT",))
                    for g in range(4):
                        n = NSEQ * PBUF
                        ins = copy(US[:, g, :, 0:PBUF], bank(("spT",))[:, n * g:n * g + n].rearrange("p (b t) -> p b t", b=NSEQ))
                        if g < 3:
                            st.run(ins)
                        else:
                            st.free(ins, ("spT",))
                    for f in range(4):
                        full(act, ("u", f))
                        ps = bank(("u", f))
                        st.run(copy(UE[:, f, PBUF:], ps[:, 0:SEQ]))
                        st.run(copy(USC[:, f, :], ps[:, SEQ:T]))
                        st.free(copy(US[:, f, :, PBUF:19], ps[:, SEQ:T].rearrange("p (b t) -> p b t", b=NSEQ)), ("u", f))
                    full(act, ("puT",))
                    st.free(copy(PUO[0:PBUF, :], bank(("puT",))[0:PBUF, :]), ("puT",))
                    full(act, ("usT",))
                    st.free(copy(spl[0:TS, :], bank(("usT",))[0:TS, :]), ("usT",))
                    for f in range(4):
                        full(act, ("r", f))
                        st.free(act.activation(MTE[:, f, :], bank(("r", f))[:, 0:T], ACT.Silu), ("r", f))
                    for name, hs, ts in ((("oT", 0), slice(0, 2), slice(0, SEQ)), (("oT", 1), slice(2, 4), slice(0, SEQ)),
                                         (("oTs",), slice(0, 4), slice(SEQ, T))):
                        full(act, name)
                        n = (hs.stop - hs.start) * (ts.stop - ts.start)
                        ps = bank(name)[:, 0:n].rearrange("p (h t) -> p h t", h=hs.stop - hs.start)
                        st.tell(act.activation(SQE[:, hs, ts], ps, ACT.Square), sem("sq"))
                        st.free(copy(AT[:, hs, ts], ps), name)
                    for f in range(2):
                        for i2 in range(2):
                            emptied(act, ("dS", 2, f, i2))
                    norm_rows(act, l, 1)
                    for h in range(H):
                        full(act, ("ms", h))
                        if h > 1:
                            act.wait_ge(sem("headnorm"), h - 1)
                        st.free(act.activation(RSE[:, h % 2, :], bank(("ms", h))[:, 0:T], ACT.Sqrt, bias=eps), ("ms", h))
                else:
                    for h in range(H):
                        for j in range(3):
                            full(act, ("vv", h, j))
                            st.free(copy(RV[:, j, :], bank(("vv", h, j))), ("vv", h, j))
                        for f in range(4):
                            full(act, ("gg", h, f))
                            st.free(act.activation(MT[:, 4 * h + f, :], bank(("gg", h, f))[:, 0:T], ACT.Silu), ("gg", h, f))
                        if h == 0:
                            act.wait_ge(sem("odd_in"), 16)
                        full(act, ("kT", h))
                        st.run(copy(KD[:, 0, :], bank(("kT", h))[:, 0:256], scale=kdec[:, 0, h:h + 1]))
                        st.free(copy(KD[:, 1, :], bank(("kT", h))[:, 256:512], scale=kdec[:, 1, h:h + 1]), ("kT", h))
                        full(act, ("kTs", h))
                        st.run(copy(KDS[:, 0, :], bank(("kTs", h))[:, 0:256], scale=kdec_s[:, 0, h:h + 1]))
                        st.free(copy(KDS[:, 1, :], bank(("kTs", h))[:, 0:256], scale=kdec_s[:, 1, h:h + 1]), ("kTs", h))
                        full(act, ("o4", h))
                        st.free(copy(O4, bank(("o4", h))), ("o4", h))
                        for e in range(2):
                            full(act, ("sp", h, e))
                            if h and e == 0:
                                act.wait_ge(sem("sp_out"), 16 * h)
                            st.free(copy(SPo[:, e, :], bank(("sp", h, e))), ("sp", h, e))
                        for f in range(4):
                            full(act, ("roT", h, f))
                            if h and f == 0:
                                act.wait_ge(sem("headmix"), h)
                            ps = bank(("roT", h, f))[:, 0:T]
                            st.tell(act.activation(RSQ[:, f, :], ps, ACT.Square), sem("osq"))
                            st.free(copy(ROT[:, f, :], ps), ("roT", h, f))
                        full(act, ("rms", h))
                        st.free(act.activation(RSQ[:, 0, :], bank(("rms", h))[:, 0:T], ACT.Sqrt, bias=eps), ("rms", h))
                    act.wait_ge(sem("mixed", l), 1)
                    norm_rows(act, l, 1)
                for j in range(3):
                    norm_root(l, 1, j, j)
                st.phase()

                act.dma_start(WR, A["w_router"][l].rearrange("(p c) n -> p (c n)", c=KC)).then_inc(sem("router_in", l), 16)
                act.dma_start(rbias, A["router_bias"][l:l + 1, :].broadcast_to([P, E])).then_inc(sem("rbias_in", l), 16)
                tokens(act, PIN, (A["p_prompt"][l, 0], A["p_sample"][l].rearrange("b s d -> (b s) d")), sem("p_in", l))
                act.wait_ge(sem("x_mid", l), 3)
                norm_rows(act, l, 2)
                x_half(f"xTb{l}", range(3))
                full(act, (f"router{l}",))
                act.wait_ge(sem("scores_cleared", l), 1)
                ps = bank((f"router{l}",))
                st.run(act.activation(SC[:, 0:2, :], ps[:, 0:2 * E].rearrange("p (j e) -> p j e", j=2), ACT.Sigmoid))
                st.free(act.activation(SC[0:TS, 2, :], ps[0:TS, 2 * E:3 * E], ACT.Sigmoid), (f"router{l}",))
                for f in range(2):
                    full(act, (f"sh{l}", f))
                    st.free(act.activation(HSf[:, f, :], bank((f"sh{l}", f))[:, 0:T], ACT.Silu), (f"sh{l}", f))
                full(act, (f"pT{l}",))
                for f in range(2):
                    ins = copy(PT[:, f, 0:SEQ], bank((f"pT{l}",))[:, 256 * f:256 * f + 256])
                    if f:
                        st.free(ins, (f"pT{l}",))
                    else:
                        st.run(ins)
                base = GRP[(f"moe{l}",)]

                def rows(u, q, ps):
                    return copy(XGT[u][:, 4 * q:4 * q + 4, :], ps.rearrange("p (c t) -> p c t", c=4))

                for q in range(2):
                    full(act, (f"rows{l}", q))
                    st.free(rows(0, q, bank((f"rows{l}", q))), (f"rows{l}", q))

                def two_pairs(it):
                    for u in range(2):
                        pr = 2 * it + u
                        act.wait_ge(bank_full[2], base[2] + pr + 1)
                        act.activation(HS[u], PS[:, 2, 0:DE], ACT.Silu).then_inc(sem("silu", l), 1)
                        for q in range(2):
                            act.wait_ge(bank_full[q], base[q] + pr + 1)
                            rows(1 - u, q, PS[:, q, :]).then_inc(bank_free[q], 1)
                        act.wait_ge(bank_full[3], base[3] + pr + 1)
                        copy(HT[u], PS[:, 3, 0:256].rearrange("p (c t) -> p c t", c=2)).then_inc(bank_free[3], 1)
                        act.wait_ge(bank_full[5], base[5] + pr + 1)
                        if not isinstance(it, int):
                            act.wait_ge(sem("scattered", l, u), 16 * it)
                        copy(YS[u][:, 512:1024], PS[:, 5, :]).then_inc(bank_free[5], 1)

                two_pairs(0)
                with act.Fori(1, PAIRS // 2) as it:
                    two_pairs(it)
                act.wait_ge(sem("flag_ready", l), 1)
                go = act.value_load(flagi[0:1, 0:1], min_val=0, max_val=1)
                with act.If(go > 0):
                    with act.Fori(0, 4) as m:
                        with act.Fori(0, PAIRS) as pr:
                            s = m * PAIRS + pr
                            act.wait_ge(sem("ov_rows", l), s + 1)
                            rows(0, 0, PS[:, 0, :])
                            rows(0, 1, PS[:, 1, :]).then_inc(sem("ov_xgt", l), 1)
                            act.wait_ge(sem("ov_gu", l), s + 1)
                            act.activation(HS[0], PS[:, 2, 0:DE], ACT.Silu).then_inc(sem("ov_silu", l), 1)
                            act.wait_ge(sem("ov_hT", l), s + 1)
                            copy(HT[0], PS[:, 3, 0:256].rearrange("p (c t) -> p c t", c=2)).then_inc(sem("ov_hTc", l), 1)
                act.nop()
                st.last = None
                for j in ORD:
                    o, r = CH[j]
                    for n in range(2):
                        full(act, (f"pw{l}", j, n))
                        st.free(copy(PP[0:r, j, 512 * n:512 * n + 512], bank((f"pw{l}", j, n))[0:r, :]), (f"pw{l}", j, n))

                def turned(i):
                    norm_root(l, 2, i, ORD[i])
                    x_half(f"xTc{l}", (ORD[i],))

                def gate(i):
                    j = ORD[i]
                    r = CH[j][1]
                    for n in range(2):
                        full(act, (f"pg{l}", j, n))
                        if i:
                            act.wait_ge(sem("gated", l), 2 * i + n - 1)
                        st.free(act.activation(SG[n][0:r, :], bank((f"pg{l}", j, n))[0:r, :], ACT.Sigmoid), (f"pg{l}", j, n))

                turned(0)
                turned(1)
                gate(0)
                turned(2)
                gate(1)
                gate(2)
                st.phase()

        def even_dve(dve, st, TT, TSc, STT):
            dve.wait_ge(sem("even_in"), 16 * 13)
            for f in range(2):
                full(dve, ("gk", f))
                st.free(TSc(LX[:, f, :], bank(("gk", f))[:, 0:T], bgk[:, f:f + 1], None, ALU.add), ("gk", f))
            st.after
            st.tell(STT(LB, LX, -1.0, LX, ALU.mult, ALU.max), sem("gate_logits"))
            st.after
            st.run(TSc(LX, LX, 0.0, None, ALU.min))
            dve.wait_ge(sem("log_term"), 1)
            st.after
            st.run(TT(LX, LX, LB, ALU.subtract))
            for f in range(2):
                st.after
                ins = dve.tensor_tensor_scan(LB[:, f, :], keep, LX[:, f, :], 0.0, ALU.mult, ALU.add)
                if f:
                    st.tell(ins, sem("summed"))
                else:
                    st.run(ins)
            st.after
            for f in range(2):
                for k, (o, n, c) in enumerate(((0, SEQ, CA), (SEQ, TS, DSEQ))):
                    b = LB[:, f, o:o + n].rearrange("p (i c) -> p i c", c=c)
                    ins = TT(KDF[:, f, o:o + n].rearrange("p (i c) -> p i c", c=c),
                             b[:, :, c - 1:c].broadcast_to([P, n // c, c]), b, ALU.subtract)
                    if f and k:
                        st.tell(ins, sem("to_end"))
                    else:
                        st.run(ins)
            dve.wait_ge(sem("decays"), 3)
            for f in range(4):
                full(dve, ("qk", f))
                ps = bank(("qk", f))[:, 0:T]
                if f < 2:
                    if f == 0:
                        dve.wait_ge(sem("queries_zeroed"), 1)
                    st.run(STT(QI[0:64, f, 0, :], ps[0:64], DKA ** -0.5, EB[0:64, f, :], ALU.mult, ALU.mult))
                    st.free(STT(QI[64:128, f, 1, :], ps[64:128], DKA ** -0.5, EB[64:128, f, :], ALU.mult, ALU.mult), ("qk", f))
                else:
                    st.run(TT(KI[:, f - 2, :], ps, EN[:, f - 2, :], ALU.mult))
                    st.free(TT(KDF[:, f - 2, :], ps, KDF[:, f - 2, :], ALU.mult), ("qk", f))

            def mask_keys(j):
                r = CH[j][1]
                if j:
                    full(dve, ("dS", j - 1, 1, 1))
                full(dve, ("kdT", j))
                m = mch if j < 2 else mch_s
                st.free(TT(KDM[0:r], bank(("kdT", j))[0:r, 0:256].unsqueeze(1).broadcast_to([r, 8, 256]),
                           m[0:r, :].unsqueeze(2).broadcast_to([r, 8, 256]), ALU.mult), ("kdT", j))

            mask_keys(0)
            for j in range(2):
                for f in range(2):
                    for i2 in range(2):
                        name = ("dS", j, f, i2)
                        full(dve, name)
                        ps = bank(name)
                        for i in range(4):
                            n = 8 * j + 4 * i2 + i
                            ds_ = ps[:, P * i:P * i + P]
                            st.after
                            if n == 0:
                                st.run(dve.tensor_copy(SS[:, f, 1, :], ds_))
                                continue
                            t = CA * n + CA - 1
                            ins = STT(SS[:, f, n + 1, :], SS[:, f, n, :], EB[:, f, t:t + 1], ds_, ALU.mult, ALU.add)
                            if i == 3:
                                st.free(ins, name)
                            else:
                                st.run(ins)
                mask_keys(j + 1)
            st.after.nop().then_inc(sem("states"), 1)
            dve.wait_ge(sem("scores_zeroed"), 1)
            for h in range(H):
                full(dve, ("att", h))
                ps = bank(("att", h))
                for o in (0, P):
                    st.run(dve.copy_predicated(AT[:, h, o:o + P], mcau, ps[:, o:o + P]))
                st.free(dve.copy_predicated(AT[0:TS, h, SEQ:T], mcau_s[0:TS, :], ps[0:TS, SEQ:T]), ("att", h))
            for f in range(2):
                for i2 in range(2):
                    full(dve, ("dS", 2, f, i2))
            for f in range(2):
                for i2 in range(2):
                    name = ("dS", 2, f, i2)
                    for i in range(4):
                        b = 4 * i2 + i
                        t = SEQ + DSEQ * b + DSEQ - 1
                        ins = STT(gsn[:, f, b, :], gs0[:, f, b, :], EB[:, f, t:t + 1], bank(name)[:, P * i:P * i + P],
                                  ALU.mult, ALU.add)
                        if i == 3:
                            st.free(ins, name)
                        else:
                            st.run(ins)
            for g in range(4):
                full(dve, ("pool", g))
                st.free(TSc(MTE[:, 4 + g, :], bank(("pool", g))[:, 0:T], bpool[:, g:g + 1], pscale[:, g:g + 1],
                            ALU.add, ALU.mult), ("pool", g))
            for h in range(H):
                emptied(dve, ("ms", h))
                rs = RSE[:, h % 2, :]
                st.run(dve.reciprocal(rs, rs))
                st.after
                st.tell(STT(AT[:, h, :], AT[:, h, :], gnorm, rs, ALU.mult, ALU.mult), sem("headnorm"))
                st.after
                ins = TT(MTE[:, h, :], MTE[:, h, :], AT[:, h, :], ALU.mult)
                if h == H - 1:
                    st.tell(ins, sem("mixed", 0))
                else:
                    st.run(ins)

        def odd_dve(dve, st, TT, TSc, STT):
            gam = [1.0 - 2.0 ** (-5.0 - h) for h in range(H)]
            for j in range(3):
                emptied(dve, ("xTa1", j, 0))
            st.after
            st.tell(dve.tensor_copy(XS4, XT[:, :, SEQ:T].unsqueeze(2).broadcast_to([P, KC, 4, TS])), sem("xs4"))
            dve.wait_ge(sem("odd_in"), 16)
            for h in range(H):
                for m in range(2):
                    ne, no = ("qkh", h, 2 * m), ("qkh", h, 2 * m + 1)
                    full(dve, ne)
                    full(dve, no)
                    pe_, po = bank(ne)[:, 0:T], bank(no)[:, 0:T]
                    st.after
                    st.run(TT(RT[:, 0, :], pe_, cos, ALU.mult))
                    st.run(TT(RT[:, 1, :], po, sin, ALU.mult))
                    st.after
                    st.run(TT(RQ[:, 2 * m, :], RT[:, 0, :], RT[:, 1, :], ALU.subtract))
                    st.after
                    st.free(TT(RT[:, 0, :], pe_, sin, ALU.mult), ne)
                    st.free(TT(RT[:, 1, :], po, cos, ALU.mult), no)
                    st.after
                    dve.wait_ge(*(bank_free[GRP[ne][0]], GRP[ne][1] + 1))
                    st.tell(TT(RQ[:, 2 * m + 1, :], RT[:, 0, :], RT[:, 1, :], ALU.add), sem("roped"))
                st.after
                for e in range(2):
                    st.run(TT(QM[:, e], RQ[:, e, SEQ:T].unsqueeze(1).broadcast_to([P, NSEQ, TS]), qmask[:, h], ALU.mult))
                for e in range(2):
                    ins = dve.tensor_copy(KS4[:, e], RQ[:, 2 + e, SEQ:T].unsqueeze(1).broadcast_to([P, 4, TS]))
                    if e:
                        st.tell(ins, sem("sample_qk"))
                    else:
                        st.run(ins)
                full(dve, ("ratt", h))
                ps = bank(("ratt", h))
                st.run(TT(RAT[:, 0:SEQ], ps[:, 0:SEQ], dmask[:, h, :], ALU.mult))
                st.run(TT(RAT[:, SEQ:SEQ + P], ps[:, SEQ:SEQ + P], dmask[:, h, 0:P], ALU.mult))
                st.free(TT(RAT[0:TS, SEQ + P:SEQ + P + TS], ps[0:TS, SEQ + P:SEQ + P + TS], dmask_s[0:TS, h, :], ALU.mult),
                        ("ratt", h))
                for b in range(NSEQ):
                    k = NSEQ * h + b
                    for e in range(2):
                        full(dve, ("sn", h, b, e))
                        s = S0[k % NS0][:, e, :]
                        st.free(STT(s, s, gam[h] ** DSEQ, bank(("sn", h, b, e)), ALU.mult, ALU.add), ("sn", h, b, e))
                emptied(dve, ("rms", h))
                st.run(dve.reciprocal(RSQ[:, 0, :], RSQ[:, 0, :]))
                st.after
                for f in range(4):
                    st.run(TT(ROT[:, f, :], ROT[:, f, :], RSQ[:, 0, :], ALU.mult))
                st.after
                for f in range(4):
                    ins = TT(MT[:, 4 * h + f, :], MT[:, 4 * h + f, :], ROT[:, f, :], ALU.mult)
                    if f < 3:
                        st.run(ins)
                    else:
                        st.tell(ins, sem("headmix"))
            st.after.nop().then_inc(sem("mixed", 1), 1)
            st.last = None

        def experts_dve(dve, st, TT, TSc, STT, l, x_half, norm):
            R3 = [P, 3, E]
            x_half(f"xTb{l}", range(3))
            st.run(dve.memset(MSK, 0.0))
            st.run(dve.memset(POS, -1.0))
            st.run(dve.memset(TAB, 0.0))
            st.after
            emptied(dve, (f"router{l}",))
            dve.wait_ge(sem("rbias_in", l), 16)
            dve.wait_ge(sem("scores_cleared", l), 1)
            st.run(TT(SEL, SC, rbias.unsqueeze(1).broadcast_to(R3), ALU.add))
            sel8 = SEL.rearrange("p j (g k) -> p (j g) k", g=EG)
            st.after
            for g in range(24):
                st.run(dve.max(G8[:, g, :], sel8[:, g, :]))
            st.after
            st.run(TT(GS, G8[:, :, 0], G8[:, :, 1], ALU.add))
            st.after
            for j in range(3):
                g = GS[:, EG * j:EG * j + EG]
                other = g.unsqueeze(1).broadcast_to([P, EG, EG])
                own = g.unsqueeze(2).broadcast_to([P, EG, EG])
                a = GT8[:, 64 * j:64 * j + 64].rearrange("p (g k) -> p g k", g=EG)
                b = GE8[:, 64 * j:64 * j + 64].rearrange("p (g k) -> p g k", g=EG)
                st.run(TT(a, other, own, ALU.is_gt))
                st.run(TT(b, other, own, ALU.is_equal))
                st.after
                st.run(TT(b, b, tri8.rearrange("p (g k) -> p g k", g=EG), ALU.mult))
                st.after
                st.run(TT(a, a, b, ALU.add))
            st.after
            st.run(dve.tensor_reduce(RK, GT8.rearrange("p (g k) -> p g k", k=EG), AX.X, ALU.add))
            st.after
            st.run(TSc(RK, RK, TOPG - 0.5, None, ALU.is_lt))
            st.after
            mk8 = MK.rearrange("p j (g k) -> p (j g) k", g=EG)
            st.run(TT(mk8, sel8, RK.unsqueeze(2).broadcast_to([P, 24, EG]), ALU.mult))
            st.run(TSc(GS, RK, BIG, -BIG, ALU.mult, ALU.add))
            st.after
            st.run(TT(mk8, mk8, GS.unsqueeze(2).broadcast_to([P, 24, EG]), ALU.add))
            st.after
            for j in range(3):
                st.run(dve.max(T8[:, j, :], MK[:, j, :]))
            st.after
            for j in range(3):
                st.run(dve.match_replace(MR[:, j, :], T8[:, j, :], MK[:, j, :], -2 * BIG))
            st.after
            st.run(TSc(MSK[:, 0:2, :], MR[:, 0:2, :], -1.5 * BIG, None, ALU.is_lt))
            st.run(TSc(MSK[0:TS, 2, :], MR[0:TS, 2, :], -1.5 * BIG, None, ALU.is_lt))
            st.after.nop().then_inc(sem("chosen", l), 1)
            st.run(TT(MR, SC, MSK, ALU.mult))
            st.after
            st.run(dve.tensor_reduce(DEN, MR, AX.X, ALU.add))
            st.after
            st.run(TSc(DEN, DEN, 1e-20, None, ALU.add))
            st.after
            st.run(dve.reciprocal(DEN, DEN))
            st.after
            for j in range(3):
                st.run(TSc(TAB[:, j, 0:E, 1], MR[:, j, :], DEN[:, j:j + 1], ROUTED, ALU.mult, ALU.mult))
            for j in range(3):
                st.run(dve.tensor_tensor_scan(SEL[:, j, :], ones[:, 0:E], MSK[:, j, :], 0.0, ALU.mult, ALU.add))
            st.after
            for j in range(3):
                st.run(TSc(TAB[:, j, 0:E, 0], SEL[:, j, :], float(T), slotc[:, j:j + 1], ALU.mult, ALU.add))
            for f in range(2):
                full(dve, (f"sh{l}", 2 + f))
                emptied(dve, (f"sh{l}", f))
                st.free(TT(HSf[:, f, :], HSf[:, f, :], bank((f"sh{l}", 2 + f))[:, 0:T], ALU.mult), (f"sh{l}", 2 + f))
            full(dve, (f"cum{l}",))
            ps = bank((f"cum{l}",))
            st.run(STT(CUM[:, 0:2, :], ps[:, 0:2 * E].rearrange("p (j e) -> p j e", j=2), 1.0, MSK[:, 0:2, :], ALU.add, ALU.mult))
            st.run(STT(CUM[0:TS, 2, :], ps[0:TS, 2 * E:3 * E], 1.0, MSK[0:TS, 2, :], ALU.add, ALU.mult))
            st.free(dve.tensor_copy(PT[:, :, SEQ:T], ps[:, 256:256 + 2 * TS].rearrange("p (f t) -> p f t", f=2)), (f"cum{l}",))
            st.after
            st.run(TSc(POS[:, 0:2, 0:E], CUM[:, 0:2, :], -1.0, None, ALU.add))
            st.run(TSc(POS[0:TS, 2, 0:E], CUM[0:TS, 2, :], -1.0, None, ALU.add))
            st.after
            st.tell(dve.tensor_reduce(colmax, POS, AX.XY, ALU.max), sem("colmax", l))

            def onehot(u, pr, off):
                pos = POS[:, :, 2 * pr:2 * pr + 2] if isinstance(pr, int) else POS[:, :, bass.ds(2 * pr, 2)]
                it_ = iota[:, 0:BLK] if isinstance(off, int) else iota[:, bass.ds(off, BLK)]
                for j in range(3):
                    last = TT(OH[u][:, j], it_.unsqueeze(1).broadcast_to([P, 2, BLK]),
                              pos[:, j].unsqueeze(2).broadcast_to([P, 2, BLK]), ALU.is_equal)
                return last

            def meta(u, ps):
                return dve.tensor_copy(META[u], ps[:, 0:4])

            def gates(u):
                dve.tensor_copy(GATE[u][0:64, :], META[u][0:64, 1:2])
                return dve.tensor_copy(GATE[u][64:128, :], META[u][64:128, 3:4])

            def slot_rows(u):
                TSc(SI[u][0:64, :], META[u][0:64, 0:1], FAR, None, ALU.add)
                return TSc(SI[u][64:128, :], META[u][64:128, 2:3], FAR, None, ALU.add)

            def hidden(u):
                return STT(HH[u], HS[u], GATE[u], PS[:, 2, DE:2 * DE], ALU.mult, ALU.mult)

            base = GRP[(f"moe{l}",)]
            st.after
            onehot(0, 0, 0).then_inc(sem("onehot", l), 1)
            full(dve, (f"flag{l}",))
            st.free(dve.tensor_reduce(flagf[0:1, :], bank((f"flag{l}",))[0:1, 0:P], AX.X, ALU.max), (f"flag{l}",))
            st.after
            st.tell(TSc(flagi[0:1, :], flagf[0:1, :], BLK - 0.5, None, ALU.is_gt), sem("flag_ready", l))
            full(dve, (f"lists{l}",))
            st.free(meta(0, bank((f"lists{l}",))), (f"lists{l}",))
            st.after
            gates(0)
            onehot(1, 1, 0).then_inc(sem("onehot", l), 1)
            for j, (o, r) in enumerate(CH):
                for n in range(2):
                    name = (f"shd{l}", j, n)
                    full(dve, name)
                    x = X[0:r, j, 512 * n:512 * n + 512]
                    st.free(STT(F[0:r, j, 512 * n:512 * n + 512], x, ALPHA, bank(name)[0:r, :], ALU.mult, ALU.add), name)

            def two_pairs(it):
                for u in range(2):
                    v = 1 - u
                    pr = 2 * it + u
                    dve.wait_ge(bank_full[6], base[6] + pr + 1)
                    dve.wait_ge(bank_free[4], base[4] + pr)
                    meta(v, PS[:, 6, :]).then_inc(bank_free[6], 1)
                    dve.wait_ge(bank_free[6], base[6] + pr + 1)
                    gates(v).then_inc(sem("gates", l), 1)
                    onehot(u, pr + 2, 0).then_inc(sem("onehot", l), 1)
                    dve.wait_ge(bank_full[2], base[2] + pr + 1)
                    dve.wait_ge(sem("silu", l), pr + 1)
                    dve.wait_ge(sem("gates", l), pr + 1)
                    hidden(u).then_inc(bank_free[2], 1)
                    if not isinstance(it, int):
                        dve.wait_ge(sem("scattered", l, u), 16 * it)
                    slot_rows(u).then_inc(sem("slot_rows", l), 1)
                    dve.wait_ge(bank_full[4], base[4] + pr + 1)
                    dve.tensor_copy(YS[u][:, 0:512], PS[:, 4, :]).then_inc(bank_free[4], 1)

            two_pairs(0)
            with dve.Fori(1, PAIRS // 2) as it:
                two_pairs(it)
            dve.wait_ge(sem("flag_ready", l), 1)
            go = dve.value_load(flagi[0:1, 0:1], min_val=0, max_val=1)
            with dve.If(go > 0):
                dve.wait_ge(sem("scattered", l, 0), 16 * (PAIRS // 2))
                dve.wait_ge(sem("scattered", l, 1), 16 * (PAIRS // 2))
                with dve.Fori(0, 4) as m:
                    with dve.Fori(0, PAIRS) as pr:
                        s = m * PAIRS + pr
                        onehot(0, pr, m * BLK + BLK).then_inc(sem("ov_onehot", l), 1)
                        dve.wait_ge(sem("ov_meta", l), s + 1)
                        meta(0, PS[:, 6, :]).then_inc(sem("ov_metac", l), 1)
                        dve.wait_ge(sem("ov_metac", l), s + 1)
                        dve.wait_ge(sem("ov_rows_left", l), s + 1)
                        gates(0)
                        slot_rows(0).then_inc(sem("ov_lists", l), 1)
                        dve.wait_ge(sem("ov_silu", l), s + 1)
                        dve.wait_ge(sem("ov_lists", l), s + 1)
                        hidden(0).then_inc(sem("ov_hidden", l), 1)
                        dve.wait_ge(sem("ov_y", l), s + 2)
                        dve.tensor_copy(YS[0][:, 0:512], PS[:, 4, :])
                        dve.tensor_copy(YS[0][:, 512:1024], PS[:, 5, :]).then_inc(sem("ov_yc", l), 1)
            dve.nop()
            st.last = None
            st.last = None

            def summed(i):
                j = ORD[i]
                r = CH[j][1]
                for n in range(2):
                    dve.wait_ge(sem("y_in", l, n), 16 * (i + 1))
                    st.after
                    st.tell(dve.tensor_reduce(YR[0:r, :], YK[n][0:r].rearrange("p k n -> p n k"), AX.X, ALU.add),
                            sem("y_summed", l))
                    st.after
                    x = X[0:r, j, 512 * n:512 * n + 512]
                    st.run(TT(x, F[0:r, j, 512 * n:512 * n + 512], YR[0:r, :], ALU.add))

            def turned(i):
                summed(i)
                norm(l, 2, i, ORD[i], sem("x_ln2", l))
                x_half(f"xTc{l}", (ORD[i],))

            def gate(i):
                j = ORD[i]
                r = CH[j][1]
                for n in range(2):
                    emptied(dve, (f"pg{l}", j, n))
                    cols = slice(512 * n, 512 * n + 512)
                    st.run(TT(SG[n][0:r, :], SG[n][0:r, :], PP[0:r, j, cols], ALU.mult))
                    x = X[0:r, j, cols]
                    st.after
                    st.tell(TT(x, x, SG[n][0:r, :], ALU.add), sem("gated", l))
                st.after
                st.tell(dve.nop(), sem("x_out", l))

            turned(0)
            turned(1)
            gate(0)
            turned(2)
            gate(1)
            gate(2)

        @block.vector
        def _(dve):
            st = Steps(dve, sem("dve_steps"))
            TT, TSc, STT = dve.tensor_tensor, dve.tensor_scalar, dve.scalar_tensor_tensor

            def x_half(tag, chunks):
                for j in chunks:
                    o, r = CH[j]
                    full(dve, (tag, j, 1))
                    st.free(dve.tensor_copy(XT[:, 4:8, o:o + r],
                                            bank((tag, j, 1)).rearrange("p (c t) -> p c t", c=4)[:, :, 0:r]), (tag, j, 1))

            def norm(l, k, i, j, done):
                r = CH[j][1]
                st.after
                for n in range(2):
                    st.run(dve.bn_stats(bnst[0:r, 6 * n:6 * n + 6], X[0:r, j, 512 * n:512 * n + 512]))
                st.after
                st.tell(dve.bn_aggr(bnag[0:r, 2 * j:2 * j + 2], bnst[0:r, :]), sem("variance", l, k))
                dve.wait_ge(sem("std", l, k), i + 1)
                st.run(dve.reciprocal(rstd[:, j:j + 1], rstd[:, j:j + 1]))
                if i == 0:
                    dve.wait_ge(sem("ln_in", l, k), 32)
                x = X[0:r, j, :]
                st.after
                st.run(TSc(x, x, bnag[0:r, 2 * j:2 * j + 1], rstd[0:r, j:j + 1], ALU.subtract, ALU.mult))
                st.after
                st.run(TT(x, x, LN[0:r, 0, :], ALU.mult))
                st.after
                st.tell(TT(x, x, LN[0:r, 1, :], ALU.add), done)

            dve.wait_ge(sem("ones_set"), 1)
            dve.wait_ge(sem("const_in"), 16)
            for l in range(DEPTH):
                x_half(f"xTa{l}", ORD)
                if l % 2 == 0:
                    even_dve(dve, st, TT, TSc, STT)
                else:
                    odd_dve(dve, st, TT, TSc, STT)
                for j, (o, r) in enumerate(CH):
                    for n in range(2):
                        name = (f"out{l}", j, n)
                        full(dve, name)
                        x = X[0:r, j, 512 * n:512 * n + 512]
                        st.free(STT(x, x, ALPHA, bank(name)[0:r, :], ALU.mult, ALU.add), name)
                    norm(l, 1, j, j, sem("x_mid", l))
                st.phase()
                experts_dve(dve, st, TT, TSc, STT, l, x_half, norm)
                st.phase()

        def even_pool(pool, st, store):
            s = sem("even_out")
            n_out = 0
            store(O["pool_sample"][0, :, 0:PBUF - DSEQ, :], A["state_pool"][0, :, DSEQ:PBUF, :], s)
            st.tell(pool.memset(QI, 0.0), sem("queries_zeroed"))
            st.run(pool.memset(UE[:, :, 0:PBUF], 0.0))
            for f in range(4):
                emptied(pool, ("u", f))
            emptied(pool, ("spT",))
            for f in range(4):
                emptied(pool, ("qk", f))
            for g, w in enumerate(WINDOWS):
                for kind in range(2):
                    if kind == 0:
                        n, new = SEQ, SEQ
                        ext = UE[:, g, :].unsqueeze(1)
                        buf = [b[:, 0:PBUF + SEQ].unsqueeze(1) for b in PWK]
                        dst = DD[:, g, 0:SEQ].unsqueeze(1)
                    else:
                        n, new = 1, DSEQ
                        ext = US[:, g]
                        buf = [b[:, 0:NSEQ * 19].rearrange("p (b t) -> p b t", b=NSEQ) for b in PWK]
                        dst = DD[:, g, SEQ:T].rearrange("p (b t) -> p b t", b=NSEQ)
                    cur, step, k, ln = ext, 1, 0, PBUF + new
                    while step < w:
                        nxt = buf[k % 2]
                        st.after
                        st.run(pool.tensor_tensor(nxt[:, :, 2 * step - 1:ln], cur[:, :, 2 * step - 1:ln],
                                                  cur[:, :, step - 1:ln - step], ALU.add))
                        cur, step, k = nxt, 2 * step, k + 1
                    win = cur[:, :, PBUF:ln]
                    st.after
                    if kind == 0:
                        st.run(pool.tensor_tensor(win[:, :, 0:16], win[:, :, 0:16],
                                                  invc[:, 16 * g:16 * g + 16].unsqueeze(1), ALU.mult))
                        st.run(pool.tensor_scalar(win[:, :, 16:SEQ], win[:, :, 16:SEQ], 1.0 / w, None, ALU.mult))
                    else:
                        st.run(pool.tensor_scalar(win, win, 1.0 / w, None, ALU.mult))
                    st.after
                    ins = pool.tensor_tensor(dst, win, ext[:, :, PBUF:ln], ALU.subtract)
                    if kind:
                        st.tell(ins, sem("pool_d"))
                    else:
                        st.run(ins)
            for f in range(4):
                emptied(pool, ("r", f))
            st.tell(pool.memset(AT, 0.0), sem("scores_zeroed"))
            emptied(pool, ("puT",))
            store(O["pool_prompt"][0, 0], PUO[0:PBUF, :], s)
            emptied(pool, ("usT",))
            for b in range(NSEQ):
                store(O["pool_sample"][0, b, PBUF - DSEQ:PBUF, :], spl[DSEQ * b:DSEQ * b + DSEQ, :], s)
            pool.wait_ge(sem("states"), 1)
            for f in range(2):
                for i2 in range(2):
                    emptied(pool, ("dS", 2, f, i2))
            for h in range(H):
                f, r = h // 2, 64 * (h % 2)
                store(O["gla_prompt"][0, 0, h], SS[r:r + 64, f, 16, :], s)
                store(O["gla_sample"][0, :, h].rearrange("b k v -> k b v"), gsn[r:r + 64, f, :, :], s)
            pool.wait_ge(s, 16 * (1 + 1 + NSEQ + 2 * H))

        def odd_pool(pool, st, store):
            def rows(x):
                return x.rearrange("(p e) v -> p e v", e=2)

            def load(k):
                pool.dma_start(S0[k % NS0], rows(A["state_ret"][0, k % NSEQ, k // NSEQ])).then_inc(sem("s0_in", k % NS0), 16)

            for k in range(NS0):
                load(k)
            for k in range(NSEQ * H):
                h, b = k // NSEQ, k % NSEQ
                for e in range(2):
                    emptied(pool, ("sn", h, b, e))
                store(rows(O["ret_sample"][0, b, h]), S0[k % NS0], sem("s0_out", k % NS0))
                if k + NS0 < NSEQ * H:
                    pool.wait_ge(sem("s0_out", k % NS0), 16 * (k // NS0 + 1))
                    load(k + NS0)
                if b == NSEQ - 1:
                    for e in range(2):
                        emptied(pool, ("sp", h, e))
                    store(rows(O["ret_prompt"][0, 0, h]), SPo, sem("sp_out"))
            pool.wait_ge(sem("sp_out"), 16 * H)
            for i in range(NS0):
                pool.wait_ge(sem("s0_out", i), 16 * ((NSEQ * H - i + NS0 - 1) // NS0))

        def experts_pool(pool, st, store, l):
            st.run(pool.memset(SC[:, 2, :], 0.0))
            st.after.nop().then_inc(sem("scores_cleared", l), 1)
            st.last = None
            base = GRP[(f"moe{l}",)]
            last_slot = pool.to_reg(TOPK * T - 1)

            def scatter(u, s):
                pool.sem_inc(sem("scatters_begun", l))
                pool.indirect_dma_start(yd, bass.IndirectOffsetOnAxis(ap=SI[u], axis=0), YS[u], None,
                                        bounds_check=last_slot, oob_is_err=False).then_inc(s, 16)

            with pool.Fori(0, PAIRS // 2) as it:
                for u in range(2):
                    pr = 2 * it + u
                    pool.wait_ge(sem("slot_rows", l), pr + 1)
                    for b in (4, 5):
                        pool.wait_ge(bank_free[b], base[b] + pr + 1)
                    scatter(u, sem("scattered", l, u))
            for u in range(2):
                pool.wait_ge(sem("scattered", l, u), 16 * (PAIRS // 2))
            pool.wait_ge(sem("flag_ready", l), 1)
            go = pool.value_load(flagi[0:1, 0:1], min_val=0, max_val=1)
            with pool.If(go > 0):
                pool.sem_inc(sem("ov_rows_left", l), 1)
                with pool.Fori(0, 4) as m:
                    with pool.Fori(0, PAIRS) as pr:
                        s = m * PAIRS + pr
                        pool.wait_ge(sem("ov_lists", l), s + 1)
                        pool.wait_ge(sem("ov_yc", l), s + 1)
                        scatter(0, sem("ov_scattered", l))
                        pool.wait_ge(sem("ov_scattered", l), 16 * s + 16)
                        pool.sem_inc(sem("ov_rows_left", l), 1)
            pool.nop().then_inc(sem("all_scattered", l), 1)


        @block.gpsimd
        def _(pool):
            st = Steps(pool, sem("pool_steps"))
            st.run(pool.memset(ones, 1.0))
            st.run(pool.memset(onesA, 1.0 / DVA))
            st.run(pool.memset(onesC, 1.0 / DVC))
            st.run(pool.memset(eps, EPS))
            st.run(pool.memset(bnag, 1.0))
            st.after.nop().then_inc(sem("ones_set"), 1)
            st.last = None

            def store(dst, src, s):
                pool.dma_start(dst, src).then_inc(s, 16)

            for l in range(DEPTH):
                if l % 2 == 0:
                    even_pool(pool, st, store)
                else:
                    odd_pool(pool, st, store)
                st.phase()
                experts_pool(pool, st, store, l)
                if l == DEPTH - 1:
                    for i, j in enumerate(ORD):
                        o, r = CH[j]
                        pool.wait_ge(sem("x_out", l), i + 1)
                        dst = O["y_prompt"][0, o:o + r, :] if j < 2 else O["y_sample"].rearrange("b s d -> (b s) d")
                        store(dst, X[0:r, j, :], sem("stored"))
                    pool.wait_ge(sem("stored"), 48)
                st.phase()

_INS = ['x_prompt', 'x_sample', 'state_gla', 'state_pool', 'state_ret', 'p_prompt', 'p_sample',
        'w_in_a', 'w_gk2', 'b_gk', 'g_norm_a', 'w_pool', 'b_pool', 'pool_scale', 'w_out_a',
        'w_in_c', 'w_out_c', 'ln1_g', 'ln1_b', 'ln2_g', 'ln2_b',
        'w_router', 'router_bias', 'w_exp_gate', 'w_exp_up', 'w_exp_down',
        'w_sh_gate', 'w_sh_up', 'w_sh_down', 'w_ple_gate', 'w_ple_proj']
_OUTS = [("y_prompt", (1, SEQ, D)), ("y_sample", (NSEQ, DSEQ, D)), ("gla_prompt", (1, 1, H, DKA, DVA)),
         ("pool_prompt", (1, 1, PBUF, 512)), ("ret_prompt", (1, 1, H, DKC, DVC)),
         ("gla_sample", (1, NSEQ, H, DKA, DVA)), ("pool_sample", (1, NSEQ, PBUF, 512)),
         ("ret_sample", (1, NSEQ, H, DKC, DVC))]


def kernel(**inputs):
    import numpy as _np
    import concourse.bacc as _bacc
    from concourse import mybir as _mybir
    from concourse.bass_utils import run_bass_kernel_spmd as _run

    nc = _bacc.Bacc("TRN2", target_bir_lowering=False, num_devices=1)
    arrays, args = {}, {}
    for name in _INS:
        a = _np.ascontiguousarray(inputs[name])
        arrays[f"in_{name}"] = a
        args[name] = nc.dram_tensor(f"in_{name}", a.shape, _mybir.dt.from_np(a.dtype), kind="ExternalInput").ap()
    tables = []
    for i, a in enumerate(constants()):
        arrays[f"table_{i}"] = a
        tables.append(nc.dram_tensor(f"table_{i}", a.shape, F32, kind="ExternalInput").ap())
    outs = {n: nc.dram_tensor(f"out_{n}", s, F32, kind="ExternalOutput").ap() for n, s in _OUTS}
    trunk(nc, args, outs, tables)
    r = _run(nc, [arrays], core_ids=[0])
    return tuple(r.results[0][f"out_{n}"] for n, _ in _OUTS)
```

```python
from contextlib import ExitStack

import numpy as np

import concourse.bass as bass
from concourse import mybir

F32 = mybir.dt.float32
F32R = mybir.dt.float32r
U32 = mybir.dt.uint32
I32 = mybir.dt.int32
ALU = mybir.AluOpType
ACT = mybir.ActivationFunctionType
AX = mybir.AxisListType

P = 128
D = 1024
SEQ = 256
NSEQ = 8
DSEQ = 4
PAST = 2048
TS = NSEQ * DSEQ
T = SEQ + TS
CH = [(0, 128), (128, 128), (256, TS)]
ORD = (2, 0, 1)
KC = D // P
DEPTH = 2
H = 4
DKA = 64
DVA = 128
RANK = 16
CA = 16
NCA = SEQ // CA
WINDOWS = (2, 4, 8, 16)
PBUF = 15
DKC = 256
DVC = 512
E = 64
EG = 8
TOPG = 4
TOPK = 8
DE = 256
ROUTED = 2.5
PD = 256
ALPHA = (2.0 * DEPTH) ** 0.25
EPS = 1e-5
BLK = 64
PAIRS = E // 2
MOE_PANELS = 3 * PAIRS - 1
SLOTS = 6
PW = 4096
FAR = 4096.0
BIG = 1e30
YW = 704
EP = E + 4
QCOL, KCOL, VCOL, RCOL, GCOL, UCOL = 0, 256, 512, 1024, 1536, 1552


class Cut:

    def __init__(self, ap, size):
        self.ap, self.size, self.at = ap, size, 0

    def take(self, n):
        a = self.ap[:, self.at:self.at + n]
        self.at += n
        assert self.at <= self.size, (self.at, self.size)
        return a


def constants():
    p = np.arange(P)
    common = [np.eye(P), (p[:, None] < p[None, :]) * 1.0,
              np.tile(np.arange(BLK * 5), (P, 1)),
              np.stack([p + o - FAR - T for o, _ in CH], 1),
              np.tile((np.arange(8)[None, :] < np.arange(8)[:, None]).reshape(-1), (P, 1)),
              np.tile(np.eye(TS), (4, 4))]
    t = np.arange(T)
    first = np.where(t < SEQ, t % CA == 0, t % DSEQ == 0)
    causal = (p[:, None] // CA == p[None, :] // CA) & (p[:, None] <= p[None, :])
    s = np.arange(TS)
    causal_s = np.zeros((P, TS), bool)
    causal_s[:TS] = (s[:, None] // DSEQ == s[None, :] // DSEQ) & (s[:, None] <= s[None, :])
    inv = np.stack([1.0 / np.minimum(np.arange(16) + 1, w) for w in WINDOWS])
    even = [np.tile(1.0 - first, (P, 1)), causal * 1.0, causal_s * 1.0,
            (p[:, None] // CA == np.arange(8)[None, :]) * 1.0,
            ((p[:, None] // DSEQ) == np.arange(8)[None, :]) * 1.0,
            np.tile(inv.reshape(-1), (P, 1))]
    f = np.float32
    freq = (f(1.0) / np.power(f(10000.0), np.linspace(0.0, 1.0, DKC // 2, dtype=f), dtype=f)).astype(f)
    pos = np.concatenate([np.arange(SEQ), np.tile(PAST + np.arange(DSEQ), NSEQ)]).astype(f)
    ang = (freq[:, None] * pos[None, :]).astype(f).astype(np.float64)
    gam = 1.0 - 2.0 ** (-5.0 - np.arange(H))
    kscale = DKC ** -0.5
    dm = np.zeros((P, H, SEQ))
    tt = np.arange(SEQ)[None, :] - p[:, None]
    for h in range(H):
        dm[:, h] = np.where(tt >= 0, gam[h] ** np.maximum(tt, 0), 0) * kscale
    ds = np.zeros((P, H, TS))
    for h in range(H):
        ds[:TS, h] = causal_s[:TS] * gam[h] ** np.maximum(s[None, :] - s[:, None], 0) * kscale
    own = np.tile(s[None, :] // DSEQ == np.arange(NSEQ)[:, None], (P, 1, 1))
    qg = np.tile(gam[:, None] ** (s[None, :] % DSEQ + 1), (P, 1, 1))
    kd = np.zeros((P, 2, H))
    for j in range(2):
        kd[:, j] = gam[None, :] ** (SEQ - 1 - 128 * j - p)[:, None] * kscale
    kds = gam[None, :] ** (DSEQ - 1 - p[:, None] % DSEQ) * kscale
    own_k = (p[:, None] % TS) // DSEQ == np.arange(NSEQ)[None, :]
    odd = [np.cos(ang), np.sin(ang), dm.reshape(P, -1), ds.reshape(P, -1), own.reshape(P, -1),
           qg.reshape(P, -1), kd.reshape(P, -1), kds, own_k]
    return [np.ascontiguousarray(np.concatenate([np.asarray(a, f) for a in x], 1), dtype=f)
            for x in (common, even, odd)]


def odd_schedule():
    steps = []
    for h in range(H):
        dense = [("qkh", h, f) for f in range(4)] + [("vstrips", h, 0), ("vv", h, 0), ("vv", h, 2), ("vv", h, 1)]
        dense += [("gg", h, f) for f in range(4)]
        rest = []
        if h:
            seqs = [("seq", h - 1, b) for b in range(NSEQ)]
            rest = [("state", h - 1, 0), ("outp", h - 1, 0), seqs[0], ("norm", h - 1, 0)] + seqs[1:]
            rest += [("outs", h - 1, 0), ("norm", h - 1, 1)]
        for i in range(len(dense)):
            steps.append(dense[i])
            steps += rest[len(rest) * i // len(dense):len(rest) * (i + 1) // len(dense)]
        steps.append(("scores", h, 0))
    h = H - 1
    seqs = [("seq", h, b) for b in range(NSEQ)]
    steps += [("state", h, 0), ("outp", h, 0)] + seqs[0:2] + [("norm", h, 0)] + seqs[2:4] + [("out", 0, 0)] + seqs[4:6]
    steps += [("out", 0, 1)] + seqs[6:8] + [("outs", h, 0), ("out", 1, 0), ("norm", h, 1), ("out", 1, 1)]
    steps += [("out", 2, 0), ("out", 2, 1), ("fold", 2, 0), ("fold", 2, 1)]
    return steps


def group_order():
    g = []

    def xt(tag, chunks):
        g.extend((tag, j, q) for j in chunks for q in range(2))

    def out(tag, chunks=range(3)):
        g.extend((tag, j, n) for j in chunks for n in range(2))
        if 2 in chunks and tag[:2] in ("ou", "pg"):
            at = g.index((tag, 2, 1)) + 1
            g[at:at] = [(tag, "fold", n) for n in range(2)]

    for l in range(DEPTH):
        xt(f"xTa{l}", ORD)
        if l % 2 == 0:
            g.append(("glr",))
            g.extend(("gk", f) for f in range(2))
            g.extend(("qk", f) for f in range(4))
            g.extend(("v", j) for j in range(3))
            g.append(("spT",))
            g.extend(("u", f) for f in range(4))
            g.extend((("kdT", 0), ("puT",), ("usT",)))
            for j in range(2):
                g.extend(("r", 2 * j + f) for f in range(2))
                g.extend(("dS", j, f, i) for f in range(2) for i in range(2))
                g.append(("kdT", j + 1))
            g.extend(("att", h) for h in range(H))
            g.extend(("dS", 2, f, i) for f in range(2) for i in range(2))
            g.extend((("oT", 0), ("oT", 1), ("oTs",)))
            g.extend(("pool", f) for f in range(4))
            g.extend(("ms", j) for j in range(3))
        else:
            for kind, h, i in odd_schedule():
                if kind == "scores":
                    g.extend((("ratt", h), ("kT", h), ("kTs", h)))
                elif kind == "state":
                    g.extend(("sp", h, e) for e in range(2))
                elif kind == "seq":
                    if i == 0:
                        g.append(("o4", h))
                    g.extend(("sn", h, i, e) for e in range(2))
                elif kind == "outp":
                    g.extend(("roT", h, f) for f in range(2))
                elif kind == "outs":
                    g.append(("roTs", h))
                elif kind == "norm":
                    g.append(("rms", h, i))
                elif kind in ("out", "fold"):
                    g.append((f"out{l}", "fold" if kind == "fold" else h, i))
                else:
                    g.append((kind, h, i))
        if l % 2 == 0:
            out(f"out{l}")
        xt(f"xTb{l}", range(3))
        g.append((f"router{l}",))
        g.extend((f"sh{l}", f) for f in (0, 2, 1))
        g.extend(((f"pT{l}",), (f"cum{l}",), (f"sh{l}", 3), (f"flag{l}",), (f"lists{l}",)))
        g.extend((f"rows{l}", q) for q in range(2))
        g.append((f"moe{l}",))
        out(f"shd{l}", ORD)
        out(f"pw{l}", ORD)
        g.extend((f"fold{l}", n) for n in range(2))
        for j in ORD:
            xt(f"xTc{l}", (j,))
            out(f"pg{l}", (j,))
    return g


ODD_GROUPS = ("qkh", "vv", "vstrips", "gg", "ratt", "kT", "kTs", "roT", "roTs", "sn", "sp", "rms", "out1")


def plan_groups():
    at, used, nxt, banks = {}, [0] * 8, 0, 8
    for name in group_order():
        if name[0].startswith("moe"):
            at[name] = list(used)
            for b in range(7):
                used[b] += PAIRS
            continue
        if name[0] == "o4":
            b = 7
        else:
            banks = 7 if name[0] in ODD_GROUPS else 8
            b = nxt % banks
            nxt += 1
        at[name] = (b, used[b])
        used[b] += 1
    return at


def plan_panels():
    p = []
    for l in range(DEPTH):
        if l % 2 == 0:
            p += [(("qk",), ("qk", 3)), (("v",), ("v", 2)), (("u",), ("u", 3)), (("r",), ("r", 3))]
            p += [((f"out{l}", n), (f"out{l}", 2, 1)) for n in range(2)]
        else:
            for h in range(H):
                p += [(("qk", h), ("qkh", h, 3)), (("v", h), ("vv", h, 1)), (("g", h), ("gg", h, 3))]
            p += [((f"out{l}", n, k), (f"out{l}", 2, 1)) for n in range(2) for k in range(2)]
        p += [((f"shgu{l}",), (f"sh{l}", 3))]
        p += [((f"moe{l}",), None)]
        p += [((f"dp{l}",), (f"pw{l}", ORD[-1], 1))]
        p += [((f"pg{l}", n), (f"pg{l}", ORD[-1], 1)) for n in range(2)]
    return p


def trunk(nc, A, O, C):
    GRP = plan_groups()
    PANELS = plan_panels()
    NUM, n = {}, 0
    for name, _ in PANELS:
        NUM[name] = n
        n += MOE_PANELS if name[0].startswith("moe") else 1
    LAST = {}
    for name, g in PANELS:
        if name[0].startswith("moe"):
            l = int(name[0][3:])
            for k in range(MOE_PANELS):
                LAST[NUM[name] + k] = (f"moe{l}", k // 3, 5 if k % 3 == 2 else 2)
        else:
            LAST[NUM[name]] = g

    with ExitStack() as ctx:
        def sb(name, cols, dt=F32):
            return ctx.enter_context(nc.sbuf_tensor(name, [P, cols], dt))

        names = {}

        def sem(*name):
            key = "_".join(map(str, name))
            if key not in names:
                names[key] = ctx.enter_context(nc.semaphore(key))
            return names[key]

        W = sb("weights", SLOTS * PW)
        Xb = sb("x_tok", 3 * D)
        XTb = sb("x_feat", KC * T)
        LNb = sb("ln_rows", 2 * D)
        CC = sb("const", C[0].shape[1])
        SIDE = sb("side", 2048)
        SMb = sb("small", 480)
        ASZ = 16830
        AR = sb("arena", ASZ)
        SPLIT = sb("split", 1024, F32R)
        PS = ctx.enter_context(nc.psum_tensor("ps", [P, 8, 512], F32))
        yd = nc.dram_tensor("y_slots", (TOPK * T, D), F32, kind="Internal").ap()

        X = Xb[:, :].rearrange("p (j n) -> p j n", j=3)
        XT = XTb[:, :].rearrange("p (c t) -> p c t", c=KC)
        LN = LNb[:, :].rearrange("p (k n) -> p k n", k=2)
        cc = Cut(CC[:, :], C[0].shape[1])
        ident, tri = cc.take(P), cc.take(P)
        iota = cc.take(BLK * 5)
        slotc = cc.take(3)
        tri8 = cc.take(64)
        fold_all = cc.take(P)
        fold4 = fold_all[:, 0:TS]

        sm = Cut(SMb[:, :], 480)
        ones = sm.take(P)
        onesA = sm.take(P)
        onesC = sm.take(P)
        eps, zero1 = sm.take(1), sm.take(1)
        rbias = sm.take(E)
        bnst = sm.take(12)
        bnag = sm.take(6)
        rstd = sm.take(3)
        colmax, flagf = sm.take(1), sm.take(1)
        flagi = sm.take(1).bitcast(I32)

        a = Cut(AR[:, :], ASZ)
        MTE = a.take(8 * T).rearrange("p (f t) -> p f t", f=8)
        CE = a.take(C[1].shape[1])
        ce = Cut(CE, C[1].shape[1])
        keep, mcau, mcau_s = ce.take(T), ce.take(P).bitcast(U32), ce.take(TS).bitcast(U32)
        mch, mch_s = ce.take(8), ce.take(8)
        invc = ce.take(64)
        gate_ops = a.take(8 * RANK + 256 + T)
        wglr = gate_ops[:, 0:128].rearrange("p (c n) -> p c n", c=8)
        wgk2 = gate_ops[:, 128:384]
        glrT = gate_ops[:, 384:384 + T]
        PUO = gate_ops[:, 0:512]
        bgk, gnorm, bpool, pscale = a.take(2), a.take(1), a.take(4), a.take(4)
        wpool = a.take(512)
        LXB = a.take(4 * T)
        LX, LB = (LXB[:, 2 * T * i:2 * T * i + 2 * T].rearrange("p (f t) -> p f t", f=2) for i in range(2))
        keys = a.take(4 * T)
        KDF, KI = (keys[:, 2 * T * i:2 * T * i + 2 * T].rearrange("p (f t) -> p f t", f=2) for i in range(2))
        RSE = [keys[:, 512 * i:512 * i + 512].rearrange("p (h t) -> p h t", h=4) for i in range(2)]
        EB = a.take(2 * T).rearrange("p (f t) -> p f t", f=2)
        QI = a.take(4 * T).rearrange("p (f k t) -> p f k t", f=2, k=2)
        EN = LX
        DD = LXB.rearrange("p (g t) -> p g t", g=4)
        V = a.take(3 * 512).rearrange("p (j n) -> p j n", j=3)
        UE = a.take(4 * (PBUF + SEQ)).rearrange("p (g t) -> p g t", g=4)
        US = a.take(4 * NSEQ * 19).rearrange("p (g b t) -> p g b t", g=4, b=NSEQ)
        PWK = [a.take(272) for _ in range(2)]
        USC = a.take(4 * TS).rearrange("p (g t) -> p g t", g=4)
        spl = a.take(512)
        SS = a.take(2 * 17 * 128).rearrange("p (f i v) -> p f i v", f=2, i=17)
        gs0 = LNb[:, :].rearrange("p (f b v) -> p f b v", f=2, b=8)
        KDM = SIDE[:, :].rearrange("p (i n) -> p i n", i=8)
        gsn = SIDE[:, :].rearrange("p (f b v) -> p f b v", f=2, b=8)
        SQE = XTb[:, 0:4 * T].rearrange("p (h t) -> p h t", h=4)
        AT = XTb[:, 4 * T:8 * T].rearrange("p (h t) -> p h t", h=4)
        a = Cut(AR[:, :], ASZ)
        MT = a.take(16 * T).rearrange("p (f t) -> p f t", f=16)
        CO = a.take(C[2].shape[1])
        co = Cut(CO, C[2].shape[1])
        cos, sin = co.take(T), co.take(T)
        dmask = co.take(4 * SEQ).rearrange("p (h t) -> p h t", h=4)
        dmask_s = co.take(4 * TS).rearrange("p (h t) -> p h t", h=4)
        own_q = co.take(NSEQ * TS).rearrange("p (b t) -> p b t", b=NSEQ)
        qdec = co.take(4 * TS).rearrange("p (h t) -> p h t", h=4)
        kdec = co.take(8).rearrange("p (j h) -> p j h", j=2)
        kdec_s, own_k = co.take(4), co.take(8)
        RQ = a.take(4 * T).rearrange("p (f t) -> p f t", f=4)
        RT = a.take(2 * T).rearrange("p (f t) -> p f t", f=2)
        RV = [a.take(3 * 512).rearrange("p (j n) -> p j n", j=3) for _ in range(2)]
        KD = a.take(2 * 256).rearrange("p (j n) -> p j n", j=2)
        KDB = [SPLIT[:, 256 * i:256 * i + 256] for i in range(2)]
        V4 = SPLIT[:, 512:1024]
        O4 = a.take(512)
        RSQ = a.take(4 * T).rearrange("p (f t) -> p f t", f=4)
        NS0 = 4
        S0 = [x.rearrange("p (e n) -> p e n", e=2) for x in [a.take(1024) for _ in range(NS0 - 1)] + [SIDE[:, 0:1024]]]
        QM = SIDE[:, 1024:1536].rearrange("p (e b t) -> p e b t", e=2, b=8)
        KS4 = SIDE[:, 1536:1792].rearrange("p (e a t) -> p e a t", e=2, a=4)
        KSC = SIDE[:, 1792:2048]
        ln = Cut(LNb[:, :], 2 * D)
        ROT = ln.take(4 * T).rearrange("p (f t) -> p f t", f=4)
        RAT = ln.take(384 + TS)
        KH = ln.take(256).bitcast(F32R)
        a = Cut(AR[:, :], ASZ)
        F, PP = (a.take(3 * D).rearrange("p (j n) -> p j n", j=3) for _ in range(2))
        YR = a.take(YW)
        HSf = a.take(2 * T).rearrange("p (f t) -> p f t", f=2)
        PT = a.take(2 * T).rearrange("p (f t) -> p f t", f=2)
        mark = a.at
        SC, SEL, MK, MR, MSK, CUM = (a.take(3 * E).rearrange("p (j e) -> p j e", j=3) for _ in range(6))
        G8 = a.take(24 * 8).rearrange("p (g k) -> p g k", g=24)
        GS, RK = a.take(24), a.take(24)
        GT8, GE8 = (a.take(192) for _ in range(2))
        T8 = a.take(24).rearrange("p (j k) -> p j k", j=3)
        DEN = a.take(3)
        POS = a.take(3 * EP).rearrange("p (j e) -> p j e", j=3)
        TAB = a.take(3 * EP * 2).rearrange("p (j e k) -> p j e k", j=3, e=EP)
        OH = [a.take(3 * P).rearrange("p (j a k) -> p j a k", j=3, a=2) for _ in range(2)]
        META = [a.take(4) for _ in range(2)]
        GATE = [a.take(1) for _ in range(2)]
        SI = [a.take(1).bitcast(U32) for _ in range(2)]
        PIN = a.take(3 * PD).rearrange("p (j n) -> p j n", j=3)
        WR = a.take(KC * E)
        HS = [a.take(DE) for _ in range(2)]
        HH = [a.take(DE) for _ in range(2)]
        HT = [a.take(2 * P).rearrange("p (c t) -> p c t", c=2) for _ in range(2)]
        YS = [SIDE[:, D * i:D * i + D] for i in range(2)]
        XGT = [XTb[:, D * i:D * i + D].rearrange("p (c t) -> p c t", c=KC) for i in range(2)]
        a = Cut(AR[:, mark:], ASZ - mark)
        YK = [a.take(TOPK * w).rearrange("p (k n) -> p k n", k=TOPK) for w in (YW, D - YW)]
        YS4 = XTb[:, 0:2 * D].rearrange("p (k n) -> p k n", k=2)
        SG = [SIDE[:, 512 * i:512 * i + 512] for i in range(2)]

        LASTW = AR[:, 0:PW]

        def wp(num):
            s = num % SLOTS
            return W[:, s * PW:(s + 1) * PW]

        bank_full = [sem("bank_full", b) for b in range(8)]
        bank_free = [sem("bank_emptied", b) for b in range(8)]
        slot_full = [sem("panel_landed", s) for s in range(SLOTS)]
        phase_end = sem("phase_end")

        def bank(name):
            return PS[:, GRP[name][0], :]

        def strip_sums(name):
            at = XTb if name[0] == "out0" else SIDE
            o = 0 if name[0] == "out0" else D
            return at[:, o + 512 * name[2]:o + 512 * name[2] + 512]

        def parts(name, r):
            ps = bank(name)
            if r == P:
                return [(ps, slice(0, 512))]
            return [(ps[TS * q:TS * q + TS, 0:P], slice(P * q, P * q + P)) for q in range(4)]

        def full(eng, name):
            b, u = GRP[name]
            eng.wait_ge(bank_full[b], u + 1)

        def emptied(eng, name):
            b, u = GRP[name]
            eng.wait_ge(bank_free[b], u + 1)

        def landed(eng, name):
            n = NUM[name]
            eng.wait_ge(slot_full[n % SLOTS], 32 * (n // SLOTS + 1))

        class Steps:

            def __init__(self, eng, s):
                self.eng, self.sem, self.n, self.last, self.counts, self.phases = eng, s, 0, None, {}, 0

            @property
            def after(self):
                if self.last is not None:
                    self.eng.wait_ge(*self.last)
                return self.eng

            def run(self, ins):
                ins.then_inc(self.sem, 1)
                self.n += 1
                self.last = (self.sem, self.n)

            def free(self, ins, name):
                b, u = GRP[name]
                ins.then_inc(bank_free[b], 1)
                self.last = (bank_free[b], u + 1)

            def empty(self, name, r, step):
                for ps, cols in parts(name, r):
                    ins = step(ps, cols)
                    if cols.stop == 512:
                        self.free(ins, name)
                    else:
                        self.run(ins)

            def tell(self, ins, s):
                k = self.counts.get(id(s), 0) + 1
                self.counts[id(s)] = k
                ins.then_inc(s, 1)
                self.last = (s, k)

            def phase(self):
                self.phases += 1
                self.after.nop().then_inc(phase_end, 1)
                self.eng.wait_ge(phase_end, 4 * self.phases)
                self.last = None

        def entry(h, i):
            k = (NSEQ + 1) * h + i
            return k, k % NS0

        def state_landed(eng, h, b):
            k, s = entry(h, b + 1)
            loads = sum(1 for m in range(k + 1) if m % NS0 == s and m % (NSEQ + 1))
            eng.wait_ge(sem("s0_in", s), 16 * loads)

        def slot_left(eng, k):
            if k >= NS0:
                eng.wait_ge(sem("s0_out", k % NS0), 16 * (k // NS0))

        block = ctx.enter_context(nc.Block())

        def tokens(eng, dst, src, s):
            pr, sa = src
            eng.dma_start(dst[:, 0:2, :], pr.rearrange("(j p) n -> p j n", p=P)).then_inc(s, 16)
            eng.dma_start(dst[0:TS, 2, :], sa).then_inc(s, 16)

        def norm_place(l, k):
            if l % 2 and k == 1:
                return dmask.rearrange("p h t -> p (h t)"), RV[0].rearrange("p j n -> p (j n)")[:, 0:D]
            return LN[:, 0, :], LN[:, 1, :]

        def norm_rows(eng, l, k):
            for i, nm in enumerate((f"ln{k}_g", f"ln{k}_b")):
                eng.dma_start(norm_place(l, k)[i], A[nm][l:l + 1, :].broadcast_to([P, D])).then_inc(sem("ln_in", l, k), 16)

        @block.sync
        def _(sp):
            def wait_slot(num):
                if num >= SLOTS:
                    g = LAST[num - SLOTS]
                    if g[0].startswith("moe"):
                        sp.wait_ge(bank_full[g[2]], GRP[(g[0],)][g[2]] + g[1] + 1)
                    else:
                        full(sp, g)

            def panel(name, parts):
                num = NUM[name]
                wait_slot(num)
                for dst, src in parts(wp(num)):
                    sp.dma_start(dst, src).then_inc(slot_full[num % SLOTS], 16)

            def split_cols(w, lo):
                s = w.rearrange("(p c) n -> p c n", c=KC)
                return lambda dst: [
                    (dst.rearrange("p (c n) -> p c n", c=KC)[:, 4 * k:4 * k + 4, :],
                     s[:, 4 * k:4 * k + 4, lo:lo + 512]) for k in range(2)]

            def out_rows(w, k0, lo):
                s = w.rearrange("(t p) n -> p t n", p=P)
                return lambda dst: [
                    (dst.rearrange("p (t n) -> p t n", t=8)[:, 4 * k:4 * k + 4, :],
                     s[:, k0 + 4 * k:k0 + 4 * k + 4, lo:lo + 512]) for k in range(2)]

            def two(a0, a1, how):
                return lambda dst: [(how(dst[:, 0:2048]), a0), (how(dst[:, 2048:4096]), a1)]

            def flat(x):
                return x

            sp.dma_start(CC[:, :], C[0]).then_inc(sem("const_in"), 16)
            tokens(sp, X, (A["x_prompt"][0], A["x_sample"].rearrange("b s d -> (b s) d")), sem("x_in"))

            for l in range(DEPTH):
                if l % 2 == 0:
                    wi = A["w_in_a"][0]
                    s = sem("even_in")
                    g = sem("gate_in")
                    sp.dma_start(wglr, wi.rearrange("(p c) n -> p c n", c=KC)[:, :, GCOL:GCOL + RANK]).then_inc(g, 16)
                    sp.dma_start(wgk2[0:RANK, :], A["w_gk2"][0]).then_inc(g, 16)
                    sp.dma_start(bgk, A["b_gk"][0].rearrange("(f p) -> p f", p=P), allow_slow_non_contiguous=True).then_inc(g, 16)
                    panel(("qk",), split_cols(wi, 0))
                    sp.dma_start(CE, C[1]).then_inc(sem("even_table"), 16)
                    sp.dma_start(spl[0:NSEQ * PBUF, :], A["state_pool"][0].rearrange("b t c -> (b t) c")).then_inc(sem("old_inputs"), 16)
                    panel(("v",), split_cols(wi, VCOL))
                    sp.dma_start(gnorm, A["g_norm_a"][0].rearrange("(p o) -> p o", o=1), allow_slow_non_contiguous=True).then_inc(s, 16)
                    sp.dma_start(bpool, A["b_pool"][0].rearrange("g p -> p g"), allow_slow_non_contiguous=True).then_inc(s, 16)
                    sp.dma_start(pscale, A["pool_scale"][0].rearrange("(g p) -> p g", p=P), allow_slow_non_contiguous=True).then_inc(s, 16)
                    sp.dma_start(wpool.rearrange("p (g n) -> p g n", g=4), A["w_pool"][0].rearrange("g c d -> c g d")).then_inc(s, 16)
                    panel(("u",), split_cols(wi, UCOL))
                    for f in range(2):
                        for r in range(2):
                            sp.dma_start(gs0[64 * r:64 * r + 64, f, :, :],
                                         A["state_gla"][0][:, 2 * f + r].rearrange("b k v -> k b v")).then_inc(s, 16)
                    panel(("r",), split_cols(wi, RCOL))
                    for n in range(2):
                        panel((f"out{l}", n), out_rows(A["w_out_a"][0], 0, 512 * n))
                else:
                    wi = A["w_in_c"][0].rearrange("(p c) n -> p c n", c=KC)
                    for h in range(H):
                        panel(("qk", h), two(wi[:, :, 256 * h:256 * h + 256], wi[:, :, 1024 + 256 * h:1280 + 256 * h],
                                             lambda x: x.rearrange("p (c n) -> p c n", c=KC)))
                        panel(("v", h), split_cols(A["w_in_c"][0], 2048 + 512 * h))
                        panel(("g", h), split_cols(A["w_in_c"][0], 4096 + 512 * h))
                    for n in range(2):
                        for k in range(2):
                            panel((f"out{l}", n, k), out_rows(A["w_out_c"][0], 8 * k, 512 * n))
                rp = lambda w: w.rearrange("(p c) n -> p (c n)", c=KC)
                panel((f"shgu{l}",), two(rp(A["w_sh_gate"][l]), rp(A["w_sh_up"][l]), flat))
                n0 = NUM[(f"moe{l}",)]
                base = GRP[(f"moe{l}",)]

                def expert_panel(num, e0, k, dst=None, s=None):
                    dst = wp(num) if dst is None else dst
                    s = slot_full[num % SLOTS] if s is None else s
                    if k < 2:
                        halves = [(A["w_exp_gate"], e0 + k), (A["w_exp_up"], e0 + k)]
                    else:
                        halves = [(A["w_exp_down"], e0), (A["w_exp_down"], e0 + 1)]
                    for q, (w, e) in enumerate(halves):
                        if isinstance(e, int):
                            src = w[l, e:e + 1]
                        else:
                            src = w[l, bass.ds(e, 1)]
                        c = KC if k < 2 else 2
                        sp.dma_start(dst[:, 2048 * q:2048 * q + 2048],
                                     src.rearrange("o (p c) n -> (o p) (c n)", c=c)).then_inc(s, 16)

                for pr in range(2):
                    for k in range(3):
                        if NUM[(f"shgu{l}",)] + (4 if l % 2 == 0 else 2) == n0 + 3 * pr + k:
                            sp.wait_ge(phase_end, 4 * (2 * l + 1))
                            sp.dma_start(WR, A["w_router"][l].rearrange("(p c) n -> p (c n)", c=KC)).then_inc(sem("router_in", l), 16)
                            sp.dma_start(rbias, A["router_bias"][l:l + 1, :].broadcast_to([P, E])).then_inc(sem("rbias_in", l), 16)
                            tokens(sp, PIN, (A["p_prompt"][l, 0], A["p_sample"][l].rearrange("b s d -> (b s) d")), sem("p_in", l))
                        wait_slot(n0 + 3 * pr + k)
                        expert_panel(n0 + 3 * pr + k, 2 * pr, k)
                expert_panel(None, E - 2, 2, LASTW, sem("last_down_in"))

                def two_pairs(it):
                    for u in range(2):
                        for k in range(3):
                            if isinstance(it, int) and u == 1 and k == 2:
                                continue
                            b = 5 if k == 2 else 2
                            sp.wait_ge(bank_full[b], base[b] + u - 1 + 2 * it)
                            expert_panel(n0 + 3 * u + k, 4 * it + 2 * u, k)

                with sp.Fori(1, PAIRS // 2 - 1) as it:
                    two_pairs(it)
                two_pairs(PAIRS // 2 - 1)
                tp = lambda w: w.rearrange("(f p) n -> p f n", p=P)
                panel((f"dp{l}",), two(tp(A["w_sh_down"][l]), tp(A["w_ple_proj"][l]),
                                       lambda x: x.rearrange("p (f n) -> p f n", f=2)))
                for n in range(2):
                    panel((f"pg{l}", n), split_cols(A["w_ple_gate"][l], 512 * n))
                for b in (2, 5):
                    sp.wait_ge(bank_full[b], base[b] + PAIRS)
                sp.wait_ge(sem("flag_ready", l), 1)
                go = sp.value_load(flagi[0:1, 0:1], min_val=0, max_val=1)
                with sp.If(go > 0):
                    sp.sem_inc(sem("ov_y", l), 1)
                    with sp.Fori(0, 4) as m:
                        with sp.Fori(0, PAIRS) as pr:
                            sp.wait_ge(sem("ov_y", l), m * PAIRS + pr + 1)
                            for k in range(3):
                                dst = wp(n0 + MOE_PANELS - 3 + k)
                                for q in range(2):
                                    w = (A["w_exp_gate"], A["w_exp_up"])[q] if k < 2 else A["w_exp_down"]
                                    e = 2 * pr + (k if k < 2 else q)
                                    sp.dma_start(dst[:, 2048 * q:2048 * q + 2048],
                                                 w[l, bass.ds(e, 1)].rearrange("o (p c) n -> (o p) (c n)", c=KC if k < 2 else 2)
                                                 ).then_inc(sem("ov_w", l), 16)
                    sp.wait_ge(sem("ov_y", l), 4 * PAIRS + 1)
                sp.nop()
                sp.wait_ge(sem("all_scattered", l), 1)
                ys = yd.rearrange("(k t) n -> t k n", k=TOPK)
                for k in range(2):
                    sp.dma_start(YS4[:, k, :], yd.rearrange("(q k t) n -> k q t n", q=4, k=2)[k, :, SEQ:T]
                                 ).then_inc(sem("y_samples"), 16)
                for i in range(4):
                    o, r = CH[ORD[1 + i // 2]]
                    if i > 1:
                        sp.wait_ge(sem("y_summed", l, i % 2), i // 2)
                    sp.dma_start(YK[i % 2][0:r, :, :], ys[o:o + r, :, YW:D] if i % 2 else ys[o:o + r, :, 0:YW]
                                 ).then_inc(sem("y_in", l, i % 2), 16)

        def even_pe(pe, st, begin, end, feat, tok):
            pe.wait_ge(sem("gate_in"), 16 * 3)
            ps = begin(("glr",))
            for c in range(KC):
                last = pe.matmul(ps[0:RANK, 0:T], wglr[:, c, :], XT[:, c, :], start=(c == 0), stop=(c == KC - 1))
            end(last, ("glr",))
            emptied(pe, ("glr",))
            for f in range(2):
                ps = begin(("gk", f))
                end(pe.matmul(ps[:, 0:T], wgk2[0:RANK, P * f:P * f + P], glrT[0:RANK, :], start=True, stop=True), ("gk", f))
            landed(pe, ("qk",))
            w = wp(NUM[("qk",)]).rearrange("p (c n) -> p c n", c=KC)
            for f in range(4):
                feat(("qk", f), lambda c: w[:, c, P * f:P * f + P])
            landed(pe, ("v",))
            w1 = wp(NUM[("v",)]).rearrange("p (c n) -> p c n", c=KC)
            for j, (o, r) in enumerate(CH):
                tok(("v", j), lambda c: XT[:, c, o:o + r], lambda c: w1[:, c, :], r, KC)
            nb = NSEQ * PBUF
            pe.wait_ge(sem("old_inputs"), 16)
            ps = begin(("spT",))
            for g in range(4):
                last = pe.transpose(ps[:, nb * g:nb * g + nb], spl[0:nb, P * g:P * g + P], ident[0:nb, 0:nb])
            end(last, ("spT",))

            def turn_keys(j):
                o, r = CH[j]
                ps = begin(("kdT", j))
                for f in range(2):
                    last = pe.transpose(ps[0:r, P * f:P * f + P], KDF[:, f, o:o + r], ident)
                end(last, ("kdT", j))

            def state_parts(j):
                r = CH[j][1]
                emptied(pe, ("kdT", j))
                emptied(pe, ("v", j))
                for f in range(2):
                    for i2 in range(2):
                        ps = begin(("dS", j, f, i2))
                        for i in range(4):
                            for k in range(2):
                                h = 2 * f + k
                                last = pe.matmul(ps[64 * k:64 * k + 64, P * i:P * i + P],
                                                 KDM[0:r, 4 * i2 + i, 64 * h:64 * h + 64],
                                                 V[0:r, j, P * h:P * h + P], start=True, stop=True)
                        end(last, ("dS", j, f, i2))

            landed(pe, ("u",))
            w2 = wp(NUM[("u",)]).rearrange("p (c n) -> p c n", c=KC)
            for f in range(4):
                feat(("u", f), lambda c: w2[:, c, P * f:P * f + P])
            for f in (2, 3):
                emptied(pe, ("qk", f))
            turn_keys(0)
            for f in range(4):
                emptied(pe, ("u", f))
            for nm, n in (("puT", PBUF), ("usT", TS)):
                ps = begin((nm,))
                for g in range(4):
                    src = UE[:, g, SEQ:SEQ + PBUF] if nm == "puT" else USC[:, g, :]
                    last = pe.transpose(ps[0:n, P * g:P * g + P], src, ident)
                end(last, (nm,))
            landed(pe, ("r",))
            w3 = wp(NUM[("r",)]).rearrange("p (c n) -> p c n", c=KC)
            for j in range(2):
                for f in range(2 * j, 2 * j + 2):
                    feat(("r", f), lambda c: w3[:, c, P * f:P * f + P])
                state_parts(j)
                turn_keys(j + 1)
            for f in range(4):
                emptied(pe, ("qk", f))
            for h in range(H):
                ps = begin(("att", h))
                for j, (o, r) in enumerate(CH):
                    last = pe.matmul(ps[0:r, o:o + r], KI[:, h // 2, o:o + r], QI[:, h // 2, h % 2, o:o + r],
                                     start=True, stop=True)
                end(last, ("att", h))
            state_parts(2)
            pe.wait_ge(sem("states"), 1)
            pe.wait_ge(sem("even_in"), 16 * 8)
            outs = []
            for f in range(2):
                out2 = begin(("oT", f)).rearrange("p (k t) -> p k t", k=2)
                outs.append(out2)
                for i in range(1, NCA):
                    pe.matmul(out2[:, :, CA * i:CA * i + CA], SS[:, f, i, :], QI[:, f, :, CA * i:CA * i + CA],
                              start=(i == 1), stop=False, skip_group_check=True)
            out4 = begin(("oTs",))[:, 0:H * TS].rearrange("p (h t) -> p h t", h=H)
            for f in range(2):
                for i in range(NSEQ):
                    c = DSEQ * i
                    pe.matmul(out4[:, 2 * f:2 * f + 2, c:c + DSEQ], gs0[:, f, i, :], QI[:, f, :, SEQ + c:SEQ + c + DSEQ],
                              start=(f == 0 and i == 0), stop=False, skip_group_check=True)
            for g in range(4):
                pe.wait_ge(sem("pool_d"), g + 1)
                ps = begin(("pool", g))
                end(pe.matmul(ps[:, 0:T], wpool[:, P * g:P * g + P], DD[:, g, :], start=True, stop=True), ("pool", g))
            for h in range(H):
                emptied(pe, ("att", h))
            for f in range(2):
                for k in range(2):
                    h = 2 * f + k
                    for j in range(2):
                        last = pe.matmul(outs[f][:, k, P * j:P * j + P], V[:, j, P * h:P * h + P],
                                         AT[:, h, P * j:P * j + P], start=False, stop=(k == 1 and j == 1),
                                         skip_group_check=True)
                end(last, ("oT", f))
            for h in range(H):
                last = pe.matmul(out4[:, h, :], V[0:TS, 2, P * h:P * h + P], AT[0:TS, h, SEQ:T],
                                 start=False, stop=(h == H - 1), skip_group_check=True)
            end(last, ("oTs",))
            for j, (o, r) in enumerate(CH):
                pe.wait_ge(sem("sq"), 3 if j == 2 else 2)
                ps = begin(("ms", j))[:, 0:H * r].rearrange("p (h t) -> p h t", h=H)
                end(pe.matmul(ps, onesA, SQE[:, :, o:o + r], start=True, stop=True), ("ms", j))

        def odd_pe(pe, st, begin, end, feat, tok, fold):
            for kind, h, i in odd_schedule():
                V = RV[h % 2]
                if kind == "qkh":
                    landed(pe, ("qk", h))
                    w = wp(NUM[("qk", h)]).rearrange("p (m c n e) -> p m c n e", m=2, c=KC, e=2)
                    feat(("qkh", h, i), lambda c: w[:, i // 2, c, :, i % 2])
                elif kind == "vv":
                    landed(pe, ("v", h))
                    w = wp(NUM[("v", h)]).rearrange("p (c n) -> p c n", c=KC)
                    o, r = CH[i]
                    if i < 2:
                        tok(("vv", h, i), lambda c: XT[:, c, o:o + r], lambda c: w[:, c, :], r, KC)
                    else:
                        emptied(pe, ("vstrips", h, 0))
                        ps = begin(("vv", h, i))
                        end(pe.matmul(ps, fold_all, O4, start=True, stop=True), ("vv", h, i))
                elif kind == "vstrips":
                    landed(pe, ("v", h))
                    w = wp(NUM[("v", h)]).rearrange("p (c n) -> p c n", c=KC)
                    tok(("vstrips", h, 0), lambda c: XT[:, c, SEQ:T], lambda c: w[:, c, :], TS, KC)
                elif kind == "gg":
                    landed(pe, ("g", h))
                    w = wp(NUM[("g", h)]).rearrange("p (c n) -> p c n", c=KC)
                    feat(("gg", h, i), lambda c: w[:, c, P * i:P * i + P])
                elif kind == "scores":
                    pe.wait_ge(sem("roped"), 2 * h + 2)
                    ps = begin(("ratt", h))
                    for (s0, t0, n, r, c0) in ((0, 0, SEQ, P, 0), (P, P, P, P, SEQ), (SEQ, SEQ, TS, TS, SEQ + P)):
                        for e in range(2):
                            last = pe.matmul(ps[0:r, c0:c0 + n], RQ[:, 2 + e, s0:s0 + r], RQ[:, e, t0:t0 + n],
                                             start=(e == 0), stop=(e == 1))
                    end(last, ("ratt", h))
                    ps = begin(("kT", h))
                    for j in range(2):
                        for e in range(2):
                            last = pe.transpose(ps[:, 256 * j + P * e:256 * j + P * e + P], RQ[:, 2 + e, P * j:P * j + P], ident)
                    end(last, ("kT", h))
                    pe.wait_ge(sem("sample_keys"), h + 1)
                    ps = begin(("kTs", h))
                    for e in range(2):
                        last = pe.transpose(ps[:, P * e:P * e + P], KS4[:, e].rearrange("p a t -> p (a t)"), ident)
                    end(last, ("kTs", h))
                elif kind == "state":
                    emptied(pe, ("kT", h))
                    for e in range(2):
                        ps = begin(("sp", h, e))
                        for j in range(2):
                            emptied(pe, ("vv", h, j))
                            last = pe.matmul(ps, KD[:, j, P * e:P * e + P], V[:, j, :], start=(j == 0), stop=(j == 1))
                        end(last, ("sp", h, e))
                elif kind == "seq":
                    b = i
                    if b == 0:
                        pso = begin(("o4", h))
                        pe.wait_ge(sem("sample_queries"), h + 1)
                        pe.wait_ge(sem("values_split"), h + 1)
                    state_landed(pe, h, b)
                    for e in range(2):
                        q = 32 * (2 * (b % 2) + e)
                        last = pe.matmul(pso[q:q + 32, :], QM[:, e, b, :], S0[entry(h, b + 1)[1]][:, e, :],
                                         start=(b < 2), stop=(b >= NSEQ - 2), skip_group_check=True)
                    if i == NSEQ - 1:
                        end(last, ("o4", h))
                    pe.wait_ge(sem("sequence_keys"), NSEQ * h + b + 1)
                    for e in range(2):
                        ps = begin(("sn", h, b, e))
                        end(pe.matmul(ps, KDB[b % 2][:, P * e:P * e + P], V4, start=True, stop=True), ("sn", h, b, e))
                elif kind == "outp":
                    emptied(pe, ("ratt", h))
                    for g in range(2):
                        ps = begin(("roT", h, g)).rearrange("p (f t) -> p f t", f=2)
                        for k in range(2):
                            vf = slice(P * (2 * g + k), P * (2 * g + k) + P)
                            pe.matmul(ps[:, k, :], V[:, 0, vf], RAT[:, 0:SEQ], start=(k == 0), stop=False,
                                      skip_group_check=True)
                            last = pe.matmul(ps[:, k, P:SEQ], V[:, 1, vf], RAT[:, SEQ:SEQ + P], start=False,
                                             stop=(k == 1), skip_group_check=True)
                        end(last, ("roT", h, g))
                elif kind == "outs":
                    emptied(pe, ("vv", h, 2))
                    emptied(pe, ("o4", h))
                    ps = begin(("roTs", h))[:, 0:4 * TS].rearrange("p (f t) -> p f t", f=4)
                    for f in range(4):
                        vf = slice(P * f, P * f + P)
                        pe.matmul(ps[:, f, :], V[0:TS, 2, vf], RAT[0:TS, SEQ + P:SEQ + P + TS], start=(f == 0), stop=False,
                                  skip_group_check=True)
                        last = pe.matmul(ps[:, f, :], O4[:, vf], fold4, start=False, stop=(f == 3), skip_group_check=True)
                    end(last, ("roTs", h))
                elif kind == "norm":
                    if i == 0:
                        pe.wait_ge(sem("squares", 0), 2 * h + 2)
                    else:
                        pe.wait_ge(sem("squares", 1), h + 1)
                    ts = slice(SEQ, T) if i else slice(0, SEQ)
                    ps = begin(("rms", h, i))
                    for f in range(4):
                        last = pe.matmul(ps[:, 0:ts.stop - ts.start], onesC, RSQ[:, f, ts], start=(f == 0), stop=(f == 3))
                    end(last, ("rms", h, i))
                elif kind == "fold":
                    if i == 0:
                        fold("out1")
                else:
                    pe.wait_ge(sem("headmix", h // 2), H)
                    landed(pe, (f"out1", i, 0))
                    landed(pe, (f"out1", i, 1))
                    w = [wp(NUM[(f"out1", i, k)]).rearrange("p (t n) -> p t n", t=8) for k in range(2)]
                    o, r = CH[h]
                    tok(("out1", h, i), lambda c: MT[:, c, o:o + r], lambda c: w[c // 8][:, c % 8, :], r, 16)

        @block.tensor
        def _(pe):
            st = Steps(pe, None)
            order = iter(group_order())

            def begin(name):
                assert next(order) == name, name
                b, u = GRP[name]
                if u:
                    pe.wait_ge(bank_free[b], u)
                return PS[:, b, :]

            def end(ins, name):
                b, u = GRP[name]
                ins.then_inc(bank_full[b], 1)
                st.last = (bank_full[b], u + 1)

            def transpose_x(tag, j, ready=None):
                if ready:
                    pe.wait_ge(*ready)
                r = CH[j][1]
                xc = X[0:r, j, :].rearrange("p (m c) -> p c m", c=KC)
                for q in range(2):
                    ps = begin((tag, j, q))
                    for c in range(4):
                        last = pe.transpose(ps[:, c * P:c * P + r], xc[:, 4 * q + c, :], ident[0:r, 0:r])
                    end(last, (tag, j, q))

            def have_xt(tag, chunks=range(3)):
                for j in chunks:
                    for q in range(2):
                        emptied(pe, (tag, j, q))

            def feat(name, lhs, n=KC):
                ps = begin(name)
                for c in range(n):
                    last = pe.matmul(ps[:, 0:T], lhs(c), XT[:, c, :], start=(c == 0), stop=(c == n - 1))
                end(last, name)

            def tok(name, lhs, rhs, r, n, w=512):
                ps = begin(name)
                if r == TS and n >= 8 and name[0] != "v":
                    for c in range(n):
                        q = c % 4
                        last = pe.matmul(ps[TS * q:TS * q + TS, :], lhs(c), rhs(c), start=(c < 4), stop=(c >= n - 4))
                    end(last, name)
                    return
                if r == TS:
                    for c in range(n):
                        for q in range(4):
                            last = pe.matmul(ps[TS * q:TS * q + TS, 0:P], lhs(c), rhs(c)[:, P * q:P * q + P],
                                             start=(c == 0), stop=(c == n - 1))
                    end(last, name)
                    return
                for c in range(n):
                    last = pe.matmul(ps[0:r, 0:w], lhs(c), rhs(c), start=(c == 0), stop=(c == n - 1))
                end(last, name)

            def fold(tag):
                for n in range(2):
                    emptied(pe, (tag, 2, n))
                    ps = begin((tag, "fold", n))
                    end(pe.matmul(ps[0:TS, :], fold4, strip_sums((tag, 2, n)), start=True, stop=True), (tag, "fold", n))

            pe.wait_ge(sem("const_in"), 16)
            pe.wait_ge(sem("x_in"), 32)
            pe.wait_ge(sem("ones_set"), 1)
            for l in range(DEPTH):
                for i, j in enumerate(ORD):
                    transpose_x(f"xTa{l}", j, (sem("x_out", l - 1), i + 1) if l else None)
                have_xt(f"xTa{l}")
                if l % 2 == 0:
                    even_pe(pe, st, begin, end, feat, tok)
                else:
                    odd_pe(pe, st, begin, end, feat, tok, fold)
                if l % 2 == 0:
                    for j, (o, r) in enumerate(CH):
                        pe.wait_ge(sem("mixed"), j + 1)
                        for n in range(2):
                            landed(pe, (f"out{l}", n))
                            w = wp(NUM[(f"out{l}", n)]).rearrange("p (t n) -> p t n", t=8)
                            tok((f"out{l}", j, n), lambda c: MTE[:, c, o:o + r], lambda c: w[:, c, :], r, 8)
                    fold(f"out{l}")
                st.phase()

                for j in range(3):
                    transpose_x(f"xTb{l}", j, (sem("x_mid", l), j + 1))
                have_xt(f"xTb{l}")
                pe.wait_ge(sem("router_in", l), 16)
                ps = begin((f"router{l}",))
                wr = WR.rearrange("p (c n) -> p c n", c=KC)
                for j, (o, r) in enumerate(CH):
                    for c in range(KC):
                        last = pe.matmul(ps[0:r, E * j:E * j + E], XT[:, c, o:o + r], wr[:, c, :],
                                         start=(c == 0), stop=(c == KC - 1))
                end(last, (f"router{l}",))
                landed(pe, (f"shgu{l}",))
                sg = wp(NUM[(f"shgu{l}",)]).rearrange("p (m c n) -> p m c n", m=2, c=KC)

                def shared(f):
                    feat((f"sh{l}", f), lambda c: sg[:, f // 2, c, P * (f % 2):P * (f % 2) + P])

                for f in (0, 2, 1):
                    shared(f)
                pe.wait_ge(sem("p_in", l), 32)
                ps = begin((f"pT{l}",))
                for f in range(2):
                    for j in range(2):
                        last = pe.transpose(ps[:, P * (2 * f + j):P * (2 * f + j) + P], PIN[:, j, P * f:P * f + P], ident)
                end(last, (f"pT{l}",))
                pe.wait_ge(sem("chosen", l), 1)
                ps = begin((f"cum{l}",))
                for j, (o, r) in enumerate(CH):
                    for jj in range(j):
                        pe.matmul(ps[0:r, E * j:E * j + E], ones[:, 0:r], MSK[:, jj, :], start=(jj == 0), stop=False)
                    last = pe.matmul(ps[0:r, E * j:E * j + E], tri[0:r, 0:r], MSK[0:r, j, :], start=(j == 0), stop=True)
                for f in range(2):
                    last = pe.transpose(ps[:, 256 + TS * f:256 + TS * f + TS], PIN[0:TS, 2, P * f:P * f + P], ident[0:TS, 0:TS])
                end(last, (f"cum{l}",))
                shared(3)
                pe.wait_ge(sem("colmax", l), 1)
                ps = begin((f"flag{l}",))
                end(pe.transpose(ps[0:1, 0:P], colmax, ident), (f"flag{l}",))
                base = GRP[(f"moe{l}",)]
                n0 = NUM[(f"moe{l}",)]

                def meta(u, pr, ps):
                    for j, (o, r) in enumerate(CH):
                        tb = TAB[0:r, j].rearrange("p e k -> p (e k)")
                        rhs = tb[:, 4 * pr:4 * pr + 4] if isinstance(pr, int) else tb[:, bass.ds(4 * pr, 4)]
                        last = pe.matmul(ps[:, 0:4], OH[u][0:r, j].rearrange("p a k -> p (a k)"), rhs,
                                         start=(j == 0), stop=(j == 2))
                    return last

                def rows(u, q, ps):
                    for c in range(4):
                        for j, (o, r) in enumerate(CH):
                            xc = X[0:r, j, :].rearrange("p (m c) -> p c m", c=KC)
                            last = pe.matmul(ps[:, c * P:c * P + P], xc[:, 4 * q + c, :],
                                             OH[u][0:r, j].rearrange("p a k -> p (a k)"), start=(j == 0), stop=(j == 2))
                    return last

                def gate_up(u, w, ps):
                    for c in range(KC):
                        for s in range(2):
                            rhs = w[s].rearrange("p (m c n) -> p m c n", m=2, c=KC)[:, :, c, :]
                            last = pe.matmul(ps[64 * s:64 * s + 64, :], XGT[u][:, c, 64 * s:64 * s + 64], rhs,
                                             start=(c == 0), stop=(c == KC - 1))
                    return last

                def turn_hidden(u, ps):
                    hc = HH[u].rearrange("p (m c) -> p c m", c=2)
                    for c in range(2):
                        last = pe.transpose(ps[:, c * P:c * P + P], hc[:, c, :], ident)
                    return last

                def down(u, n, w, ps):
                    wd = w.rearrange("p (s c n) -> p s c n", s=2, c=2)
                    for c in range(2):
                        for s in range(2):
                            last = pe.matmul(ps[64 * s:64 * s + 64, :], HT[u][:, c, 64 * s:64 * s + 64],
                                             wd[:, s, c, 512 * n:512 * n + 512], start=(c == 0), stop=(c == 1))
                    return last

                pe.wait_ge(sem("onehot", l), 1)
                end(meta(0, 0, begin((f"lists{l}",))), (f"lists{l}",))
                for q in range(2):
                    end(rows(0, q, begin((f"rows{l}", q))), (f"rows{l}", q))
                assert next(order) == (f"moe{l}",)
                for q in range(2):
                    emptied(pe, (f"rows{l}", q))
                for b in range(7):
                    pe.wait_ge(bank_free[b], base[b])
                def two_pairs(it):
                    for u in range(2):
                        v = 1 - u
                        pr = 2 * it + u
                        pe.wait_ge(sem("onehot", l), pr + 2)
                        pe.wait_ge(bank_free[6], base[6] + pr)
                        meta(v, pr + 1, PS[:, 6, :]).then_inc(bank_full[6], 1)
                        for q in range(2):
                            pe.wait_ge(bank_free[q], base[q] + pr)
                        for k in range(2):
                            n = n0 + 3 * u + k
                            pe.wait_ge(slot_full[n % SLOTS], 32 * (n // SLOTS + 1) + 32 * it)
                        pe.wait_ge(bank_free[2], base[2] + pr)
                        gate_up(u, [wp(n0 + 3 * u), wp(n0 + 3 * u + 1)], PS[:, 2, :]).then_inc(bank_full[2], 1)
                        for q in range(2):
                            rows(v, q, PS[:, q, :]).then_inc(bank_full[q], 1)
                        pe.wait_ge(bank_free[2], base[2] + pr + 1)
                        pe.wait_ge(bank_free[3], base[3] + pr)
                        turn_hidden(u, PS[:, 3, :]).then_inc(bank_full[3], 1)
                        pe.wait_ge(bank_free[3], base[3] + pr + 1)
                        if isinstance(it, int) and u == 1:
                            wd = LASTW
                            pe.wait_ge(sem("last_down_in"), 32 * (l + 1))
                        else:
                            n = n0 + 3 * u + 2
                            wd = wp(n)
                            pe.wait_ge(slot_full[n % SLOTS], 32 * (n // SLOTS + 1) + 32 * it)
                        for h in range(2):
                            pe.wait_ge(bank_free[4 + h], base[4 + h] + pr)
                            down(u, h, wd, PS[:, 4 + h, :]).then_inc(bank_full[4 + h], 1)
                with pe.Fori(0, PAIRS // 2 - 1) as it:
                    two_pairs(it)
                two_pairs(PAIRS // 2 - 1)
                pe.wait_ge(sem("flag_ready", l), 1)
                last_panels = [wp(n0 + MOE_PANELS - 3 + k) for k in range(3)]
                go = pe.value_load(flagi[0:1, 0:1], min_val=0, max_val=1)
                with pe.If(go > 0):
                    for b in range(7):
                        pe.wait_ge(bank_free[b], base[b] + PAIRS)
                    with pe.Fori(0, 4) as m:
                        with pe.Fori(0, PAIRS) as pr:
                            s = m * PAIRS + pr
                            pe.wait_ge(sem("ov_onehot", l), s + 1)
                            meta(0, pr, PS[:, 6, :]).then_inc(sem("ov_meta", l), 1)
                            rows(0, 0, PS[:, 0, :])
                            rows(0, 1, PS[:, 1, :]).then_inc(sem("ov_rows", l), 1)
                            pe.wait_ge(sem("ov_xgt", l), s + 1)
                            pe.wait_ge(sem("ov_w", l), 96 * s + 96)
                            gate_up(0, last_panels[0:2], PS[:, 2, :]).then_inc(sem("ov_gu", l), 1)
                            pe.wait_ge(sem("ov_hidden", l), s + 1)
                            turn_hidden(0, PS[:, 3, :]).then_inc(sem("ov_hT", l), 1)
                            pe.wait_ge(sem("ov_hTc", l), s + 1)
                            down(0, 0, last_panels[2], PS[:, 4, :])
                            down(0, 1, last_panels[2], PS[:, 5, :]).then_inc(sem("ov_y", l), 1)
                    pe.wait_ge(sem("ov_yc", l), 4 * PAIRS)
                pe.nop()
                st.last = None

                for f in range(2):
                    emptied(pe, (f"sh{l}", 2 + f))
                emptied(pe, (f"pT{l}",))
                emptied(pe, (f"cum{l}",))
                landed(pe, (f"dp{l}",))
                dp = wp(NUM[(f"dp{l}",)]).rearrange("p (m f n) -> p m f n", m=2, f=2)
                for m, (nm, src) in enumerate(((f"shd{l}", HSf), (f"pw{l}", PT))):
                    for j in ORD:
                        o, r = CH[j]
                        for n in range(2):
                            tok((nm, j, n), lambda c: src[:, c, o:o + r], lambda c: dp[:, m, c, 512 * n:512 * n + 512], r, 2)
                pe.wait_ge(sem("y_samples_summed"), l + 1)
                for n in range(2):
                    ps = begin((f"fold{l}", n))
                    end(pe.matmul(ps[0:TS, :], fold4, YS4[:, 0, 512 * n:512 * n + 512], start=True, stop=True),
                        (f"fold{l}", n))
                for i, j in enumerate(ORD):
                    o, r = CH[j]
                    transpose_x(f"xTc{l}", j, (sem("x_ln2", l), i + 1))
                    have_xt(f"xTc{l}", (j,))
                    for n in range(2):
                        landed(pe, (f"pg{l}", n))
                        w = wp(NUM[(f"pg{l}", n)]).rearrange("p (c n) -> p c n", c=KC)
                        tok((f"pg{l}", j, n), lambda c: XT[:, c, o:o + r], lambda c: w[:, c, :], r, KC)
                    if j == 2:
                        fold(f"pg{l}")
                st.phase()

        @block.scalar
        def _(act):
            st = Steps(act, sem("act_steps"))

            def copy(dst, src, **k):
                return act.activation(dst, src, ACT.Copy, **k)

            def x_half(tag, chunks):
                for j in chunks:
                    o, r = CH[j]
                    full(act, (tag, j, 0))
                    st.free(copy(XT[:, 0:4, o:o + r],
                                 bank((tag, j, 0)).rearrange("p (c t) -> p c t", c=4)[:, :, 0:r]), (tag, j, 0))

            def norm_root(l, k, i, j):
                act.wait_ge(sem("variance", l, k), i + 1)
                st.tell(act.activation(rstd[:, j:j + 1], bnag[:, 2 * j + 1:2 * j + 2], ACT.Sqrt, bias=eps), sem("std", l, k))

            def keep_strips(tag):
                for n in range(2):
                    full(act, (tag, 2, n))
                    st.free(copy(strip_sums((tag, 2, n)), bank((tag, 2, n))), (tag, 2, n))

            act.wait_ge(sem("ones_set"), 1)
            for l in range(DEPTH):
                if l % 2:
                    act.dma_start(CO, C[2]).then_inc(sem("odd_in"), 16)
                x_half(f"xTa{l}", ORD)
                if l % 2 == 0:
                    full(act, ("glr",))
                    st.free(copy(glrT[0:RANK, :], bank(("glr",))[0:RANK, 0:T]), ("glr",))
                    act.wait_ge(sem("gate_logits"), 1)
                    st.run(act.activation(LB, LB, ACT.Exp, scale=-1.0))
                    st.tell(st.after.activation(LB, LB, ACT.Ln, bias=ones[:, 0:1]), sem("log_term"))
                    act.wait_ge(sem("summed"), 1)
                    st.tell(act.activation(EB, LB, ACT.Exp, scale=1.0 / 16), sem("decays"))
                    st.tell(act.activation(EN, LB, ACT.Exp, scale=-1.0 / 16), sem("decays"))
                    act.wait_ge(sem("to_end"), 1)
                    st.tell(act.activation(KDF, KDF, ACT.Exp, scale=1.0 / 16), sem("decays"))
                    for j, (o, r) in enumerate(CH):
                        full(act, ("v", j))
                        st.empty(("v", j), r, lambda ps, c: copy(V[0:r, j, c], ps))
                    full(act, ("spT",))
                    for g in range(4):
                        n = NSEQ * PBUF
                        ins = copy(US[:, g, :, 0:PBUF], bank(("spT",))[:, n * g:n * g + n].rearrange("p (b t) -> p b t", b=NSEQ))
                        if g < 3:
                            st.run(ins)
                        else:
                            st.free(ins, ("spT",))
                    for f in range(4):
                        full(act, ("u", f))
                        ps = bank(("u", f))
                        st.run(copy(UE[:, f, PBUF:], ps[:, 0:SEQ]))
                        st.run(copy(USC[:, f, :], ps[:, SEQ:T]))
                        st.free(copy(US[:, f, :, PBUF:19], ps[:, SEQ:T].rearrange("p (b t) -> p b t", b=NSEQ)), ("u", f))
                    full(act, ("puT",))
                    st.free(copy(PUO[0:PBUF, :], bank(("puT",))[0:PBUF, :]), ("puT",))
                    full(act, ("usT",))
                    st.free(copy(spl[0:TS, :], bank(("usT",))[0:TS, :]), ("usT",))
                    for f in range(4):
                        full(act, ("r", f))
                        st.free(act.activation(MTE[:, f, :], bank(("r", f))[:, 0:T], ACT.Silu), ("r", f))
                    for name, hs, ts in ((("oT", 0), slice(0, 2), slice(0, SEQ)), (("oT", 1), slice(2, 4), slice(0, SEQ)),
                                         (("oTs",), slice(0, 4), slice(SEQ, T))):
                        full(act, name)
                        n = (hs.stop - hs.start) * (ts.stop - ts.start)
                        ps = bank(name)[:, 0:n].rearrange("p (h t) -> p h t", h=hs.stop - hs.start)
                        st.tell(act.activation(SQE[:, hs, ts], ps, ACT.Square), sem("sq"))
                        st.free(copy(AT[:, hs, ts], ps), name)
                    for f in range(2):
                        for i2 in range(2):
                            emptied(act, ("dS", 2, f, i2))
                    norm_rows(act, l, 1)
                    for j, (o, r) in enumerate(CH):
                        full(act, ("ms", j))
                        if j == 2:
                            act.wait_ge(sem("mixed"), 1)
                        st.free(act.activation(RSE[j % 2][:, :, 0:r], bank(("ms", j))[:, 0:H * r].rearrange("p (h t) -> p h t", h=H),
                                               ACT.Sqrt, bias=eps), ("ms", j))
                else:
                    def one_sequence(h, b):
                        if b > 1:
                            full(act, ("sn", h, b - 2, 1))
                        elif h:
                            full(act, ("sn", h - 1, NSEQ - 2 + b, 1))
                        st.tell(copy(KDB[b % 2], KH, scale=own_k[:, b:b + 1]), sem("sequence_keys"))

                    act.wait_ge(sem("odd_in"), 16)
                    for kind, h, i in odd_schedule():
                        if kind == "vv":
                            full(act, ("vv", h, i))
                            st.free(copy(RV[h % 2][:, i, :], bank(("vv", h, i))), ("vv", h, i))
                        elif kind == "vstrips":
                            full(act, ("vstrips", h, 0))
                            st.free(copy(O4, bank(("vstrips", h, 0))), ("vstrips", h, 0))
                        elif kind == "gg":
                            full(act, ("gg", h, i))
                            st.free(act.activation(MT[:, 4 * h + i, :], bank(("gg", h, i))[:, 0:T], ACT.Silu), ("gg", h, i))
                        elif kind == "scores":
                            full(act, ("kT", h))
                            st.run(copy(KD[:, 0, :], bank(("kT", h))[:, 0:256], scale=kdec[:, 0, h:h + 1]))
                            st.free(copy(KD[:, 1, :], bank(("kT", h))[:, 256:512], scale=kdec[:, 1, h:h + 1]), ("kT", h))
                        elif kind == "state":
                            if h == H - 1:
                                emptied(act, ("ratt", h))
                                full(act, ("roTs", h - 1))
                                norm_rows(act, l, 1)
                            act.wait_ge(sem("keys_split"), h + 1)
                            one_sequence(h, 0)
                            k, s = entry(h, 0)
                            slot_left(act, k)
                            for e in range(2):
                                full(act, ("sp", h, e))
                                st.free(copy(S0[s][:, e, :], bank(("sp", h, e))), ("sp", h, e))
                        elif kind == "seq":
                            if i < NSEQ - 1:
                                one_sequence(h, i + 1)
                            if i == NSEQ - 1:
                                full(act, ("o4", h))
                                st.free(copy(O4, bank(("o4", h))), ("o4", h))
                        elif kind == "outp":
                            for g in range(2):
                                full(act, ("roT", h, g))
                                if h and g == 0:
                                    act.wait_ge(sem("headmix", 0), h)
                                ps = bank(("roT", h, g)).rearrange("p (f t) -> p f t", f=2)
                                st.tell(act.activation(RSQ[:, 2 * g:2 * g + 2, 0:SEQ], ps, ACT.Square), sem("squares", 0))
                                st.free(copy(ROT[:, 2 * g:2 * g + 2, 0:SEQ], ps), ("roT", h, g))
                        elif kind == "outs":
                            full(act, ("roTs", h))
                            if h:
                                act.wait_ge(sem("headmix", 1), h)
                            ps = bank(("roTs", h))[:, 0:4 * TS].rearrange("p (f t) -> p f t", f=4)
                            st.tell(act.activation(RSQ[:, :, SEQ:T], ps, ACT.Square), sem("squares", 1))
                            st.free(copy(ROT[:, :, SEQ:T], ps), ("roTs", h))
                        elif kind == "norm":
                            ts = slice(SEQ, T) if i else slice(0, SEQ)
                            full(act, ("rms", h, i))
                            st.free(act.activation(RSQ[:, 0, ts], bank(("rms", h, i))[:, 0:ts.stop - ts.start], ACT.Sqrt,
                                                   bias=eps), ("rms", h, i))
                        elif kind == "out" and h < 2 and i:
                            norm_root(l, 1, h, h)
                        elif kind == "fold" and i == 0:
                            keep_strips("out1")
                            norm_root(l, 1, h, h)
                if l % 2 == 0:
                    for j in range(3):
                        if j == 2:
                            keep_strips(f"out{l}")
                        norm_root(l, 1, j, j)
                st.phase()

                act.wait_ge(sem("x_mid", l), 3)
                norm_rows(act, l, 2)
                x_half(f"xTb{l}", range(3))
                full(act, (f"router{l}",))
                act.wait_ge(sem("scores_cleared", l), 1)
                ps = bank((f"router{l}",))
                st.run(act.activation(SC[:, 0:2, :], ps[:, 0:2 * E].rearrange("p (j e) -> p j e", j=2), ACT.Sigmoid))
                st.free(act.activation(SC[0:TS, 2, :], ps[0:TS, 2 * E:3 * E], ACT.Sigmoid), (f"router{l}",))

                def shared(f):
                    full(act, (f"sh{l}", f))
                    st.free(act.activation(HSf[:, f, :], bank((f"sh{l}", f))[:, 0:T], ACT.Silu), (f"sh{l}", f))

                for f in range(2):
                    shared(f)
                full(act, (f"pT{l}",))
                for f in range(2):
                    ins = copy(PT[:, f, 0:SEQ], bank((f"pT{l}",))[:, 256 * f:256 * f + 256])
                    if f:
                        st.free(ins, (f"pT{l}",))
                    else:
                        st.run(ins)
                base = GRP[(f"moe{l}",)]

                def rows(u, q, ps):
                    return copy(XGT[u][:, 4 * q:4 * q + 4, :], ps.rearrange("p (c t) -> p c t", c=4))

                for q in range(2):
                    full(act, (f"rows{l}", q))
                    st.free(rows(0, q, bank((f"rows{l}", q))), (f"rows{l}", q))

                def two_pairs(it):
                    for u in range(2):
                        pr = 2 * it + u
                        act.wait_ge(bank_full[2], base[2] + pr + 1)
                        act.activation(HS[u], PS[:, 2, 0:DE], ACT.Silu).then_inc(sem("silu", l), 1)
                        for q in range(2):
                            act.wait_ge(bank_full[q], base[q] + pr + 1)
                            rows(1 - u, q, PS[:, q, :]).then_inc(bank_free[q], 1)
                        act.wait_ge(bank_full[3], base[3] + pr + 1)
                        copy(HT[u], PS[:, 3, 0:256].rearrange("p (c t) -> p c t", c=2)).then_inc(bank_free[3], 1)
                        act.wait_ge(bank_full[5], base[5] + pr + 1)
                        if not isinstance(it, int):
                            act.wait_ge(sem("scattered", l, u), 16 * it)
                        copy(YS[u][:, 512:1024], PS[:, 5, :]).then_inc(bank_free[5], 1)

                two_pairs(0)
                with act.Fori(1, PAIRS // 2) as it:
                    two_pairs(it)
                act.wait_ge(sem("flag_ready", l), 1)
                go = act.value_load(flagi[0:1, 0:1], min_val=0, max_val=1)
                with act.If(go > 0):
                    with act.Fori(0, 4) as m:
                        with act.Fori(0, PAIRS) as pr:
                            s = m * PAIRS + pr
                            act.wait_ge(sem("ov_rows", l), s + 1)
                            rows(0, 0, PS[:, 0, :])
                            rows(0, 1, PS[:, 1, :]).then_inc(sem("ov_xgt", l), 1)
                            act.wait_ge(sem("ov_gu", l), s + 1)
                            act.activation(HS[0], PS[:, 2, 0:DE], ACT.Silu).then_inc(sem("ov_silu", l), 1)
                            act.wait_ge(sem("ov_hT", l), s + 1)
                            copy(HT[0], PS[:, 3, 0:256].rearrange("p (c t) -> p c t", c=2)).then_inc(sem("ov_hTc", l), 1)
                act.nop()
                st.last = None
                for j in ORD:
                    o, r = CH[j]
                    for n in range(2):
                        full(act, (f"pw{l}", j, n))
                        pp = PP[0:r, j, 512 * n:512 * n + 512]
                        st.empty((f"pw{l}", j, n), r, lambda ps, c: copy(pp[:, c], ps))

                def turned(i):
                    norm_root(l, 2, i, ORD[i])
                    x_half(f"xTc{l}", (ORD[i],))

                def gate(i):
                    j = ORD[i]
                    r = CH[j][1]
                    for n in range(2):
                        name = (f"pg{l}", "fold" if j == 2 else j, n)
                        full(act, name)
                        if i:
                            act.wait_ge(sem("gated", l), 2 * i + n - 1)
                        st.free(act.activation(SG[n][0:r, :], bank(name)[0:r, :], ACT.Sigmoid), name)

                turned(0)
                keep_strips(f"pg{l}")
                turned(1)
                gate(0)
                turned(2)
                gate(1)
                gate(2)
                st.phase()

        def even_dve(dve, st, TT, TSc, STT):
            dve.wait_ge(sem("gate_in"), 16 * 3)
            for f in range(2):
                full(dve, ("gk", f))
                st.free(TSc(LX[:, f, :], bank(("gk", f))[:, 0:T], bgk[:, f:f + 1], None, ALU.add), ("gk", f))
            st.after
            st.tell(STT(LB, LX, -1.0, LX, ALU.mult, ALU.max), sem("gate_logits"))
            st.after
            st.run(TSc(LX, LX, 0.0, None, ALU.min))
            dve.wait_ge(sem("log_term"), 1)
            st.after
            st.run(TT(LX, LX, LB, ALU.subtract))
            dve.wait_ge(sem("even_table"), 16)
            for f in range(2):
                st.after
                ins = dve.tensor_tensor_scan(LB[:, f, :], keep, LX[:, f, :], 0.0, ALU.mult, ALU.add)
                if f:
                    st.tell(ins, sem("summed"))
                else:
                    st.run(ins)
            st.after
            for f in range(2):
                for k, (o, n, c) in enumerate(((0, SEQ, CA), (SEQ, TS, DSEQ))):
                    b = LB[:, f, o:o + n].rearrange("p (i c) -> p i c", c=c)
                    ins = TT(KDF[:, f, o:o + n].rearrange("p (i c) -> p i c", c=c),
                             b[:, :, c - 1:c].broadcast_to([P, n // c, c]), b, ALU.subtract)
                    if f and k:
                        st.tell(ins, sem("to_end"))
                    else:
                        st.run(ins)
            dve.wait_ge(sem("decays"), 3)
            for f in range(4):
                full(dve, ("qk", f))
                ps = bank(("qk", f))[:, 0:T]
                if f < 2:
                    if f == 0:
                        dve.wait_ge(sem("queries_zeroed"), 1)
                    st.run(STT(QI[0:64, f, 0, :], ps[0:64], DKA ** -0.5, EB[0:64, f, :], ALU.mult, ALU.mult))
                    st.free(STT(QI[64:128, f, 1, :], ps[64:128], DKA ** -0.5, EB[64:128, f, :], ALU.mult, ALU.mult), ("qk", f))
                else:
                    st.run(TT(KI[:, f - 2, :], ps, EN[:, f - 2, :], ALU.mult))
                    st.free(TT(KDF[:, f - 2, :], ps, KDF[:, f - 2, :], ALU.mult), ("qk", f))

            def mask_keys(j):
                r = CH[j][1]
                if j:
                    full(dve, ("dS", j - 1, 1, 1))
                full(dve, ("kdT", j))
                m = mch if j < 2 else mch_s
                st.free(TT(KDM[0:r], bank(("kdT", j))[0:r, 0:256].unsqueeze(1).broadcast_to([r, 8, 256]),
                           m[0:r, :].unsqueeze(2).broadcast_to([r, 8, 256]), ALU.mult), ("kdT", j))

            mask_keys(0)
            for j in range(2):
                for f in range(2):
                    for i2 in range(2):
                        name = ("dS", j, f, i2)
                        full(dve, name)
                        ps = bank(name)
                        for i in range(4):
                            n = 8 * j + 4 * i2 + i
                            ds_ = ps[:, P * i:P * i + P]
                            st.after
                            if n == 0:
                                st.run(dve.tensor_copy(SS[:, f, 1, :], ds_))
                                continue
                            t = CA * n + CA - 1
                            ins = STT(SS[:, f, n + 1, :], SS[:, f, n, :], EB[:, f, t:t + 1], ds_, ALU.mult, ALU.add)
                            if i == 3:
                                st.free(ins, name)
                            else:
                                st.run(ins)
                mask_keys(j + 1)
            st.after.nop().then_inc(sem("states"), 1)
            for f in range(4):
                full(dve, ("r", f))
            st.run(dve.memset(AT, 0.0))
            st.after
            for h in range(H):
                full(dve, ("att", h))
                ps = bank(("att", h))
                for o in (0, P):
                    st.run(dve.copy_predicated(AT[:, h, o:o + P], mcau, ps[:, o:o + P]))
                st.free(dve.copy_predicated(AT[0:TS, h, SEQ:T], mcau_s[0:TS, :], ps[0:TS, SEQ:T]), ("att", h))
            dve.wait_ge(sem("even_in"), 16 * 8)
            for f in range(2):
                for i2 in range(2):
                    full(dve, ("dS", 2, f, i2))
            for f in range(2):
                for i2 in range(2):
                    name = ("dS", 2, f, i2)
                    for i in range(4):
                        b = 4 * i2 + i
                        t = SEQ + DSEQ * b + DSEQ - 1
                        ins = STT(gsn[:, f, b, :], gs0[:, f, b, :], EB[:, f, t:t + 1], bank(name)[:, P * i:P * i + P],
                                  ALU.mult, ALU.add)
                        if i == 3:
                            st.free(ins, name)
                        else:
                            st.run(ins)
            for g in range(4):
                full(dve, ("pool", g))
                st.free(TSc(MTE[:, 4 + g, :], bank(("pool", g))[:, 0:T], bpool[:, g:g + 1], pscale[:, g:g + 1],
                            ALU.add, ALU.mult), ("pool", g))
            for j, (o, r) in enumerate(CH):
                emptied(dve, ("ms", j))
                rs, att, mix = RSE[j % 2][:, :, 0:r], AT[:, :, o:o + r], MTE[:, 0:H, o:o + r]
                st.run(dve.reciprocal(rs, rs))
                st.after
                st.run(STT(att, att, gnorm, rs, ALU.mult, ALU.mult))
                st.after
                st.tell(TT(mix, mix, att, ALU.mult), sem("mixed"))

        def odd_dve(dve, st, TT, TSc, STT, norm, residual):
            gam = [1.0 - 2.0 ** (-5.0 - h) for h in range(H)]
            dve.wait_ge(sem("odd_in"), 16)
            for kind, h, i in odd_schedule():
                if kind == "qkh" and i % 2:
                    m = i // 2
                    ne, no = ("qkh", h, 2 * m), ("qkh", h, 2 * m + 1)
                    full(dve, ne)
                    full(dve, no)
                    pe_, po = bank(ne)[:, 0:T], bank(no)[:, 0:T]
                    st.after
                    st.run(TT(RT[:, 0, :], pe_, cos, ALU.mult))
                    st.run(TT(RT[:, 1, :], po, sin, ALU.mult))
                    st.after
                    st.run(TT(RQ[:, 2 * m, :], RT[:, 0, :], RT[:, 1, :], ALU.subtract))
                    st.after
                    st.free(TT(RT[:, 0, :], pe_, sin, ALU.mult), ne)
                    st.free(TT(RT[:, 1, :], po, cos, ALU.mult), no)
                    st.after
                    emptied(dve, ne)
                    st.tell(TT(RQ[:, 2 * m + 1, :], RT[:, 0, :], RT[:, 1, :], ALU.add), sem("roped"))
                elif kind == "scores":
                    st.after
                    for e in range(2):
                        ins = dve.tensor_copy(KS4[:, e], RQ[:, 2 + e, SEQ:T].unsqueeze(1).broadcast_to([P, 4, TS]))
                        if e:
                            st.tell(ins, sem("sample_keys"))
                        else:
                            st.run(ins)
                    full(dve, ("ratt", h))
                    ps = bank(("ratt", h))
                    st.run(TT(RAT[:, 0:SEQ], ps[:, 0:SEQ], dmask[:, h, :], ALU.mult))
                    st.run(TT(RAT[:, SEQ:SEQ + P], ps[:, SEQ:SEQ + P], dmask[:, h, 0:P], ALU.mult))
                    st.free(TT(RAT[0:TS, SEQ + P:SEQ + P + TS], ps[0:TS, SEQ + P:SEQ + P + TS], dmask_s[0:TS, h, :], ALU.mult),
                            ("ratt", h))
                    for e in range(2):
                        st.run(TT(RT[:, e, 0:TS], RQ[:, e, SEQ:T], qdec[:, h, :], ALU.mult))
                    st.after
                    for e in range(2):
                        ins = TT(QM[:, e], RT[:, e, 0:TS].unsqueeze(1).broadcast_to([P, NSEQ, TS]), own_q, ALU.mult)
                        if e:
                            st.tell(ins, sem("sample_queries"))
                        else:
                            st.run(ins)
                    full(dve, ("kTs", h))
                    st.free(TSc(KSC, bank(("kTs", h))[:, 0:256], kdec_s[:, h:h + 1], None, ALU.mult), ("kTs", h))
                    if h:
                        dve.wait_ge(sem("sequence_keys"), NSEQ * h)
                    st.after
                    st.run(dve.tensor_copy(KH, KSC))
                    st.after
                    st.tell(TT(KH[64:128, :], KSC[64:128, :], KH[64:128, :], ALU.subtract), sem("keys_split"))
                    emptied(dve, ("vv", h, 2))
                    v = RV[h % 2][:, 2, :]
                    st.run(dve.tensor_copy(V4, v))
                    st.after
                    st.run(TT(V4[32:64, :], v[32:64, :], V4[32:64, :], ALU.subtract))
                    st.tell(TT(V4[96:128, :], v[96:128, :], V4[96:128, :], ALU.subtract), sem("values_split"))
                elif kind == "seq":
                    for e in range(2):
                        full(dve, ("sn", h, i, e))
                        s0 = S0[entry(h, i + 1)[1]][:, e, :]
                        st.free(STT(s0, s0, gam[h] ** DSEQ, bank(("sn", h, i, e)), ALU.mult, ALU.add), ("sn", h, i, e))
                elif kind == "norm":
                    ts = slice(SEQ, T) if i else slice(0, SEQ)
                    n = ts.stop - ts.start
                    emptied(dve, ("rms", h, i))
                    st.run(dve.reciprocal(RSQ[:, 0, ts], RSQ[:, 0, ts]))
                    st.after
                    st.run(TT(ROT[:, :, ts], ROT[:, :, ts], RSQ[:, 0, ts].unsqueeze(1).broadcast_to([P, 4, n]), ALU.mult))
                    st.after
                    emptied(dve, ("gg", h, 3))
                    st.tell(TT(MT[:, 4 * h:4 * h + 4, ts], MT[:, 4 * h:4 * h + 4, ts], ROT[:, :, ts], ALU.mult),
                            sem("headmix", i))
                elif kind == "fold" or kind == "out" and h < 2:
                    residual(1, h, i)
                    if i:
                        norm(1, 1, h, h, sem("x_mid", 1))

        def experts_dve(dve, st, TT, TSc, STT, l, x_half, norm):
            R3 = [P, 3, E]
            x_half(f"xTb{l}", range(3))
            st.run(dve.memset(MSK, 0.0))
            st.run(dve.memset(POS, -1.0))
            st.run(dve.memset(TAB, 0.0))
            st.after
            emptied(dve, (f"router{l}",))
            dve.wait_ge(sem("rbias_in", l), 16)
            dve.wait_ge(sem("scores_cleared", l), 1)
            st.run(TT(SEL, SC, rbias.unsqueeze(1).broadcast_to(R3), ALU.add))
            sel8 = SEL.rearrange("p j (g k) -> p (j g) k", g=EG)
            st.after
            for g in range(24):
                st.run(dve.max(G8[:, g, :], sel8[:, g, :]))
            st.after
            st.run(TT(GS, G8[:, :, 0], G8[:, :, 1], ALU.add))
            st.after
            g3 = GS.rearrange("p (j g) -> p j g", j=3)
            other, own = g3.unsqueeze(2).broadcast_to([P, 3, EG, EG]), g3.unsqueeze(3).broadcast_to([P, 3, EG, EG])
            a, b = (y.rearrange("p (j g k) -> p j g k", j=3, g=EG) for y in (GT8, GE8))
            st.run(TT(a, other, own, ALU.is_gt))
            st.run(TT(b, other, own, ALU.is_equal))
            st.after
            st.run(TT(b, b, tri8.rearrange("p (g k) -> p g k", g=EG).unsqueeze(1).broadcast_to([P, 3, EG, EG]), ALU.mult))
            st.after
            st.run(TT(GT8, GT8, GE8, ALU.add))
            st.after
            st.run(dve.tensor_reduce(RK, GT8.rearrange("p (g k) -> p g k", k=EG), AX.X, ALU.add))
            st.after
            st.run(TSc(RK, RK, TOPG - 0.5, None, ALU.is_lt))
            st.after
            mk8 = MK.rearrange("p j (g k) -> p (j g) k", g=EG)
            st.run(TT(mk8, sel8, RK.unsqueeze(2).broadcast_to([P, 24, EG]), ALU.mult))
            st.run(TSc(GS, RK, BIG, -BIG, ALU.mult, ALU.add))
            st.after
            st.run(TT(mk8, mk8, GS.unsqueeze(2).broadcast_to([P, 24, EG]), ALU.add))
            st.after
            for j in range(3):
                st.run(dve.max(T8[:, j, :], MK[:, j, :]))
            st.after
            for j in range(3):
                st.run(dve.match_replace(MR[:, j, :], T8[:, j, :], MK[:, j, :], -2 * BIG))
            st.after
            st.run(TSc(MSK[:, 0:2, :], MR[:, 0:2, :], -1.5 * BIG, None, ALU.is_lt))
            st.run(TSc(MSK[0:TS, 2, :], MR[0:TS, 2, :], -1.5 * BIG, None, ALU.is_lt))
            st.after.nop().then_inc(sem("chosen", l), 1)
            st.run(TT(MR, SC, MSK, ALU.mult))
            st.after
            st.run(dve.tensor_reduce(DEN, MR, AX.X, ALU.add))
            st.after
            st.run(TSc(DEN, DEN, 1e-20, None, ALU.add))
            st.after
            st.run(dve.reciprocal(DEN, DEN))
            st.after
            for j in range(3):
                st.run(TSc(TAB[:, j, 0:E, 1], MR[:, j, :], DEN[:, j:j + 1], ROUTED, ALU.mult, ALU.mult))
            for j in range(3):
                st.run(dve.tensor_tensor_scan(SEL[:, j, :], ones[:, 0:E], MSK[:, j, :], 0.0, ALU.mult, ALU.add))
            st.after
            for j in range(3):
                st.run(TSc(TAB[:, j, 0:E, 0], SEL[:, j, :], float(T), slotc[:, j:j + 1], ALU.mult, ALU.add))

            def shared(f):
                full(dve, (f"sh{l}", 2 + f))
                emptied(dve, (f"sh{l}", f))
                st.free(TT(HSf[:, f, :], HSf[:, f, :], bank((f"sh{l}", 2 + f))[:, 0:T], ALU.mult), (f"sh{l}", 2 + f))

            shared(0)
            full(dve, (f"cum{l}",))
            ps = bank((f"cum{l}",))
            st.run(STT(CUM[:, 0:2, :], ps[:, 0:2 * E].rearrange("p (j e) -> p j e", j=2), 1.0, MSK[:, 0:2, :], ALU.add, ALU.mult))
            st.run(STT(CUM[0:TS, 2, :], ps[0:TS, 2 * E:3 * E], 1.0, MSK[0:TS, 2, :], ALU.add, ALU.mult))
            st.free(dve.tensor_copy(PT[:, :, SEQ:T], ps[:, 256:256 + 2 * TS].rearrange("p (f t) -> p f t", f=2)), (f"cum{l}",))
            st.after
            st.run(TSc(POS[:, 0:2, 0:E], CUM[:, 0:2, :], -1.0, None, ALU.add))
            st.run(TSc(POS[0:TS, 2, 0:E], CUM[0:TS, 2, :], -1.0, None, ALU.add))
            st.after
            st.tell(dve.tensor_reduce(colmax, POS, AX.XY, ALU.max), sem("colmax", l))

            def onehot(u, pr, off):
                pos = POS[:, :, 2 * pr:2 * pr + 2] if isinstance(pr, int) else POS[:, :, bass.ds(2 * pr, 2)]
                it_ = iota[:, 0:BLK] if isinstance(off, int) else iota[:, bass.ds(off, BLK)]
                for j in range(3):
                    last = TT(OH[u][:, j], it_.unsqueeze(1).broadcast_to([P, 2, BLK]),
                              pos[:, j].unsqueeze(2).broadcast_to([P, 2, BLK]), ALU.is_equal)
                return last

            def meta(u, ps):
                return dve.tensor_copy(META[u], ps[:, 0:4])

            def gates(u):
                dve.tensor_copy(GATE[u][0:64, :], META[u][0:64, 1:2])
                return dve.tensor_copy(GATE[u][64:128, :], META[u][64:128, 3:4])

            def slot_rows(u):
                TSc(SI[u][0:64, :], META[u][0:64, 0:1], FAR, None, ALU.add)
                return TSc(SI[u][64:128, :], META[u][64:128, 2:3], FAR, None, ALU.add)

            def hidden(u):
                return STT(HH[u], HS[u], GATE[u], PS[:, 2, DE:2 * DE], ALU.mult, ALU.mult)

            base = GRP[(f"moe{l}",)]
            st.after
            onehot(0, 0, 0).then_inc(sem("onehot", l), 1)
            full(dve, (f"flag{l}",))
            st.free(dve.tensor_reduce(flagf[0:1, :], bank((f"flag{l}",))[0:1, 0:P], AX.X, ALU.max), (f"flag{l}",))
            st.after
            st.tell(TSc(flagi[0:1, :], flagf[0:1, :], BLK - 0.5, None, ALU.is_gt), sem("flag_ready", l))
            full(dve, (f"lists{l}",))
            st.free(meta(0, bank((f"lists{l}",))), (f"lists{l}",))
            st.after
            gates(0)
            onehot(1, 1, 0).then_inc(sem("onehot", l), 1)
            shared(1)

            def two_pairs(it):
                for u in range(2):
                    v = 1 - u
                    pr = 2 * it + u
                    dve.wait_ge(bank_full[6], base[6] + pr + 1)
                    dve.wait_ge(bank_free[4], base[4] + pr)
                    meta(v, PS[:, 6, :]).then_inc(bank_free[6], 1)
                    dve.wait_ge(bank_free[6], base[6] + pr + 1)
                    gates(v).then_inc(sem("gates", l), 1)
                    onehot(u, pr + 2, 0).then_inc(sem("onehot", l), 1)
                    dve.wait_ge(bank_full[2], base[2] + pr + 1)
                    dve.wait_ge(sem("silu", l), pr + 1)
                    dve.wait_ge(sem("gates", l), pr + 1)
                    hidden(u).then_inc(bank_free[2], 1)
                    if not isinstance(it, int):
                        dve.wait_ge(sem("scattered", l, u), 16 * it)
                    slot_rows(u).then_inc(sem("slot_rows", l), 1)
                    dve.wait_ge(bank_full[4], base[4] + pr + 1)
                    dve.tensor_copy(YS[u][:, 0:512], PS[:, 4, :]).then_inc(bank_free[4], 1)

            two_pairs(0)
            with dve.Fori(1, PAIRS // 2) as it:
                two_pairs(it)
            dve.wait_ge(sem("flag_ready", l), 1)
            go = dve.value_load(flagi[0:1, 0:1], min_val=0, max_val=1)
            with dve.If(go > 0):
                dve.wait_ge(sem("scattered", l, 0), 16 * (PAIRS // 2))
                dve.wait_ge(sem("scattered", l, 1), 16 * (PAIRS // 2))
                with dve.Fori(0, 4) as m:
                    with dve.Fori(0, PAIRS) as pr:
                        s = m * PAIRS + pr
                        onehot(0, pr, m * BLK + BLK).then_inc(sem("ov_onehot", l), 1)
                        dve.wait_ge(sem("ov_meta", l), s + 1)
                        meta(0, PS[:, 6, :]).then_inc(sem("ov_metac", l), 1)
                        dve.wait_ge(sem("ov_metac", l), s + 1)
                        dve.wait_ge(sem("ov_rows_left", l), s + 1)
                        gates(0)
                        slot_rows(0).then_inc(sem("ov_lists", l), 1)
                        dve.wait_ge(sem("ov_silu", l), s + 1)
                        dve.wait_ge(sem("ov_lists", l), s + 1)
                        hidden(0).then_inc(sem("ov_hidden", l), 1)
                        dve.wait_ge(sem("ov_y", l), s + 2)
                        dve.tensor_copy(YS[0][:, 0:512], PS[:, 4, :])
                        dve.tensor_copy(YS[0][:, 512:1024], PS[:, 5, :]).then_inc(sem("ov_yc", l), 1)
            dve.nop()
            st.last = None
            st.last = None

            for j in ORD:
                r = CH[j][1]
                for n in range(2):
                    name = (f"shd{l}", j, n)
                    full(dve, name)
                    x, f = (y[0:r, j, 512 * n:512 * n + 512] for y in (X, F))
                    st.empty(name, r, lambda ps, c: STT(f[:, c], x[:, c], ALPHA, ps, ALU.mult, ALU.add))

            def summed(i):
                j = ORD[i]
                r = CH[j][1]
                if i == 0:
                    dve.wait_ge(sem("y_samples"), 32 * (l + 1))
                    st.tell(TT(YS4[:, 0, :], YS4[:, 0, :], YS4[:, 1, :], ALU.add), sem("y_samples_summed"))
                    for n in range(2):
                        name, cols = (f"fold{l}", n), slice(512 * n, 512 * n + 512)
                        full(dve, name)
                        st.free(TT(X[0:r, j, cols], F[0:r, j, cols], bank(name)[0:r, :], ALU.add), name)
                    return
                dve.wait_ge(sem("y_in", l, 0), 16 * i)
                st.after
                st.tell(dve.tensor_reduce(YR[0:r, :], YK[0][0:r].rearrange("p k n -> p n k"), AX.X, ALU.add),
                        sem("y_summed", l, 0))
                st.after
                st.run(TT(X[0:r, j, 0:YW], F[0:r, j, 0:YW], YR[0:r, :], ALU.add))

            def turned(i):
                summed(i)
                norm(l, 2, i, ORD[i], sem("x_ln2", l), sem("y_summed", l, 1) if i else None)
                x_half(f"xTc{l}", (ORD[i],))

            def gate(i):
                j = ORD[i]
                r = CH[j][1]
                for n in range(2):
                    emptied(dve, (f"pg{l}", "fold" if j == 2 else j, n))
                    cols = slice(512 * n, 512 * n + 512)
                    st.run(TT(SG[n][0:r, :], SG[n][0:r, :], PP[0:r, j, cols], ALU.mult))
                    x = X[0:r, j, cols]
                    st.after
                    st.tell(TT(x, x, SG[n][0:r, :], ALU.add), sem("gated", l))
                st.after
                st.tell(dve.nop(), sem("x_out", l))

            turned(0)
            turned(1)
            gate(0)
            turned(2)
            gate(1)
            gate(2)

        @block.vector
        def _(dve):
            st = Steps(dve, sem("dve_steps"))
            TT, TSc, STT = dve.tensor_tensor, dve.tensor_scalar, dve.scalar_tensor_tensor

            def x_half(tag, chunks):
                for j in chunks:
                    o, r = CH[j]
                    full(dve, (tag, j, 1))
                    st.free(dve.tensor_copy(XT[:, 4:8, o:o + r],
                                            bank((tag, j, 1)).rearrange("p (c t) -> p c t", c=4)[:, :, 0:r]), (tag, j, 1))

            def residual(l, j, n):
                name, r = (f"out{l}", "fold" if j == 2 else j, n), CH[j][1]
                full(dve, name)
                x = X[0:r, j, 512 * n:512 * n + 512]
                st.free(STT(x, x, ALPHA, bank(name)[0:r, :], ALU.mult, ALU.add), name)

            def norm(l, k, i, j, done, half=None):
                r = CH[j][1]
                st.after
                for n in range(2):
                    if n and half:
                        dve.wait_ge(half, i)
                    st.run(dve.bn_stats(bnst[0:r, 6 * n:6 * n + 6], X[0:r, j, 512 * n:512 * n + 512]))
                st.after
                st.tell(dve.bn_aggr(bnag[0:r, 2 * j:2 * j + 2], bnst[0:r, :]), sem("variance", l, k))
                dve.wait_ge(sem("std", l, k), i + 1)
                st.run(dve.reciprocal(rstd[:, j:j + 1], rstd[:, j:j + 1]))
                if i == 0:
                    dve.wait_ge(sem("ln_in", l, k), 32)
                x = X[0:r, j, :]
                st.after
                st.run(TSc(x, x, bnag[0:r, 2 * j:2 * j + 1], rstd[0:r, j:j + 1], ALU.subtract, ALU.mult))
                st.after
                st.run(TT(x, x, norm_place(l, k)[0][0:r, :], ALU.mult))
                st.after
                st.tell(TT(x, x, norm_place(l, k)[1][0:r, :], ALU.add), done)

            dve.wait_ge(sem("ones_set"), 1)
            dve.wait_ge(sem("const_in"), 16)
            for l in range(DEPTH):
                x_half(f"xTa{l}", ORD)
                if l % 2 == 0:
                    even_dve(dve, st, TT, TSc, STT)
                else:
                    odd_dve(dve, st, TT, TSc, STT, norm, residual)
                if l % 2 == 0:
                    for j in range(3):
                        for n in range(2):
                            residual(l, j, n)
                        norm(l, 1, j, j, sem("x_mid", l))
                st.phase()
                experts_dve(dve, st, TT, TSc, STT, l, x_half, norm)
                st.phase()

        def even_pool(pool, st, store):
            s = sem("even_out")
            n_out = 0
            store(O["pool_sample"][0, :, 0:PBUF - DSEQ, :], A["state_pool"][0, :, DSEQ:PBUF, :], s)
            st.tell(pool.memset(QI, 0.0), sem("queries_zeroed"))
            st.run(pool.memset(UE[:, :, 0:PBUF], 0.0))
            for f in range(4):
                emptied(pool, ("u", f))
            emptied(pool, ("spT",))
            pool.wait_ge(sem("even_table"), 16)
            for f in range(4):
                emptied(pool, ("qk", f))
            for g, w in enumerate(WINDOWS):
                for kind in range(2):
                    if kind == 0:
                        n, new = SEQ, SEQ
                        ext = UE[:, g, :].unsqueeze(1)
                        buf = [b[:, 0:PBUF + SEQ].unsqueeze(1) for b in PWK]
                        dst = DD[:, g, 0:SEQ].unsqueeze(1)
                    else:
                        n, new = 1, DSEQ
                        ext = US[:, g]
                        buf = [b[:, 0:NSEQ * 19].rearrange("p (b t) -> p b t", b=NSEQ) for b in PWK]
                        dst = DD[:, g, SEQ:T].rearrange("p (b t) -> p b t", b=NSEQ)
                    cur, step, k, ln = ext, 1, 0, PBUF + new
                    while step < w:
                        nxt = buf[k % 2]
                        st.after
                        st.run(pool.tensor_tensor(nxt[:, :, 2 * step - 1:ln], cur[:, :, 2 * step - 1:ln],
                                                  cur[:, :, step - 1:ln - step], ALU.add))
                        cur, step, k = nxt, 2 * step, k + 1
                    win = cur[:, :, PBUF:ln]
                    st.after
                    if kind == 0:
                        st.run(pool.tensor_tensor(win[:, :, 0:16], win[:, :, 0:16],
                                                  invc[:, 16 * g:16 * g + 16].unsqueeze(1), ALU.mult))
                        st.run(pool.tensor_scalar(win[:, :, 16:SEQ], win[:, :, 16:SEQ], 1.0 / w, None, ALU.mult))
                    else:
                        st.run(pool.tensor_scalar(win, win, 1.0 / w, None, ALU.mult))
                    st.after
                    ins = pool.tensor_tensor(dst, win, ext[:, :, PBUF:ln], ALU.subtract)
                    if kind:
                        st.tell(ins, sem("pool_d"))
                    else:
                        st.run(ins)
            emptied(pool, ("puT",))
            store(O["pool_prompt"][0, 0], PUO[0:PBUF, :], s)
            emptied(pool, ("usT",))
            for b in range(NSEQ):
                store(O["pool_sample"][0, b, PBUF - DSEQ:PBUF, :], spl[DSEQ * b:DSEQ * b + DSEQ, :], s)
            pool.wait_ge(sem("states"), 1)
            for f in range(2):
                for i2 in range(2):
                    emptied(pool, ("dS", 2, f, i2))
            for h in range(H):
                f, r = h // 2, 64 * (h % 2)
                store(O["gla_prompt"][0, 0, h], SS[r:r + 64, f, 16, :], s)
                store(O["gla_sample"][0, :, h].rearrange("b k v -> k b v"), gsn[r:r + 64, f, :, :], s)
            pool.wait_ge(s, 16 * (1 + 1 + NSEQ + 2 * H))

        def odd_pool(pool, st, store):
            def rows(x):
                return x.rearrange("(p e) v -> p e v", e=2)

            def load(k):
                h, i = k // (NSEQ + 1), k % (NSEQ + 1)
                if i:
                    pool.dma_start(S0[k % NS0], rows(A["state_ret"][0, i - 1, h])).then_inc(sem("s0_in", k % NS0), 16)

            n = (NSEQ + 1) * H
            for k in range(NS0):
                load(k)
            for k in range(n):
                h, i = k // (NSEQ + 1), k % (NSEQ + 1)
                for e in range(2):
                    emptied(pool, ("sn", h, i - 1, e) if i else ("sp", h, e))
                store(rows(O["ret_sample"][0, i - 1, h] if i else O["ret_prompt"][0, 0, h]), S0[k % NS0],
                      sem("s0_out", k % NS0))
                if k and k - 1 + NS0 < n:
                    slot_left(pool, k - 1 + NS0)
                    load(k - 1 + NS0)
            for i in range(NS0):
                pool.wait_ge(sem("s0_out", i), 16 * ((n - i + NS0 - 1) // NS0))

        def experts_pool(pool, st, store, l):
            st.run(pool.memset(SC[:, 2, :], 0.0))
            st.after.nop().then_inc(sem("scores_cleared", l), 1)
            st.last = None
            base = GRP[(f"moe{l}",)]
            last_slot = pool.to_reg(TOPK * T - 1)

            def scatter(u, s):
                pool.sem_inc(sem("scatters_begun"))
                pool.indirect_dma_start(yd, bass.IndirectOffsetOnAxis(ap=SI[u], axis=0), YS[u], None,
                                        bounds_check=last_slot, oob_is_err=False).then_inc(s, 16)

            with pool.Fori(0, PAIRS // 2) as it:
                for u in range(2):
                    pr = 2 * it + u
                    pool.wait_ge(sem("slot_rows", l), pr + 1)
                    for b in (4, 5):
                        pool.wait_ge(bank_free[b], base[b] + pr + 1)
                    scatter(u, sem("scattered", l, u))
            for u in range(2):
                pool.wait_ge(sem("scattered", l, u), 16 * (PAIRS // 2))
            pool.wait_ge(sem("flag_ready", l), 1)
            go = pool.value_load(flagi[0:1, 0:1], min_val=0, max_val=1)
            with pool.If(go > 0):
                pool.sem_inc(sem("ov_rows_left", l), 1)
                with pool.Fori(0, 4) as m:
                    with pool.Fori(0, PAIRS) as pr:
                        s = m * PAIRS + pr
                        pool.wait_ge(sem("ov_lists", l), s + 1)
                        pool.wait_ge(sem("ov_yc", l), s + 1)
                        scatter(0, sem("ov_scattered", l))
                        pool.wait_ge(sem("ov_scattered", l), 16 * s + 16)
                        pool.sem_inc(sem("ov_rows_left", l), 1)
            pool.nop().then_inc(sem("all_scattered", l), 1)
            st.last = None
            for i, j in enumerate(ORD[1:]):
                r = CH[j][1]
                y = YK[1][0:r]
                pool.wait_ge(sem("y_in", l, 1), 16 * (i + 1))
                for k in (4, 2, 1):
                    st.after
                    st.run(pool.tensor_tensor(y[:, 0:k, :], y[:, 0:k, :], y[:, k:2 * k, :], ALU.add))
                emptied(pool, (f"shd{l}", j, 1))
                st.after
                st.tell(pool.tensor_tensor(X[0:r, j, YW:D], F[0:r, j, YW:D], y[:, 0, :], ALU.add), sem("y_summed", l, 1))


        @block.gpsimd
        def _(pool):
            st = Steps(pool, sem("pool_steps"))
            st.run(pool.memset(ones, 1.0))
            st.run(pool.memset(onesA, 1.0 / DVA))
            st.run(pool.memset(onesC, 1.0 / DVC))
            st.run(pool.memset(eps, EPS))
            st.run(pool.memset(bnag, 1.0))
            st.after.nop().then_inc(sem("ones_set"), 1)
            st.last = None

            def store(dst, src, s):
                pool.dma_start(dst, src).then_inc(s, 16)

            for l in range(DEPTH):
                if l % 2 == 0:
                    even_pool(pool, st, store)
                else:
                    odd_pool(pool, st, store)
                st.phase()
                experts_pool(pool, st, store, l)
                if l == DEPTH - 1:
                    for i, j in enumerate(ORD):
                        o, r = CH[j]
                        pool.wait_ge(sem("x_out", l), i + 1)
                        dst = O["y_prompt"][0, o:o + r, :] if j < 2 else O["y_sample"].rearrange("b s d -> (b s) d")
                        store(dst, X[0:r, j, :], sem("stored"))
                    pool.wait_ge(sem("stored"), 48)
                st.phase()

_INS = ['x_prompt', 'x_sample', 'state_gla', 'state_pool', 'state_ret', 'p_prompt', 'p_sample',
        'w_in_a', 'w_gk2', 'b_gk', 'g_norm_a', 'w_pool', 'b_pool', 'pool_scale', 'w_out_a',
        'w_in_c', 'w_out_c', 'ln1_g', 'ln1_b', 'ln2_g', 'ln2_b',
        'w_router', 'router_bias', 'w_exp_gate', 'w_exp_up', 'w_exp_down',
        'w_sh_gate', 'w_sh_up', 'w_sh_down', 'w_ple_gate', 'w_ple_proj']
_OUTS = [("y_prompt", (1, SEQ, D)), ("y_sample", (NSEQ, DSEQ, D)), ("gla_prompt", (1, 1, H, DKA, DVA)),
         ("pool_prompt", (1, 1, PBUF, 512)), ("ret_prompt", (1, 1, H, DKC, DVC)),
         ("gla_sample", (1, NSEQ, H, DKA, DVA)), ("pool_sample", (1, NSEQ, PBUF, 512)),
         ("ret_sample", (1, NSEQ, H, DKC, DVC))]


def kernel(**inputs):
    import numpy as _np
    import concourse.bacc as _bacc
    from concourse import mybir as _mybir
    from concourse.bass_utils import run_bass_kernel_spmd as _run

    nc = _bacc.Bacc("TRN2", target_bir_lowering=False, num_devices=1)
    arrays, args = {}, {}
    for name in _INS:
        a = _np.ascontiguousarray(inputs[name])
        arrays[f"in_{name}"] = a
        args[name] = nc.dram_tensor(f"in_{name}", a.shape, _mybir.dt.from_np(a.dtype), kind="ExternalInput").ap()
    tables = []
    for i, a in enumerate(constants()):
        arrays[f"table_{i}"] = a
        tables.append(nc.dram_tensor(f"table_{i}", a.shape, F32, kind="ExternalInput").ap())
    outs = {n: nc.dram_tensor(f"out_{n}", s, F32, kind="ExternalOutput").ap() for n, s in _OUTS}
    trunk(nc, args, outs, tables)
    r = _run(nc, [arrays], core_ids=[0])
    return tuple(r.results[0][f"out_{n}"] for n, _ in _OUTS)
```
